# Optimizing a Trainium2 kernel written in Bass

```python
import jax, jax.numpy as jnp
from jax import lax
import numpy as np

D_MODEL = 1024
BATCH = 1
SEQ = 1024
DEPTH = 1

CTX_LEN = 256
GRID_W = 64
D_MIX = D_MODEL
RET_HEADS = 4
RET_DK = 64
RET_DV = 128
D_RET_QK = RET_HEADS * RET_DK
D_RET_V = RET_HEADS * RET_DV
FOURIER_GROUPS = 4
FOURIER_CH = 128
D_FOURIER = FOURIER_GROUPS * FOURIER_CH
D_IN = 2 * D_RET_QK + 3 * D_RET_V + D_FOURIER
D_FF = 2816
RET_CHUNK = 128
ROPE_BASE = 10000.0
N_MOD = 9
EPS = 1e-6

kernel_name = "hybrid_retention_fourier_macaron_dit_block"

def _rms_norm(x, g):
    xf = x.astype(jnp.float32)
    y = xf * lax.rsqrt(jnp.mean(xf * xf, axis=-1, keepdims=True) + EPS)
    return (y * g.astype(jnp.float32)).astype(x.dtype)

def _modulate(x, shift, scale):
    return x * (1.0 + scale) + shift

def _swiglu(x, w13, w2):
    a, b = jnp.split(x @ w13, 2, axis=-1)
    return (jax.nn.silu(a) * b) @ w2

def _split_heads(t, dh):
    b, n, _ = t.shape
    return t.reshape(b, n, -1, dh).transpose(0, 2, 1, 3)

def _rope_tables(rows, cols):
    n_freq = RET_DK // 4
    inv_freq = ROPE_BASE ** (-jnp.arange(n_freq, dtype=jnp.float32) / n_freq)
    ang = jnp.concatenate([rows.astype(jnp.float32)[:, None] * inv_freq,
                           cols.astype(jnp.float32)[:, None] * inv_freq], axis=-1)
    return jnp.cos(ang), jnp.sin(ang)

def _rope(t, cos, sin):
    half = RET_DK // 2
    t1, t2 = t[..., :half], t[..., half:]
    return jnp.concatenate([t1 * cos - t2 * sin, t2 * cos + t1 * sin], axis=-1)

def _chunk(t):
    b, h, n, d = t.shape
    return t.reshape(b, h, n // RET_CHUNK, RET_CHUNK, d)

def _decay_terms(lg):
    pos = jnp.arange(RET_CHUNK, dtype=jnp.float32)
    diff = pos[:, None] - pos[None, :]
    lower = diff >= 0
    d_intra = jnp.where(lower[None], jnp.exp(jnp.maximum(diff, 0.0)[None] * lg[:, None, None]), 0.0)
    xi = jnp.exp((pos[None] + 1.0) * lg[:, None])
    zeta = jnp.exp((RET_CHUNK - 1.0 - pos[None]) * lg[:, None])
    decay_chunk = jnp.exp(RET_CHUNK * lg)
    return d_intra, xi, zeta, decay_chunk

def _retention_states(k, v, lg, s0):
    _, _, zeta, decay_chunk = _decay_terms(lg)
    u = jnp.einsum('bhncd,hc,bhnce->nbhde', _chunk(k), zeta, _chunk(v))

    def step(s, u_i):
        return decay_chunk[None, :, None, None] * s + u_i, s

    final, prev = lax.scan(step, s0, u)
    return prev, final

def _retention_outputs(q, k, v, lg, prev):
    d_intra, xi, _, _ = _decay_terms(lg)
    qc, kc, vc = _chunk(q), _chunk(k), _chunk(v)
    scores = jnp.einsum('bhncd,bhnmd->bhncm', qc, kc) * d_intra[None, :, None]
    o = (jnp.einsum('bhncm,bhnme->bhnce', scores, vc)
         + jnp.einsum('bhncd,nbhde->bhnce', qc, prev) * xi[None, :, None, :, None])
    b, h, nc, cl, dv = o.shape
    return o.reshape(b, h, nc * cl, dv)

def _flip(t):
    return jnp.flip(t, axis=2)

def _group_norm(o):
    mu = jnp.mean(o, axis=-1, keepdims=True)
    var = jnp.mean(jnp.square(o - mu), axis=-1, keepdims=True)
    y = (o - mu) * lax.rsqrt(var + EPS)
    b, h, n, dv = y.shape
    return y.transpose(0, 2, 1, 3).reshape(b, n, h * dv)

def _gated_sum(o_f, o_b, g_f, g_b):
    y = (jax.nn.silu(g_f.astype(jnp.float32)) * _group_norm(o_f)
         + jax.nn.silu(g_b.astype(jnp.float32)) * _group_norm(o_b))
    return y.astype(g_f.dtype)

def _fourier_mix(u):
    b, n, _ = u.shape
    ug = u.astype(jnp.float32).reshape(b, n, FOURIER_GROUPS, FOURIER_CH)
    f = jnp.fft.fft2(ug, axes=(1, 3), norm="ortho").real
    return f.reshape(b, n, D_FOURIER).astype(u.dtype)

def _split_projection(p):
    i1 = D_RET_QK
    i2 = i1 + D_RET_QK
    i3 = i2 + D_RET_V
    i4 = i3 + D_RET_V
    i5 = i4 + D_RET_V
    return p[..., :i1], p[..., i1:i2], p[..., i2:i3], p[..., i3:i4], p[..., i4:i5], p[..., i5:]

def _retention_heads(q, k, v, rope=None):
    qh = _split_heads(q, RET_DK).astype(jnp.float32)
    kh = _split_heads(k, RET_DK).astype(jnp.float32) * (RET_DK ** -0.5)
    vh = _split_heads(v, RET_DV).astype(jnp.float32)
    if rope is not None:
        cos, sin = rope
        qh, kh = _rope(qh, cos, sin), _rope(kh, cos, sin)
    return qh, kh, vh

def setup_inputs(seed: int = 0) -> dict:
    key = jax.random.key(seed)
    ks = jax.random.split(key, 18)
    f32 = jnp.float32
    nrm = lambda k, shape, s: (jax.random.normal(k, shape, f32) * s)
    gain = lambda k, shape: 1.0 + 0.02 * jax.random.normal(k, shape, f32)
    base_decay = jnp.log(1.0 - 2.0 ** (-5.0 - jnp.arange(RET_HEADS, dtype=f32)))
    ret_log_decay = base_decay[None, None, :] * (1.0 + 0.05 * jax.random.normal(ks[11], (DEPTH, 2, RET_HEADS), f32))
    return {
        "x": nrm(ks[0], (BATCH, SEQ, D_MODEL), 1.0),
        "c": nrm(ks[1], (BATCH, D_MODEL), 1.0),
        "ctx": nrm(ks[2], (BATCH, CTX_LEN, D_MODEL), 1.0),
        "c_ctx": nrm(ks[3], (D_MODEL,), 1.0),
        "w_mod": nrm(ks[4], (DEPTH, D_MODEL, N_MOD * D_MODEL), 0.5 * D_MODEL ** -0.5),
        "b_mod": nrm(ks[5], (DEPTH, N_MOD * D_MODEL), 0.02),
        "norm_ffn1": gain(ks[6], (DEPTH, D_MODEL)),
        "w13_ffn1": nrm(ks[7], (DEPTH, D_MODEL, 2 * D_FF), D_MODEL ** -0.5),
        "w2_ffn1": nrm(ks[8], (DEPTH, D_FF, D_MODEL), D_FF ** -0.5),
        "norm_mix": gain(ks[9], (DEPTH, D_MODEL)),
        "w_in": nrm(ks[10], (DEPTH, D_MODEL, D_IN), D_MODEL ** -0.5),
        "ret_log_decay": ret_log_decay,
        "w_out": nrm(ks[12], (DEPTH, D_MIX, D_MODEL), D_MIX ** -0.5),
        "norm_ffn2": gain(ks[13], (DEPTH, D_MODEL)),
        "w13_ffn2": nrm(ks[14], (DEPTH, D_MODEL, 2 * D_FF), D_MODEL ** -0.5),
        "w2_ffn2": nrm(ks[15], (DEPTH, D_FF, D_MODEL), D_FF ** -0.5),
        "norm_final": gain(ks[16], (D_MODEL,)),
    }

def reference(x, c, ctx, c_ctx, w_mod, b_mod, norm_ffn1, w13_ffn1, w2_ffn1, norm_mix, w_in,
              ret_log_decay, w_out, norm_ffn2, w13_ffn2, w2_ffn2, norm_final):
    b, n, _ = x.shape
    n_rows = n // GRID_W
    rows = jnp.repeat(jnp.arange(n_rows), GRID_W)
    cols = jnp.tile(jnp.arange(GRID_W), n_rows)
    rope = _rope_tables(rows, cols)
    cond = jax.nn.silu(c)
    cond_ctx = jax.nn.silu(c_ctx)
    h, hc = x, ctx
    for l in range(DEPTH):
        last = l == DEPTH - 1
        m = jnp.split((cond @ w_mod[l] + b_mod[l])[:, None, :], N_MOD, axis=-1)
        mc = jnp.split((cond_ctx @ w_mod[l] + b_mod[l])[None, None, :], N_MOD, axis=-1)

        h = h + 0.5 * m[2] * _swiglu(_modulate(_rms_norm(h, norm_ffn1[l]), m[0], m[1]), w13_ffn1[l], w2_ffn1[l])
        hc = hc + 0.5 * mc[2] * _swiglu(_modulate(_rms_norm(hc, norm_ffn1[l]), mc[0], mc[1]), w13_ffn1[l], w2_ffn1[l])

        xn = _modulate(_rms_norm(h, norm_mix[l]), m[3], m[4])
        xcn = _modulate(_rms_norm(hc, norm_mix[l]), mc[3], mc[4])
        q_x, k_x, v_x, gf_x, gb_x, fu_x = _split_projection(xn @ w_in[l])
        q_c, k_c, v_c, gf_c, gb_c, fu_c = _split_projection(xcn @ w_in[l])
        qx, kx, vx = _retention_heads(q_x, k_x, v_x, rope)
        qc, kc, vc = _retention_heads(q_c, k_c, v_c)
        lg = ret_log_decay[l].astype(jnp.float32)
        lg_f, lg_b = lg[0], lg[1]
        zeros = jnp.zeros((b, RET_HEADS, RET_DK, RET_DV), jnp.float32)

        prev_cf, s_cf = _retention_states(kc, vc, lg_f, zeros)
        prev_cb, s_cb = _retention_states(_flip(kc), _flip(vc), lg_b, zeros)
        prev_lf, _ = _retention_states(kx, vx, lg_f, s_cf)
        o_lf = _retention_outputs(qx, kx, vx, lg_f, prev_lf)
        prev_lb, _ = _retention_states(_flip(kx), _flip(vx), lg_b, s_cb)
        o_lb = _flip(_retention_outputs(_flip(qx), _flip(kx), _flip(vx), lg_b, prev_lb))
        ret_x = _gated_sum(o_lf, o_lb, gf_x, gb_x)
        four_x = _fourier_mix(fu_x)
        h = h + m[5] * (jnp.concatenate([ret_x, four_x], axis=-1) @ w_out[l])

        if not last:
            o_cf = _retention_outputs(qc, kc, vc, lg_f, prev_cf)
            o_cb = _flip(_retention_outputs(_flip(qc), _flip(kc), _flip(vc), lg_b, prev_cb))
            ret_c = _gated_sum(o_cf, o_cb, gf_c, gb_c)
            four_c = _fourier_mix(fu_c)
            hc = hc + mc[5] * (jnp.concatenate([ret_c, four_c], axis=-1) @ w_out[l])

        h = h + 0.5 * m[8] * _swiglu(_modulate(_rms_norm(h, norm_ffn2[l]), m[6], m[7]), w13_ffn2[l], w2_ffn2[l])
        if not last:
            hc = hc + 0.5 * mc[8] * _swiglu(_modulate(_rms_norm(hc, norm_ffn2[l]), mc[6], mc[7]), w13_ffn2[l], w2_ffn2[l])

    return _rms_norm(h, norm_final)


_drawn_inputs = setup_inputs


def setup_inputs(seed=0):
    import zlib

    import numpy as np

    out = dict(_drawn_inputs(seed))
    spreads = {}
    factors = {'norm_ffn1': 8.0, 'norm_mix': 32.967, 'norm_ffn2': 22.326, 'norm_final': 8.366}
    for name, (base, spread) in spreads.items():
        noise = np.random.default_rng([zlib.crc32(name.encode()), seed]).standard_normal(out[name].shape)
        drawn = base * np.exp(spread * noise) if base else spread * noise
        out[name] = __import__('jax').numpy.asarray(drawn.astype(out[name].dtype))
    for name, factor in factors.items():
        out[name] = (out[name] * factor).astype(out[name].dtype)
    return out
```

```python
from contextlib import ExitStack

import numpy as np

import concourse.bass as bass
from concourse import mybir
from concourse.alu_op_type import AluOpType as ALU

F32 = mybir.dt.float32
F32R = mybir.dt.float32r
ACT = mybir.ActivationFunctionType

P = 128
D = 1024
KT = D // P
SEQ, CTX = 1024, 256
TOK = SEQ + CTX
FF = 2816
FT = FF // P
GROUPS = FT // 2
NMOD = 9
H, DK, DV = 4, 64, 128
FG, FC = 4, 128
CH = 128
NCH, NCC = SEQ // CH, CTX // CH
EPS = 1e-6
SLOTS = 3
UNIT = 1024
HALF = 512
NQ = SEQ // 4

UP_UNITS = 6
U_FFN1 = 0
U_MIX = U_FFN1 + UP_UNITS * GROUPS
MIX_GROUPS = (("fu", 4), ("kc", 0), ("vc", 1), ("qk", 0), ("v", 1), ("gf", 2), ("gb", 3))
U_DFT = U_MIX + 4 * len(MIX_GROUPS)
U_OUT = U_DFT + 4
U_FFN2 = U_OUT + KT
U_END = U_FFN2 + UP_UNITS * GROUPS
LO_BIAS = SLOTS


def ring(u):
    return u if u < U_DFT else u - 4


class Ffn:

    def __init__(self, tag, u0, chunks, gate, with_mods):
        self.tag, self.u0, self.chunks, self.gate, self.with_mods = tag, u0, chunks, gate, with_mods
        self.C = len(chunks)


LAT = ((0, 512, 0), (512, 512, 0))
ALL = LAT + ((1024, 256, 1),)


def slab_offset(nc, slab):
    return nc.lookup_mloc(slab.name).addr


def build(nc, t):
    ctx = ExitStack()
    with ctx:
        sem = lambda name: ctx.enter_context(nc.semaphore(name))

        slab = ctx.enter_context(nc.sbuf_tensor("slab", [P, 53000], F32))
        base = slab_offset(nc, slab)

        def place(name, words, offset, dtype=F32, shape=None):
            return nc.alloc_sbuf_tensor_at(name, [P, words] if shape is None else [P, *shape], dtype,
                                           offset=base + 4 * offset)

        o = 0
        h_lat = place("h_lat", 0, o, shape=[KT, SEQ]); o += KT * SEQ
        O_HCTX = o
        h_ctx = place("h_ctx", 0, o, shape=[KT, CTX]); o += KT * CTX
        O_X = o
        x_hi = place("x_hi", 0, o, F32R, [KT, TOK]); o += KT * TOK
        x_lo = place("x_lo", 0, o, F32R, [KT, TOK]); o += KT * TOK
        w_hi = place("w_hi", 0, o, F32R, [SLOTS, UNIT]); o += SLOTS * UNIT
        w_lo = place("w_lo", 0, o, F32R, [SLOTS, UNIT]); o += SLOTS * UNIT
        stage = place("stage", 0, o, shape=[SLOTS, UNIT]); o += SLOTS * UNIT
        O_R = o
        g_hi = place("g_hi", 0, o, F32R, [2, TOK]); o += 2 * TOK
        g_lo = place("g_lo", 0, o, F32R, [2, TOK]); o += 2 * TOK
        scr = place("scr", 0, o, shape=[7, HALF]); o += 7 * HALF
        mod_stage = place("mod_stage", 0, o, shape=[2, UNIT]); o += 2 * UNIT
        def small(name, *shape):
            nonlocal o
            words = int(np.prod(shape))
            x = place(name, 0, o, shape=list(shape)); o += words + (-words) % 8
            return x
        mods = small("mods", NMOD, KT, 2)
        b_mod = small("b_mod", NMOD * KT)
        gains = small("gains", 4, KT)
        cond = small("cond", KT, 2)
        acol = small("acol", 3, KT, 2)
        atmp = small("atmp", KT, 2)
        ghalf = small("ghalf", 2, KT, 2)
        lg = small("lg", 2, H)
        pvec = small("pvec", 2, 2)
        zx = small("zx", 2, 2, H)
        dcs = small("dcs", H)
        stats = small("stats", 2 * H, 6)
        mv = small("mv", 2 * H, 2)
        rs = small("rs", 2 * H)
        nmr = small("nmr", 2 * H)
        ones = small("ones", P)
        ident = small("ident", P)
        chan = small("chan", 2 * FC)
        O_ROPE = o
        rope = small("rope", NCH, 2, DK // 2)
        rtmp = small("rtmp", 2, 2 * H, DK // 2)
        assert o <= 53000, o

        mod_pre = place("mod_pre", 0, O_X, shape=[2 * KT, UNIT])
        qk = place("qk", 0, O_R, shape=[NCH, HALF])
        ab_out = place("ab_out", 0, O_R, shape=[4, UNIT])
        kc = place("kc", 0, O_R + 4096, shape=[NCC, H * DK])
        v = place("v", 0, O_R + 4608, shape=[NCH + NCC, HALF])
        ut = place("ut", 0, O_R + 4608, shape=[FG, SEQ])
        gbuf_a = place("gbuf_a", 0, O_R + 9728, shape=[2, HALF])
        gbuf_b = place("gbuf_b", 0, O_HCTX, shape=[4, HALF])
        q = O_X
        ret_hi = place("ret_hi", 0, q, F32R, [H, SEQ]); q += H * SEQ
        ret_lo = place("ret_lo", 0, q, F32R, [H, SEQ]); q += H * SEQ
        O_TMP = q
        ust = place("ust", 0, q, shape=[NCH + NCC, H * DV]); q += (NCH + NCC) * H * DV
        qx = place("qx", 0, q, shape=[H, P]); q += 512
        qT = place("qT", 0, q, shape=[H, CH]); q += 512
        kT = place("kT", 0, q, shape=[H, CH]); q += 512
        qxT = place("qxT", 0, q, shape=[2, H, CH]); q += 1024
        pr = place("pr", 0, q, shape=[2, H, CH])
        dmask = place("dmask", 0, q, shape=[2, 2, CH]); q += 1024
        on = place("on", 0, q, shape=[2, H, DV])
        kz = place("kz", 0, q, shape=[2, H, P]); q += 1024
        gin = place("gin", 0, q, shape=[2, 2, HALF]); q += 2048
        y = place("y", 0, q, shape=[H, DV]); q += 512
        assert q <= O_X + 2 * KT * TOK
        dm = place("dm", 0, O_R + 9728, shape=[2, H, CH])
        q = O_TMP
        df_hi = place("df_hi", 0, q, F32R, [4, UNIT]); q += 4096
        df_lo = place("df_lo", 0, q, F32R, [4, UNIT]); q += 4096
        z_hi = place("z_hi", 0, q, F32R, [4, 2, 2, FC]); q += 2048
        z_lo = place("z_lo", 0, q, F32R, [4, 2, 2, FC]); q += 2048
        assert q <= O_X + 2 * KT * TOK
        four_hi = place("four_hi", 0, O_R, F32R, [FG, SEQ])
        four_lo = place("four_lo", 0, O_R + 4096, F32R, [FG, SEQ])
        abuf = place("abuf", 0, O_R + 8192, shape=[4, 2, 2, FC])
        zf = place("zf", 0, O_HCTX, shape=[4, 2, 2, FC])
        ebuf = place("ebuf", 0, O_ROPE, shape=[2, 2, 2, FC])

        ps = ctx.enter_context(nc.psum_tensor("ps", [P, 8, HALF], F32))
        ab_dram = nc.dram_tensor("ab_dram", (NCH, P, UNIT), F32).ap()
        gate_dram = nc.dram_tensor("gate_dram", (NCH, P, 2, HALF), F32).ap()

        stage_in = [sem(f"stage_in{i}") for i in range(SLOTS)]
        hi_done, lo_done, mix_unit = sem("hi_done"), sem("lo_done"), sem("mix_unit")
        mod_in = [sem(f"mod_in{i}") for i in range(2)]
        mod_used, mod_mm, mod_ready = sem("mod_used"), sem("mod_mm"), sem("mod_ready")
        gate_ready = sem("gate_ready")
        pre_in, x_in, small_in, cond_ready, ones_set = (sem(n) for n in ("pre_in", "x_in", "small_in", "cond_ready", "ones_set"))
        dve_step, act_prep = sem("dve_step"), sem("act_prep")

        FFN = [Ffn("1", U_FFN1, ALL, 0, True), Ffn("2", U_FFN2, LAT, 1, False)]
        for f in FFN:
            f.up_done, f.silu_done, f.mult_done, f.ghi_done, f.glo_done, f.down_done, f.acc_done = (
                sem(n + f.tag) for n in ("up_done", "silu_done", "mult_done", "ghi_done", "glo_done", "down_done", "acc_done"))

        class Norm:
            pass
        NORM = []
        for tag, chunks, shift, scale, gain in (("a", ALL, 0, 1, 0), ("m", ALL, 3, 4, 1), ("b", LAT, 6, 7, 2), ("f", LAT, None, None, 3)):
            n = Norm()
            n.tag, n.chunks, n.shift, n.scale, n.gain = tag, chunks, shift, scale, gain
            n.sq, n.add, n.stat, n.var, n.root, n.rec, n.t, n.xf, n.hi, n.lo = (
                sem(s + "_" + tag) for s in ("n_sq", "n_add", "n_stat", "n_var", "n_root", "n_rec", "n_t", "n_xf", "n_hi", "n_lo"))
            NORM.append(n)
        acol_ready = sem("acol_ready")

        mix_mm, mix_act, mix_dve = sem("mix_mm"), sem("mix_act"), sem("mix_dve")
        ab_spill = [sem(f"ab_spill{i}") for i in range(4)]
        gate_spill = [sem(f"gate_spill{i}") for i in range(6)]
        rope_done = sem("rope_done")
        mask_in, dm_exp, dm_done = sem("mask_in"), sem("dm_exp"), sem("dm_done")
        kz_done, u_mm, u_ev, rec_done = sem("kz_done"), sem("u_mm"), sem("u_ev"), sem("rec_done")
        qx_done, t_mm, t_act, t_dve = sem("qx_done"), sem("t_mm"), sem("t_act"), sem("t_dve")
        s_mm, p_done, o_mm, var_done, root_done, rs_done = (sem(n) for n in ("s_mm", "p_done", "o_mm", "var_done", "root_done", "rs_done"))
        on_done, y_done, y_mm, yhi_done, ylo_done = (sem(n) for n in ("on_done", "y_done", "y_mm", "yhi_done", "ylo_done"))
        gate_in = [sem(f"gate_in{i}") for i in range(2)]
        ab_in, z_done, zhi_done, zlo_done, f_mm, fhi_done, flo_done = (
            sem(n) for n in ("ab_in", "z_done", "zhi_done", "zlo_done", "f_mm", "fhi_done", "flo_done"))
        out_mm, out_acc = sem("out_mm"), sem("out_acc")
        fin_done, stored = sem("fin_done"), sem("stored")

        block = ctx.enter_context(nc.Block())

        def h_of(m, chunk):
            start, n, which = chunk
            return h_ctx[:, m, :] if which else h_lat[:, m, start:start + n]

        outs = []
        for name, _ in MIX_GROUPS:
            if name == "fu":
                outs += [("fu", n, (n,), "ad"[n % 2 == 0]) for n in range(8)]
            elif name == "kc":
                outs += [("kc", n, (n,), "a") for n in range(NCC)]
            elif name == "vc":
                outs += [("vc", n, (2 + n,), "da"[n]) for n in range(NCC)]
                outs += [("ab", n, (4 + 2 * (n % 2), 5 + 2 * (n % 2)), "a") for n in range(NCH)]
            else:
                outs += [(name, n, (n,), "a" if name in ("gf", "gb") else "ad"[n % 2 == 0]) for n in range(NCH)]
        order = {}
        counts = {"a": 0, "d": 0}
        last_in_bank = {}
        for n, (kind, i, banks, who) in enumerate(outs):
            counts[who] += 1
            before = [last_in_bank[b] for b in banks if b in last_in_bank]
            order[kind, i] = (n + 1, who, counts[who], before)
            for b in banks:
                last_in_bank[b] = (who, counts[who])
        MIX_A, MIX_D = counts["a"], counts["d"]

        def wait_copied(e, who, count):
            e.wait_ge(mix_act if who == "a" else mix_dve, count)

        def mm3(pe, out, wh, wl, xh, xl, start, stop):
            pe.matmul(out, wl, xh, start=start, stop=False)
            pe.matmul(out, wh, xl, start=False, stop=False)
            return pe.matmul(out, wh, xh, start=False, stop=stop)

        @block.sync
        def _(sp):
            def unit(u, src, more=0):
                s = u % SLOTS
                sp.wait_ge(lo_done, more + (u - SLOTS + 1 + LO_BIAS))
                sp.dma_start(stage[:, s, :], src).then_inc(stage_in[s], 16)

            sp.dma_start(cond[:, :, :], t["cond"]).then_inc(small_in, 16)
            sp.dma_start(b_mod[:, :], t["b_mod"]).then_inc(small_in, 16)
            sp.dma_start(gains[:, :, :], t["gains"]).then_inc(small_in, 16)
            for dst, name in ((ident[:, :], "ident"), (chan[:, :], "chan"), (pvec[:, :, :], "pvec"),
                              (rope[:, :, :, :], "rope")):
                sp.dma_start(dst, t[name]).then_inc(small_in, 16)
            sp.dma_start(lg[:, :, :], t["lg"]).then_inc(small_in, 16)
            for m in range(KT):
                sp.dma_start(h_lat[:, m, :], t["x"][m]).then_inc(x_in, 16)
                sp.dma_start(h_ctx[:, m, :], t["ctx"][m]).then_inc(x_in, 16)
            for n in range(4):
                sp.dma_start(mod_pre[:, 4 * n:4 * n + 4, :],
                             t["w_mod"][4 * n:4 * n + 4].rearrange("n p c -> p n c")).then_inc(pre_in, 16)

            def ffn_units(f, w13, w2):
                def body(i, mod):
                    for u in range(UP_UNITS):
                        src = w13[bass.ds(4 * i + u, 1)] if u < 4 else w2[bass.ds(2 * i + (u - 4), 1)]
                        unit(f.u0 + u, src.rearrange("o p c -> (o p) c"), UP_UNITS * i)
                        if mod and u < 4:
                            for j in (2 * u, 2 * u + 1):
                                sp.wait_ge(mod_used, KT * i + (j + 1))
                                sp.dma_start(mod_stage[:, j % 2, :],
                                             t["w_mod"][bass.ds(KT * i + (2 * KT + j), 1)].rearrange("o p c -> (o p) c"))\
                                    .then_inc(mod_in[j % 2], 16)
                cut = NMOD - 2 if f.with_mods else 0
                if cut:
                    with sp.Fori(0, cut) as i:
                        body(i, True)
                with sp.Fori(cut, GROUPS) as i:
                    body(i, False)

            ffn_units(FFN[0], t["w13_1"], t["w2_1"])
            for g, (name, cols) in enumerate(MIX_GROUPS):
                for u in range(4):
                    unit(U_MIX + 4 * g + u, t["w_in"][cols, u])
            for u in range(3):
                unit(U_DFT + u, t["dft"][u])
            sp.wait_ge(mix_mm, len(outs))
            sp.dma_start(dmask[:, :, :, :], t["dmask"]).then_inc(mask_in, 16)
            for n in range(6):
                sp.wait_ge(gate_spill[n], 16 * len(range(n, 2 * NCH, 6)))
            for i in range(NCH):
                if i >= 2:
                    sp.wait_ge(y_done, i - 1)
                sp.dma_start(gin[:, i % 2, :, :], gate_dram[i]).then_inc(gate_in[i % 2], 16)
            unit(U_DFT + 3, t["dft"][3])
            for n in range(4):
                sp.wait_ge(ab_spill[n], 16 * 2)
            for g in range(FG):
                if g == 0:
                    sp.wait_ge(y_mm, NCH)
                    sp.wait_ge(ylo_done, NCH)
                else:
                    sp.wait_ge(z_done, g)
                sp.dma_start(abuf[:, :, :, :, :].rearrange("p j t a c -> p (j t) (a c)"),
                             ab_dram[:, :, g * 2 * FC:(g + 1) * 2 * FC].rearrange("t p c -> p t c")).then_inc(ab_in, 16)
                if g == 0:
                    for u in range(3):
                        unit(U_OUT + u, t["w_out"][u])
            for u in range(3, KT):
                unit(U_OUT + u, t["w_out"][u])
            ffn_units(FFN[1], t["w13_2"], t["w2_2"])
            for c in range(2):
                for m in range(KT):
                    sp.wait_ge(fin_done, c * KT + m + 1)
                    sp.dma_start(t["out"][m, :, c * HALF:(c + 1) * HALF], h_lat[:, m, c * HALF:(c + 1) * HALF]).then_inc(stored, 16)
            sp.wait_ge(stored, 16 * 2 * KT)

        @block.tensor
        def _(pe):
            def norm_stat(n):
                for c, (start, size, which) in enumerate(n.chunks):
                    pe.wait_ge(n.add, (KT - 1) * (c + 1))
                    if c:
                        pe.wait_ge(n.var, c)
                    pe.matmul(ps[:, 7, 0:size], ones[:, :], scr[:, 2, 0:size], start=True, stop=True).then_inc(n.stat, 1)

            def mod_tile(w, col):
                for k in range(KT):
                    mm = pe.matmul(col, w[:, k * P:(k + 1) * P], cond[:, k, :], start=(k == 0), stop=(k == KT - 1))
                return mm

            def ffn(f, n):
                C = f.C

                def body(i, mod):
                    for u in range(4):
                        s = ring(f.u0 + u) % SLOTS
                        pe.wait_ge(lo_done, UP_UNITS * i + (f.u0 + u + 1 + LO_BIAS))
                        for c, (start, size, _) in enumerate(f.chunks):
                            b = (u % 2) * C + c
                            if u < 2:
                                pe.wait_ge(f.acc_done, KT * C * i + (b + 1))
                            elif u == 2:
                                pe.wait_ge(f.silu_done, 2 * C * i + (c + 1))
                            else:
                                pe.wait_ge(f.mult_done, 2 * C * i + (c + 1))
                            for k in range(KT):
                                w = slice(k * P, (k + 1) * P)
                                mm = mm3(pe, ps[:, b, 0:size], w_hi[:, s, w], w_lo[:, s, w],
                                         x_hi[:, k, start:start + size], x_lo[:, k, start:start + size], k == 0, k == KT - 1)
                            mm.then_inc(f.up_done, 1)
                        if mod:
                            for j in (2 * u, 2 * u + 1):
                                if j == 0:
                                    pe.wait_ge(mod_ready, i + 2)
                                pe.wait_ge(mod_in[j % 2], 16 * 4 * i + 16 * (j // 2 + 1))
                                mod_tile(mod_stage[:, j % 2, :], ps[:, 6, 2 * j:2 * j + 2]).then_inc(mod_used, 1)
                    s4, s5 = (ring(f.u0 + u) % SLOTS for u in (4, 5))
                    pe.wait_ge(lo_done, UP_UNITS * i + (f.u0 + 6 + LO_BIAS))
                    step = 0
                    for c, (start, size, _) in enumerate(f.chunks):
                        pe.wait_ge(f.glo_done, 2 * C * i + (2 * C + c + 1))
                        for m in range(KT):
                            b = step % (2 * C)
                            if step < C:
                                pe.wait_ge(f.silu_done, 2 * C * i + (C + step + 1))
                            elif step < 2 * C:
                                pe.wait_ge(f.mult_done, 2 * C * i + (step + 1))
                            else:
                                pe.wait_ge(f.acc_done, KT * C * i + (step + 1))
                            w = slice(m * P, (m + 1) * P)
                            for j, s in enumerate((s4, s5)):
                                mm = mm3(pe, ps[:, b, 0:size], w_hi[:, s, w], w_lo[:, s, w],
                                         g_hi[:, j, start:start + size], g_lo[:, j, start:start + size], j == 0, j == 1)
                            mm.then_inc(f.down_done, 1)
                            step += 1

                pe.wait_ge(n.lo, KT * C)
                cut = NMOD - 2 if f.with_mods else 0
                if cut:
                    with pe.Fori(0, cut) as i:
                        body(i, True)
                with pe.Fori(cut, GROUPS) as i:
                    body(i, False)

            pe.wait_ge(cond_ready, 1)
            for n in range(2 * KT):
                if n % 4 == 0:
                    pe.wait_ge(pre_in, 16 * 4)
                mm = mod_tile(mod_pre[:, n, :], ps[:, 5 + n // KT, 2 * (n % KT):2 * (n % KT) + 2])
                if n % KT == KT - 1:
                    mm.then_inc(mod_mm, 1)
            pe.wait_ge(ones_set, 1)
            norm_stat(NORM[0])
            ffn(FFN[0], NORM[0])
            norm_stat(NORM[1])

            def banks_free(kind, i):
                for who, count in order[kind, i][3]:
                    wait_copied(pe, who, count)

            pe.wait_ge(NORM[1].lo, KT * 3)
            pe.wait_ge(FFN[0].acc_done, 2 * 3 + KT * 3 * GROUPS)
            for g, (name, _) in enumerate(MIX_GROUPS):
                for u in range(4):
                    U = U_MIX + 4 * g + u
                    s = ring(U) % SLOTS
                    pe.wait_ge(lo_done, U + 1 + LO_BIAS)
                    for kk in range(2):
                        k = 2 * u + kk
                        n_out = NCC if name in ("kc", "vc") else 8
                        for n in range(n_out):
                            if k == 0:
                                banks_free(name, n)
                            w0 = kk * HALF
                            if name == "fu":
                                fg, c = n // 2, n % 2
                                w = slice(w0 + fg * FC, w0 + (fg + 1) * FC)
                                mm = mm3(pe, ps[:, n, :], w_hi[:, s, w], w_lo[:, s, w],
                                         x_hi[:, k, c * HALF:(c + 1) * HALF], x_lo[:, k, c * HALF:(c + 1) * HALF], k == 0, k == KT - 1)
                            else:
                                tok = slice(n * P, (n + 1) * P) if n_out == 8 else slice(SEQ + n * P, SEQ + (n + 1) * P)
                                w = slice(w0 + H * DK, w0 + HALF) if name == "kc" else slice(w0, w0 + HALF)
                                bank = n + (NCC if name == "vc" else 0)
                                mm = mm3(pe, ps[:, bank, 0:w.stop - w.start], x_hi[:, k, tok], x_lo[:, k, tok],
                                         w_hi[:, s, w], w_lo[:, s, w], k == 0, k == KT - 1)
                            if k == KT - 1:
                                mm.then_inc(mix_mm, 1)
                    if u < 3:
                        mm.then_inc(mix_unit, 1)
                if name == "vc":
                    for kind_i in range(8):
                        _, who, count, _ = order["fu", kind_i]
                        wait_copied(pe, who, count)
                    for n in range(NCH):
                        banks_free("ab", n)
                        for fg in range(FG):
                            mm = pe.matmul(ps[:, 4 + 2 * (n % 2) + fg // 2, (fg % 2) * 2 * FC:(fg % 2 + 1) * 2 * FC],
                                           ut[:, fg, n * P:(n + 1) * P], chan[:, :], start=True, stop=True)
                        mm.then_inc(mix_mm, 1)

            pe.wait_ge(mix_act, MIX_A)
            pe.wait_ge(mix_dve, MIX_D)
            for st in range(NCC + NCH):
                pe.wait_ge(kz_done, st + 1)
                if st >= 2:
                    pe.wait_ge(u_ev, st - 1)
                for hd in range(H):
                    mm = pe.matmul(ps[:, st % 2, hd * DV:(hd + 1) * DV], kz[:, st % 2, hd, :],
                                   v[:, (NCH + st) if st < NCC else st - NCC, hd * DV:(hd + 1) * DV], start=True, stop=True)
                mm.then_inc(u_mm, 1)
            pe.wait_ge(u_ev, NCC + NCH)

            def turn(i):
                pe.wait_ge(qx_done, i + 1)
                if i:
                    pe.wait_ge(t_act, i)
                    pe.wait_ge(t_dve, i)
                for hd in range(H):
                    pe.transpose(ps[0:DK, 0, hd * CH:(hd + 1) * CH], qk[:, i, hd * DK:(hd + 1) * DK], ident[:, :])
                for hd in range(H):
                    pe.transpose(ps[0:DK, 1, hd * CH:(hd + 1) * CH], qk[:, i, (H + hd) * DK:(H + hd + 1) * DK], ident[:, :])
                for hd in range(H):
                    mm = pe.transpose(ps[:, 2, hd * CH:(hd + 1) * CH], qx[:, hd, :], ident[:, :])
                mm.then_inc(t_mm, 1)

            def turn_y(i):
                pe.wait_ge(y_done, i + 1)
                if i:
                    pe.wait_ge(ylo_done, i)
                for hd in range(H):
                    mm = pe.transpose(ps[:, 6, hd * DV:(hd + 1) * DV], y[:, hd, :], ident[:, :])
                mm.then_inc(y_mm, 1)

            pe.wait_ge(rope_done, NCH)
            turn(0)
            for i in range(NCH):
                pe.wait_ge(t_act, i + 1)
                if i:
                    pe.wait_ge(p_done, i)
                for hd in range(H):
                    mm = pe.matmul(ps[:, 3, hd * CH:(hd + 1) * CH], kT[0:DK, hd, :], qT[0:DK, hd, :], start=True, stop=True)
                mm.then_inc(s_mm, 1)
                if i < NCH - 1:
                    turn(i + 1)
                pe.wait_ge(p_done, i + 1)
                pe.wait_ge(t_dve, i + 1)
                if i:
                    pe.wait_ge(on_done, i)
                else:
                    pe.wait_ge(rec_done, NCH)
                for d in range(2):
                    rows = slice(d * DK, (d + 1) * DK)
                    prev = 1 + (i if d == 0 else NCH - 1 - i)
                    for hd in range(H):
                        o_ = ps[:, 4 + d, hd * DV:(hd + 1) * DV]
                        pe.matmul(o_, pr[:, d, hd, :], v[:, i, hd * DV:(hd + 1) * DV], start=True, stop=False)
                        mm = pe.matmul(o_, qxT[rows, i % 2, hd, :], ust[rows, prev, hd * DV:(hd + 1) * DV], start=False, stop=True)
                mm.then_inc(o_mm, 1)
                if i:
                    turn_y(i - 1)
            turn_y(NCH - 1)

            pe.wait_ge(lo_done, U_DFT + 4 + LO_BIAS)
            pe.wait_ge(ylo_done, NCH)
            for fg in range(FG):
                pe.wait_ge(zlo_done, fg + 1)
                for s in range(4):
                    n = 4 * fg + s
                    if n >= 8:
                        pe.wait_ge(flo_done, n - 7)
                    b = n % 8
                    for ta in range(4):
                        w = z_hi[:, s, ta // 2, ta % 2, :], z_lo[:, s, ta // 2, ta % 2, :]
                        cols = slice(s * NQ, (s + 1) * NQ)
                        mm = mm3(pe, ps[:, b, 0:NQ], *w, df_hi[:, ta, cols], df_lo[:, ta, cols], ta == 0, ta == 3)
                    mm.then_inc(f_mm, 1)

            pe.wait_ge(flo_done, 4 * FG)
            for m in range(KT):
                U = U_OUT + m
                s = ring(U) % SLOTS
                pe.wait_ge(lo_done, U + 1 + LO_BIAS)
                for c in range(2):
                    n = 2 * m + c
                    if n >= 4:
                        pe.wait_ge(out_acc, n - 3)
                    cols = slice(c * HALF, (c + 1) * HALF)
                    for k in range(KT):
                        xh, xl = (ret_hi[:, k, cols], ret_lo[:, k, cols]) if k < H else (four_hi[:, k - H, cols], four_lo[:, k - H, cols])
                        w = slice(k * P, (k + 1) * P)
                        mm = mm3(pe, ps[:, n % 4, :], w_hi[:, s, w], w_lo[:, s, w], xh, xl, k == 0, k == KT - 1)
                    mm.then_inc(out_mm, 1)
            norm_stat(NORM[2])
            ffn(FFN[1], NORM[2])
            norm_stat(NORM[3])

        @block.scalar
        def _(act):
            def hi(u, i=None, dst=None):
                s = u % SLOTS
                landed = 16 * (u // SLOTS + 1)
                act.wait_ge(stage_in[s], landed if i is None else i * (16 * UP_UNITS // SLOTS) + landed)
                act.activation(w_hi[:, ring(u) % SLOTS, :] if dst is None else dst, stage[:, s, :], ACT.Copy).then_inc(hi_done, 1)

            def added(q):
                return q // KT * (KT - 1) + max(q % KT, 1)

            def norm(n, ready):
                for c, chunk in enumerate(n.chunks):
                    size = chunk[1]
                    ready(act, c)
                    for m in range(KT):
                        q = c * KT + m
                        if q >= 2:
                            act.wait_ge(n.add, added(q - 2))
                        act.activation(scr[:, q % 2, 0:size], h_of(m, chunk), ACT.Square).then_inc(n.sq, 1)
                    act.wait_ge(n.var, c + 1)
                    act.activation(scr[:, 3, 0:size], scr[:, 3, 0:size], ACT.Sqrt).then_inc(n.root, 1)
                    if n.shift is None:
                        continue
                    if c == 0:
                        act.wait_ge(acol_ready, NORM.index(n) + 1)
                    for m in range(KT):
                        q = c * KT + m
                        act.wait_ge(n.t, q + 1)
                        x = scr[:, 4 + q % 3, 0:size]
                        act.activation(x, x, ACT.Identity, scale=acol[:, NORM.index(n), m, chunk[2]:chunk[2] + 1],
                                       bias=mods[:, n.shift, m, chunk[2]:chunk[2] + 1]).then_inc(n.xf, 1)

            def ffn(f):
                C = f.C

                def body(i, last):
                    for u in range(4):
                        for c, (start, size, _) in enumerate(f.chunks):
                            if u % 2 == 0:
                                act.wait_ge(f.up_done, 4 * C * i + (u * C + c + 1))
                                if u == 2:
                                    act.wait_ge(f.mult_done, 2 * C * i + (c + 1))
                                act.activation(scr[:, c, 0:size], ps[:, c, 0:size], ACT.Silu).then_inc(f.silu_done, 1)
                            else:
                                act.wait_ge(f.mult_done, 2 * C * i + ((u // 2) * C + c + 1))
                                act.activation(g_hi[:, u // 2, start:start + size], scr[:, 3 + c, 0:size], ACT.Copy)\
                                    .then_inc(f.ghi_done, 1)
                        if last and u + SLOTS >= UP_UNITS:
                            continue
                        act.wait_ge(f.up_done, 4 * C * i + (u + 1) * C)
                        hi(f.u0 + u + SLOTS, i)
                    if last:
                        return
                    act.wait_ge(f.down_done, KT * C * i + KT * C)
                    hi(f.u0 + 4 + SLOTS, i)
                    hi(f.u0 + 5 + SLOTS, i)

                end = f.u0 + UP_UNITS * GROUPS == U_END
                with act.Fori(0, GROUPS - end) as i:
                    body(i, False)
                if end:
                    body(GROUPS - 1, True)

            act.wait_ge(small_in, 16 * 8)
            act.activation(cond[:, :, :], cond[:, :, :], ACT.Silu).then_inc(cond_ready, 1)
            act.wait_ge(dve_step, 1)
            act.activation(zx[:, :, :, :], zx[:, :, :, :], ACT.Exp).then_inc(act_prep, 1)
            for d in range(2):
                rows = slice(d * DK, (d + 1) * DK)
                act.activation(dcs[rows, :], lg[rows, d, :], ACT.Exp, scale=float(CH)).then_inc(act_prep, 1)

            norm(NORM[0], lambda e, c: e.wait_ge(x_in, 16 * 2 * KT))
            for u in range(SLOTS):
                hi(u)
            ffn(FFN[0])
            norm(NORM[1], lambda e, c: e.wait_ge(FFN[0].acc_done, 2 * 3 + KT * 3 * (GROUPS - 1) + KT * (c + 1)))

            def copy_out(kind, i):
                mm, who, _, _ = order[kind, i]
                if who != "a":
                    return
                act.wait_ge(mix_mm, mm)
                if kind == "fu":
                    act.activation(ut[:, i // 2, (i % 2) * HALF:(i % 2 + 1) * HALF], ps[:, i, :], ACT.Copy).then_inc(mix_act, 1)
                elif kind == "kc":
                    act.activation(kc[:, i, :], ps[:, i, 0:H * DK], ACT.Copy, scale=DK ** -0.5).then_inc(mix_act, 1)
                elif kind == "vc":
                    act.activation(v[:, NCH + i, :], ps[:, 2 + i, :], ACT.Copy).then_inc(mix_act, 1)
                elif kind == "ab":
                    if i >= 4:
                        act.wait_ge(ab_spill[i % 4], 16 * (i // 4))
                    b = 4 + 2 * (i % 2)
                    act.activation(ab_out[:, i % 4, :].rearrange("p (b c) -> p b c", b=2), ps[:, b:b + 2, :], ACT.Copy).then_inc(mix_act, 1)
                    act.wait_ge(mix_act, order[kind, i][2])
                    act.dma_start(ab_dram[i], ab_out[:, i % 4, :]).then_inc(ab_spill[i % 4], 16)
                elif kind == "qk":
                    if i == 1:
                        for n in range(4):
                            act.wait_ge(ab_spill[n], 32)
                    act.activation(qk[:, i, 0:H * DK], ps[:, i, 0:H * DK], ACT.Copy)
                    act.activation(qk[:, i, H * DK:HALF], ps[:, i, H * DK:HALF], ACT.Copy, scale=DK ** -0.5).then_inc(mix_act, 1)
                elif kind == "v":
                    act.activation(v[:, i, :], ps[:, i, :], ACT.Copy).then_inc(mix_act, 1)
                else:
                    n = i + (NCH if kind == "gb" else 0)
                    if n >= 6:
                        act.wait_ge(gate_spill[n % 6], 16 * (n // 6))
                    gb = gbuf_a[:, n % 6, :] if n % 6 < 2 else gbuf_b[:, n % 6 - 2, :]
                    act.activation(gb, ps[:, i, :], ACT.Silu).then_inc(mix_act, 1)
                    act.wait_ge(mix_act, order[kind, i][2])
                    act.dma_start(gate_dram[i, :, n // NCH, :], gb).then_inc(gate_spill[n % 6], 16)

            for g, (name, _) in enumerate(MIX_GROUPS):
                n_out = NCC if name in ("kc", "vc") else 8
                U = U_MIX + 4 * g + SLOTS
                for u in range(3):
                    if U + u < U_DFT:
                        act.wait_ge(mix_unit, 3 * g + u + 1)
                        hi(U + u)
                for i in range(n_out):
                    copy_out(name, i)
                if U + 3 < U_DFT:
                    act.wait_ge(mix_mm, order[name, n_out - 1][0])
                    hi(U + 3)
                if name == "vc":
                    for i in range(NCH):
                        copy_out("ab", i)

            act.wait_ge(mask_in, 16)
            act.wait_ge(gate_spill[0], 16 * len(range(0, 2 * NCH, 6)))
            act.wait_ge(gate_spill[1], 16 * len(range(1, 2 * NCH, 6)))
            for d in range(2):
                for hd in range(H):
                    act.activation(dm[:, d, hd, :], dmask[:, 0, d, :], ACT.Exp, scale=lg[:, d, hd:hd + 1]).then_inc(dm_exp, 1)
            for st in range(NCC + NCH):
                fw = st
                bw = NCC - 1 - st if st < NCC else NCC + NCH - 1 - (st - NCC)
                act.wait_ge(u_mm, st + 1)
                act.activation(ust[0:DK, fw, :], ps[0:DK, st % 2, :], ACT.Copy)
                act.activation(ust[DK:P, bw, :], ps[DK:P, st % 2, :], ACT.Copy).then_inc(u_ev, 1)

            def turned(i):
                act.wait_ge(t_mm, i + 1)
                act.activation(qT[0:DK, :, :], ps[0:DK, 0, :].rearrange("p (h c) -> p h c", h=H), ACT.Copy)
                act.activation(kT[0:DK, :, :], ps[0:DK, 1, :].rearrange("p (h c) -> p h c", h=H), ACT.Copy).then_inc(t_act, 1)

            def y_hi(i):
                act.wait_ge(y_mm, i + 1)
                act.activation(ret_hi[:, :, i * CH:(i + 1) * CH], ps[:, 6, :].rearrange("p (h c) -> p h c", h=H), ACT.Copy)\
                    .then_inc(yhi_done, 1)

            turned(0)
            for i in range(NCH):
                if i < NCH - 1:
                    turned(i + 1)
                act.wait_ge(var_done, i + 1)
                act.activation(rs[:, :], rs[:, :], ACT.Sqrt).then_inc(root_done, 1)
                if i:
                    y_hi(i - 1)
                act.wait_ge(rs_done, i + 1)
                if i:
                    act.wait_ge(y_done, i)
                for d in range(2):
                    for hd in range(H):
                        n = d * H + hd
                        a = act.activation(on[:, d, hd, :], ps[:, 4 + d, hd * DV:(hd + 1) * DV], ACT.Identity,
                                           scale=rs[:, n:n + 1], bias=nmr[:, n:n + 1])
                a.then_inc(on_done, 1)
            y_hi(NCH - 1)

            act.wait_ge(ylo_done, NCH)
            act.wait_ge(rec_done, NCH)
            for u in range(4):
                hi(U_DFT + u, dst=df_hi[:, u, :])
            for u in range(3):
                hi(U_OUT + u)
            for fg in range(FG):
                act.wait_ge(z_done, fg + 1)
                if fg:
                    act.wait_ge(f_mm, 4 * fg)
                act.activation(z_hi[:, :, :, :, :], zf[:, :, :, :, :], ACT.Copy).then_inc(zhi_done, 1)
                for s in range(4):
                    n = 4 * fg + s
                    act.wait_ge(f_mm, n + 1)
                    act.activation(four_hi[:, fg, s:SEQ:4], ps[:, n % 8, 0:NQ], ACT.Copy).then_inc(fhi_done, 1)
            for m in range(KT):
                act.wait_ge(out_mm, 2 * m + 2)
                hi(U_OUT + m + 3)
            norm(NORM[2], lambda e, c: e.wait_ge(out_acc, 2 * KT))
            ffn(FFN[1])
            norm(NORM[3], lambda e, c: e.wait_ge(FFN[1].acc_done, 2 * 2 + KT * 2 * GROUPS))

        @block.gpsimd
        def _(pool):
            pool.memset(ones[:, :], 1.0).then_inc(ones_set, 1)

            def lo(u, i=None, dst=None, src=None):
                s = u % SLOTS
                pool.wait_ge(hi_done, u + 1 if i is None else UP_UNITS * i + (u + 1))
                r = ring(u)
                a, b = (w_hi[:, r % SLOTS, :], w_lo[:, r % SLOTS, :]) if dst is None else (src, dst)
                pool.tensor_tensor(b, stage[:, s, :], a.bitcast(F32), ALU.subtract).then_inc(lo_done, 1)

            def norm(n):
                for c, chunk in enumerate(n.chunks):
                    start, size = chunk[:2]
                    for m in range(1, KT):
                        pool.wait_ge(n.sq, c * KT + m + 1)
                        if m == 1:
                            if c:
                                pool.wait_ge(n.stat, c)
                            a = scr[:, 0, 0:size]
                        else:
                            pool.wait_ge(n.add, c * (KT - 1) + m - 1)
                            a = scr[:, 2, 0:size]
                        pool.tensor_tensor(scr[:, 2, 0:size], a, scr[:, m % 2, 0:size], ALU.add).then_inc(n.add, 1)
                    if n.shift is None:
                        continue
                    for m in range(KT):
                        q = c * KT + m
                        pool.wait_ge(n.hi, q + 1)
                        pool.tensor_tensor(x_lo[:, m, start:start + size], scr[:, 4 + q % 3, 0:size],
                                           x_hi[:, m, start:start + size].bitcast(F32), ALU.subtract).then_inc(n.lo, 1)

            def ffn(f):
                end = f.u0 + UP_UNITS * GROUPS == U_END
                with pool.Fori(0, GROUPS - end) as i:
                    for u in range(UP_UNITS):
                        lo(f.u0 + u + SLOTS, i)
                if end:
                    for u in range(UP_UNITS - SLOTS):
                        lo(f.u0 + u + SLOTS, GROUPS - 1)

            norm(NORM[0])
            for u in range(SLOTS):
                lo(u)
            ffn(FFN[0])
            norm(NORM[1])
            for u in range(U_MIX + SLOTS, U_DFT):
                lo(u)
            for u in range(4):
                lo(U_DFT + u, dst=df_lo[:, u, :], src=df_hi[:, u, :])
            for u in range(3):
                lo(U_OUT + u)
            for fg in range(FG):
                pool.wait_ge(zhi_done, fg + 1)
                pool.tensor_tensor(z_lo[:, :, :, :, :].rearrange("p a b c d -> p (a b c d)"),
                                   zf[:, :, :, :, :].rearrange("p a b c d -> p (a b c d)"),
                                   z_hi[:, :, :, :, :].bitcast(F32).rearrange("p a b c d -> p (a b c d)"), ALU.subtract).then_inc(zlo_done, 1)
            for m in range(KT):
                lo(U_OUT + m + 3)
            norm(NORM[2])
            ffn(FFN[1])
            norm(NORM[3])

        @block.vector
        def _(dve):
            steps = [0]

            def step(ins):
                steps[0] += 1
                ins.then_inc(dve_step, 1)
                dve.wait_ge(dve_step, steps[0])

            def mods_add_bias(i, bank):
                return dve.tensor_tensor(mods[:, bass.ds(i, 1), :, :].rearrange("p o k w -> p (o k) w"),
                                         ps[:, bank, 0:2 * KT].rearrange("p (k w) -> p k w", w=2),
                                         b_mod[:, bass.ds(i * KT, KT)].unsqueeze(2).to_broadcast([P, KT, 2]), ALU.add)

            def norm(n):
                j = NORM.index(n)
                if n.shift is not None:
                    step(dve.tensor_scalar(atmp[:, :, :], mods[:, n.scale, :, :], 1.0, None, ALU.add))
                    dve.tensor_tensor(acol[:, j, :, :], atmp[:, :, :], gains[:, n.gain, :].unsqueeze(2).to_broadcast([P, KT, 2]), ALU.mult)\
                        .then_inc(acol_ready, 1)
                for c, chunk in enumerate(n.chunks):
                    start, size = chunk[:2]
                    dve.wait_ge(n.stat, c + 1)
                    if n.shift is None and c:
                        dve.wait_ge(fin_done, c * KT)
                    r = scr[:, 3, 0:size]
                    dve.tensor_scalar(r, ps[:, 7, 0:size], 1.0 / D, EPS, ALU.mult, ALU.add).then_inc(n.var, 1)
                    dve.wait_ge(n.root, c + 1)
                    dve.reciprocal(r, r).then_inc(n.rec, 1)
                    dve.wait_ge(n.rec, c + 1)
                    if n.shift is None:
                        for m in range(KT):
                            dve.scalar_tensor_tensor(h_of(m, chunk), h_of(m, chunk), gains[:, n.gain, m:m + 1], r, ALU.mult, ALU.mult)\
                                .then_inc(fin_done, 1)
                        continue

                    def scaled(m):
                        q = c * KT + m
                        if q >= 3:
                            dve.wait_ge(n.lo, q - 2)
                        dve.tensor_tensor(scr[:, 4 + q % 3, 0:size], h_of(m, chunk), r, ALU.mult).then_inc(n.t, 1)

                    scaled(0)
                    for m in range(KT):
                        q = c * KT + m
                        if m < KT - 1:
                            scaled(m + 1)
                        dve.wait_ge(n.xf, q + 1)
                        dve.tensor_copy(x_hi[:, m, start:start + size], scr[:, 4 + q % 3, 0:size]).then_inc(n.hi, 1)

            def ffn(f):
                C = f.C

                def body(i, mod):
                    for j in range(2):
                        def product(c):
                            start, size, _ = f.chunks[c]
                            dve.wait_ge(f.up_done, 4 * C * i + ((2 * j + 1) * C + c + 1))
                            dve.wait_ge(f.silu_done, 2 * C * i + (j * C + c + 1))
                            dve.wait_ge(f.glo_done, 2 * C * i + (j * C + c + 1))
                            dve.tensor_tensor(scr[:, 3 + c, 0:size], scr[:, c, 0:size], ps[:, C + c, 0:size], ALU.mult)\
                                .then_inc(f.mult_done, 1)

                        def rest(c):
                            start, size, _ = f.chunks[c]
                            dve.wait_ge(f.ghi_done, 2 * C * i + (j * C + c + 1))
                            g = slice(start, start + size)
                            dve.tensor_tensor(g_lo[:, j, g], scr[:, 3 + c, 0:size], g_hi[:, j, g].bitcast(F32), ALU.subtract)\
                                .then_inc(f.glo_done, 1)

                        product(0)
                        for c in range(1, C):
                            product(c)
                            rest(c - 1)
                        rest(C - 1)
                    if mod:
                        dve.wait_ge(mod_used, KT * i + (2 + KT))
                        mods_add_bias(i + 2, 6).then_inc(mod_ready, 1)
                        dve.wait_ge(mod_ready, i + 3)
                        dve.tensor_scalar(ghalf[:, 0, :, :], mods[:, 2, :, :], 0.5, None, ALU.mult).then_inc(gate_ready, 1)
                        dve.wait_ge(gate_ready, i + 1)
                    s = 0
                    for c, chunk in enumerate(f.chunks):
                        for m in range(KT):
                            dve.wait_ge(f.down_done, KT * C * i + (s + 1))
                            hh = h_of(m, chunk)
                            dve.scalar_tensor_tensor(hh, ps[:, s % (2 * C), 0:chunk[1]], ghalf[:, f.gate, m, chunk[2]:chunk[2] + 1], hh,
                                                     ALU.mult, ALU.add).then_inc(f.acc_done, 1)
                            s += 1

                cut = NMOD - 2 if f.with_mods else 0
                if cut:
                    with dve.Fori(0, cut) as i:
                        body(i, True)
                with dve.Fori(cut, GROUPS) as i:
                    body(i, False)

            dve.memset(rtmp[:, 0, 0, 0:1], 0.0).then_inc(lo_done, LO_BIAS)
            dve.memset(rtmp[:, 0, 0, 1:2], 0.0).then_inc(mod_used, 2)
            dve.memset(rtmp[:, 0, 0, 2:3], 0.0).then_inc(FFN[0].acc_done, 2 * 3)
            dve.memset(rtmp[:, 0, 0, 3:4], 0.0).then_inc(FFN[1].acc_done, 2 * 2)
            dve.memset(rtmp[:, 0, 0, 4:5], 0.0).then_inc(FFN[0].glo_done, 3)
            dve.memset(rtmp[:, 0, 0, 5:6], 0.0).then_inc(FFN[1].glo_done, 2)

            dve.wait_ge(small_in, 16 * 8)
            for kind in range(2):
                for d in range(2):
                    zz = dve.tensor_scalar(zx[:, kind, d, :], lg[:, d, :], pvec[:, kind, d:d + 1], None, ALU.mult)
            step(zz)
            for i in range(2):
                dve.wait_ge(mod_mm, i + 1)
                mods_add_bias(i, 5 + i).then_inc(mod_ready, 1)
            dve.wait_ge(mod_ready, 2)
            norm(NORM[0])
            ffn(FFN[0])
            norm(NORM[1])

            def copy_out(kind, i):
                mm, who, _, _ = order[kind, i]
                if who != "d":
                    return
                dve.wait_ge(mix_mm, mm)
                if kind == "fu":
                    dve.tensor_copy(ut[:, i // 2, (i % 2) * HALF:(i % 2 + 1) * HALF], ps[:, i, :]).then_inc(mix_dve, 1)
                elif kind == "vc":
                    dve.tensor_copy(v[:, NCH + i, :], ps[:, 2 + i, :]).then_inc(mix_dve, 1)
                elif kind == "qk":
                    if i == 0:
                        for n in range(4):
                            dve.wait_ge(ab_spill[n], 32)
                    dve.tensor_copy(qk[:, i, 0:H * DK], ps[:, i, 0:H * DK])
                    dve.tensor_scalar(qk[:, i, H * DK:HALF], ps[:, i, H * DK:HALF], DK ** -0.5, None, ALU.mult).then_inc(mix_dve, 1)
                elif kind == "v":
                    dve.tensor_copy(v[:, i, :], ps[:, i, :]).then_inc(mix_dve, 1)

            def rotate(i):
                _, who, count, _ = order["qk", i]
                wait_copied(dve, who, count)
                heads = qk[:, i, :].rearrange("p (n s c) -> p n s c", n=2 * H, s=2)
                cos = rope[:, i, 0, :].unsqueeze(1).to_broadcast([P, 2 * H, DK // 2])
                sin = rope[:, i, 1, :].unsqueeze(1).to_broadcast([P, 2 * H, DK // 2])
                dve.tensor_tensor(rtmp[:, 0, :, :], heads[:, :, 1, :], sin, ALU.mult)
                step(dve.tensor_tensor(rtmp[:, 1, :, :], heads[:, :, 0, :], sin, ALU.mult))
                dve.tensor_tensor(heads[:, :, 0, :], heads[:, :, 0, :], cos, ALU.mult)
                step(dve.tensor_tensor(heads[:, :, 1, :], heads[:, :, 1, :], cos, ALU.mult))
                dve.tensor_tensor(heads[:, :, 0, :], heads[:, :, 0, :], rtmp[:, 0, :, :], ALU.subtract)
                dve.tensor_tensor(heads[:, :, 1, :], heads[:, :, 1, :], rtmp[:, 1, :, :], ALU.add).then_inc(rope_done, 1)
                dve.wait_ge(rope_done, i + 1)

            for g, (name, _) in enumerate(MIX_GROUPS):
                if name in ("gf", "gb"):
                    continue
                for i in range(NCC if name in ("kc", "vc") else 8):
                    copy_out(name, i)
                if name == "qk":
                    for i in range(NCH):
                        rotate(i)

            dve.wait_ge(mask_in, 16)
            for d in range(2):
                dve.wait_ge(dm_exp, H * (d + 1))
                dve.tensor_tensor(dm[:, d, :, :], dm[:, d, :, :], dmask[:, 1, d, :].unsqueeze(1).to_broadcast([P, H, CH]), ALU.mult)\
                    .then_inc(dm_done, 1)
            dve.wait_ge(act_prep, 3)
            dve.wait_ge(mix_act, MIX_A)
            for st in range(NCC + NCH):
                k = (kc[:, st, :] if st < NCC else qk[:, st - NCC, H * DK:HALF]).rearrange("p (h c) -> p h c", h=H)
                if st >= 2:
                    dve.wait_ge(u_mm, st - 1)
                for d in range(2):
                    kk = dve.tensor_tensor(kz[:, st % 2, :, d * DK:(d + 1) * DK], k,
                                           zx[:, 0, d, :].unsqueeze(2).to_broadcast([P, H, DK]), ALU.mult)
                kk.then_inc(kz_done, 1)
            dve.wait_ge(u_ev, NCC + NCH)
            for j in range(NCH):
                if j:
                    dve.wait_ge(rec_done, j)
                for hd in range(H):
                    e = slice(hd * DV, (hd + 1) * DV)
                    a = dve.scalar_tensor_tensor(ust[:, j + 1, e], ust[:, j, e], dcs[:, hd:hd + 1], ust[:, j + 1, e], ALU.mult, ALU.add)
                a.then_inc(rec_done, 1)

            def decayed_q(i):
                qq = qk[:, i, 0:H * DK].rearrange("p (h c) -> p h c", h=H)
                if i:
                    dve.wait_ge(t_mm, i)
                for d in range(2):
                    a = dve.tensor_tensor(qx[:, :, d * DK:(d + 1) * DK], qq, zx[:, 1, d, :].unsqueeze(2).to_broadcast([P, H, DK]), ALU.mult)
                a.then_inc(qx_done, 1)

            def turned(i):
                dve.wait_ge(t_mm, i + 1)
                dve.tensor_copy(qxT[:, i % 2, :, :], ps[:, 2, :].rearrange("p (h c) -> p h c", h=H)).then_inc(t_dve, 1)

            def y_lo(i):
                dve.wait_ge(yhi_done, i + 1)
                cc = slice(i * CH, (i + 1) * CH)
                dve.tensor_tensor(ret_lo[:, :, cc], ps[:, 6, :].rearrange("p (h c) -> p h c", h=H), ret_hi[:, :, cc].bitcast(F32), ALU.subtract)\
                    .then_inc(ylo_done, 1)

            dve.wait_ge(dm_done, 2)
            decayed_q(0)
            turned(0)
            for i in range(NCH):
                dve.wait_ge(s_mm, i + 1)
                if i:
                    dve.wait_ge(o_mm, i)
                for d in range(2):
                    a = dve.tensor_tensor(pr[:, d, :, :], ps[:, 3, :].rearrange("p (h c) -> p h c", h=H), dm[:, d, :, :], ALU.mult)
                a.then_inc(p_done, 1)
                if i < NCH - 1:
                    decayed_q(i + 1)
                    turned(i + 1)
                dve.wait_ge(o_mm, i + 1)
                if i:
                    dve.wait_ge(on_done, i)
                for n in range(2 * H):
                    a = dve.bn_stats(stats[:, n, :], ps[:, 4 + n // H, (n % H) * DV:(n % H + 1) * DV])
                step(a)
                for n in range(2 * H):
                    a = dve.bn_aggr(mv[:, n, :], stats[:, n, :])
                step(a)
                dve.tensor_scalar(rs[:, :], mv[:, :, 1], EPS, None, ALU.add).then_inc(var_done, 1)
                dve.wait_ge(root_done, i + 1)
                step(dve.reciprocal(rs[:, :], rs[:, :]))
                dve.scalar_tensor_tensor(nmr[:, :], mv[:, :, 0], -1.0, rs[:, :], ALU.mult, ALU.mult).then_inc(rs_done, 1)
                if i:
                    y_lo(i - 1)
                dve.wait_ge(on_done, i + 1)
                dve.wait_ge(gate_in[i % 2], 16 * (i // 2 + 1))
                o2 = on[:, :, :, :].rearrange("p d h c -> p d (h c)")
                step(dve.tensor_tensor(o2, o2, gin[:, i % 2, :, :], ALU.mult))
                if i:
                    dve.wait_ge(y_mm, i)
                dve.tensor_tensor(y[:, :, :], on[:, 0, :, :], on[:, 1, :, :], ALU.add).then_inc(y_done, 1)
            y_lo(NCH - 1)

            def butterflies(fg):
                dve.wait_ge(ab_in, 16 * (fg + 1))
                x02, x13 = abuf[:, 0:2, :, :, :].rearrange("p j t a c -> p (j t a c)"), abuf[:, 2:4, :, :, :].rearrange("p j t a c -> p (j t a c)")
                step(dve.tensor_tensor(ebuf[:, :, :, :, :].rearrange("p j t a c -> p (j t a c)"), x02, x13, ALU.add))
                step(dve.tensor_tensor(x13, x02, x13, ALU.subtract))
                if fg:
                    dve.wait_ge(zlo_done, fg)
                e0, e1, d0, d1 = ebuf[:, 0, :, :, :], ebuf[:, 1, :, :, :], abuf[:, 2, :, :, :], abuf[:, 3, :, :, :]
                flat = lambda a: a.rearrange("p t a c -> p (t a c)")
                dve.tensor_tensor(flat(zf[:, 0, :, :, :]), flat(e0), flat(e1), ALU.add)
                dve.tensor_tensor(flat(zf[:, 2, :, :, :]), flat(e0), flat(e1), ALU.subtract)
                dve.tensor_tensor(zf[:, 1, :, 0, :], d0[:, :, 0, :], d1[:, :, 1, :], ALU.subtract)
                dve.tensor_tensor(zf[:, 1, :, 1, :], d0[:, :, 1, :], d1[:, :, 0, :], ALU.add)
                dve.tensor_tensor(zf[:, 3, :, 0, :], d0[:, :, 0, :], d1[:, :, 1, :], ALU.add)
                dve.tensor_tensor(zf[:, 3, :, 1, :], d0[:, :, 1, :], d1[:, :, 0, :], ALU.subtract).then_inc(z_done, 1)

            butterflies(0)
            for fg in range(FG):
                if fg < FG - 1:
                    butterflies(fg + 1)
                for s in range(4):
                    n = 4 * fg + s
                    dve.wait_ge(fhi_done, n + 1)
                    dve.tensor_tensor(four_lo[:, fg, s:SEQ:4], ps[:, n % 8, 0:NQ], four_hi[:, fg, s:SEQ:4].bitcast(F32), ALU.subtract)\
                        .then_inc(flo_done, 1)

            step(dve.tensor_scalar(ghalf[:, 1, :, :], mods[:, 8, :, :], 0.5, None, ALU.mult))
            for m in range(KT):
                for c in range(2):
                    n = 2 * m + c
                    dve.wait_ge(out_mm, n + 1)
                    hh = h_lat[:, m, c * HALF:(c + 1) * HALF]
                    dve.scalar_tensor_tensor(hh, ps[:, n % 4, :], mods[:, 5, m, 0:1], hh, ALU.mult, ALU.add).then_inc(out_acc, 1)
            norm(NORM[2])
            ffn(FFN[1])
            norm(NORM[3])


def constants():
    f = np.float32
    pos = np.arange(CH, dtype=np.float64)
    n_freq = DK // 4
    inv = (f(10000.0) ** (-np.arange(n_freq, dtype=f) / f(n_freq))).astype(f)
    tok = np.arange(SEQ)
    ang = np.concatenate([(tok // 64).astype(f)[:, None] * inv, (tok % 64).astype(f)[:, None] * inv], axis=-1).astype(np.float64)
    rope = np.stack([np.cos(ang), np.sin(ang)], 1).astype(f)
    diff = pos[None, :] - pos[:, None]
    dmask = np.stack([np.stack([np.maximum(diff, 0), np.maximum(-diff, 0)]),
                      np.stack([diff >= 0, diff <= 0])]).astype(f)
    pvec = np.stack([np.stack([CH - 1 - pos, pos]), np.stack([pos + 1, CH - pos])]).astype(f)
    a = 2 * np.pi * np.outer(np.arange(FC), np.arange(FC)) / FC
    chan = np.concatenate([np.cos(a), np.sin(a)], 1) / np.sqrt(SEQ * FC)
    n = np.arange(NQ)[:, None, None]
    k = 4 * np.arange(NQ)[None, None, :] + np.arange(4)[None, :, None]
    a = 2 * np.pi * (n * k % SEQ) / SEQ
    dft = np.stack([np.cos(a), -np.sin(a)], 0).reshape(2, 2, P, 4 * NQ).transpose(1, 0, 2, 3).reshape(4, P, 4 * NQ)
    return {
        "ident": np.eye(P, dtype=f),
        "chan": chan.astype(f),
        "pvec": np.ascontiguousarray(pvec.transpose(2, 0, 1)),
        "rope": np.ascontiguousarray(rope.reshape(NCH, P, 2, DK // 2).transpose(1, 0, 2, 3)),
        "dmask": np.ascontiguousarray(dmask.transpose(2, 0, 1, 3)),
        "dft": np.ascontiguousarray(dft.astype(f)),
    }


def kernel(x, c, ctx, c_ctx, w_mod, b_mod, norm_ffn1, w13_ffn1, w2_ffn1, norm_mix, w_in, ret_log_decay, w_out,
           norm_ffn2, w13_ffn2, w2_ffn2, norm_final):
    import concourse.bacc as bacc
    from concourse.bass_utils import run_bass_kernel_spmd

    A = lambda a: np.asarray(a)
    tiles = lambda a: A(a).reshape(KT, P, -1)
    columns = lambda a: A(a).reshape(-1, P).T

    def w13(a):
        return A(a)[0].reshape(KT, P, 2, FT, P).transpose(3, 2, 1, 0, 4).reshape(2 * FT, P, UNIT)

    arrays = {
        "x": tiles(A(x)[0].T), "ctx": tiles(A(ctx)[0].T),
        "cond": np.stack([columns(A(c)[0]), columns(c_ctx)], 2),
        "w_mod": A(w_mod)[0].reshape(KT, P, NMOD * KT, P).transpose(2, 1, 0, 3).reshape(NMOD * KT, P, UNIT),
        "b_mod": columns(A(b_mod)[0]),
        "gains": np.stack([columns(A(g).reshape(-1)) for g in (norm_ffn1, norm_mix, norm_ffn2, norm_final)], 1),
        "w13_1": w13(w13_ffn1), "w2_1": A(w2_ffn1)[0].reshape(FT, P, D),
        "w13_2": w13(w13_ffn2), "w2_2": A(w2_ffn2)[0].reshape(FT, P, D),
        "w_in": A(w_in)[0].reshape(4, 2, P, 5, HALF).transpose(3, 0, 2, 1, 4).reshape(5, 4, P, UNIT),
        "lg": A(ret_log_decay)[0],
        "w_out": A(w_out)[0].reshape(KT, P, KT, P).transpose(2, 1, 0, 3).reshape(KT, P, UNIT),
        **constants(),
    }
    arrays = {"in_" + k: np.ascontiguousarray(a) for k, a in arrays.items()}
    nc = bacc.Bacc("TRN2", target_bir_lowering=False, num_devices=1)
    t = {k[3:]: nc.dram_tensor(k, a.shape, F32, kind="ExternalInput").ap() for k, a in arrays.items()}
    t["lg"] = t["lg"].partition_broadcast(P)
    t["out"] = nc.dram_tensor("out", (KT, P, SEQ), F32, kind="ExternalOutput").ap()
    build(nc, t)
    got = run_bass_kernel_spmd(nc, [arrays], core_ids=[0]).results[0]["out"]
    return np.ascontiguousarray(got.reshape(D, SEQ).T)[None]
```

```python
from contextlib import ExitStack

import numpy as np

import concourse.bass as bass
from concourse import mybir
from concourse.alu_op_type import AluOpType as ALU

F32 = mybir.dt.float32
F32R = mybir.dt.float32r
ACT = mybir.ActivationFunctionType

P = 128
D = 1024
KT = D // P
SEQ, CTX = 1024, 256
TOK = SEQ + CTX
FF = 2816
FT = FF // P
GROUPS = FT // 2
NMOD = 9
H, DK, DV = 4, 64, 128
FG, FC = 4, 128
CH = 128
NCH, NCC = SEQ // CH, CTX // CH
EPS = 1e-6
SLOTS = 3
UNIT = 1024
HALF = 512
NQ = SEQ // 4

UP_UNITS = 6
U_FFN1 = 0
U_MIX = U_FFN1 + UP_UNITS * GROUPS
MIX_GROUPS = (("fu", 4), ("kc", 0), ("vc", 1), ("qk", 0), ("v", 1), ("gf", 2), ("gb", 3))
U_DFT = U_MIX + 4 * len(MIX_GROUPS)
U_OUT = U_DFT + 4
U_FFN2 = U_OUT + KT
U_END = U_FFN2 + UP_UNITS * GROUPS
STATES = tuple(range(NCC)) + tuple(NCC + c for j in range(NCH // 2) for c in (j, NCH - 1 - j))
WORDS = 53208
BRANCHES = (0, 2, 1, 3)
FOUR_BANKS = (0, 1, 2, 4)
LO_BIAS = SLOTS


def ring(u):
    return u if u < U_DFT else u - 4


class Ffn:

    def __init__(self, tag, u0, chunks, gate, with_mods):
        self.tag, self.u0, self.chunks, self.gate, self.with_mods = tag, u0, chunks, gate, with_mods
        self.C = len(chunks)
        self.spans = ((0, 3, 2), (3, NMOD - 2, 1), (NMOD - 2, GROUPS - 1, 0)) if with_mods else ((0, GROUPS - 1, 0),)


class Norm:

    def __init__(self, tag, chunks, shift, scale, gain):
        self.tag, self.chunks, self.shift, self.scale, self.gain = tag, chunks, shift, scale, gain
        C = len(chunks)
        tiles = [(c, m) for m in range(KT) for c in range(C)] if tag == "b" else [(c, m) for c in range(C) for m in range(KT)]
        self.at = {x: n for n, x in enumerate(tiles)}
        adds = [x for x in tiles if x[1]]
        self.add_at = {x: n for n, x in enumerate(adds)}
        self.added = {c: self.add_at[c, KT - 1] + 1 for c in range(C)}


def last_pass(C):
    if C == 3:
        plan = [("d", 0, m) for m in range(KT)] + [("d", 1, m) for m in range(4)] + [("s", 0, 0)]
        for m in range(4):
            plan += [("d", 1, 4 + m), ("n", 0, m)]
        for m in range(4):
            plan += [("d", 2, m), ("n", 0, 4 + m)]
        plan += [("d", 2, 4 + m) for m in range(4)]
    else:
        plan = [("d", 0, m) for m in range(KT)] + [("d", 1, m) for m in range(4)] + [("s", 0, 0)]
        for m in range(4):
            plan += [("d", 1, 4 + m), ("n", 0, m)]
        plan += [("n", 0, 4 + m) for m in range(4)]
    return plan + norms_from(1, C)


def norms_from(c0, C):
    return [x for c in range(c0, C) for x in [("s", c, 0)] + [("n", c, m) for m in range(KT)]]


LAT = ((0, 512, 0), (512, 512, 0))
ALL = LAT + ((1024, 256, 1),)


def slab_offset(nc, slab):
    return nc.lookup_mloc(slab.name).addr


def build(nc, t):
    ctx = ExitStack()
    with ctx:
        sem = lambda name: ctx.enter_context(nc.semaphore(name))

        slab = ctx.enter_context(nc.sbuf_tensor("slab", [P, WORDS], F32))
        base = slab_offset(nc, slab)

        def place(name, words, offset, dtype=F32, shape=None):
            return nc.alloc_sbuf_tensor_at(name, [P, words] if shape is None else [P, *shape], dtype,
                                           offset=base + 4 * offset)

        o = 0
        h_lat = place("h_lat", 0, o, shape=[KT, SEQ]); o += KT * SEQ
        O_HCTX = o
        h_ctx = place("h_ctx", 0, o, shape=[KT, CTX]); o += KT * CTX
        O_X = o
        x_hi = place("x_hi", 0, o, F32R, [KT, TOK]); o += KT * TOK
        x_lo = place("x_lo", 0, o, F32R, [KT, TOK]); o += KT * TOK
        O_W = o
        w_hi = place("w_hi", 0, o, F32R, [SLOTS, UNIT]); o += SLOTS * UNIT
        w_lo = place("w_lo", 0, o, F32R, [SLOTS, UNIT]); o += SLOTS * UNIT
        stage = place("stage", 0, o, shape=[SLOTS, UNIT]); o += SLOTS * UNIT
        O_R = o
        g_hi = place("g_hi", 0, o, F32R, [2, TOK]); o += 2 * TOK
        g_lo = place("g_lo", 0, o, F32R, [2, TOK]); o += 2 * TOK
        O_SCR = o
        silu_a = [place(f"silu_a{c}", 0, o + at, shape=[HALF // (1 + (c == 2))]) for c, at in enumerate((0, 512, 2048))]
        prod = [place(f"prod{c}", 0, o + at, shape=[HALF // (1 + (c == 2))]) for c, at in enumerate((1024, 1536, 2304))]
        mod_acc_ctx = place("mod_acc_ctx", 0, o + 2560, shape=[D]); o += 3584
        O_MS = o
        mod_stage = place("mod_stage", 0, o, shape=[2, UNIT]); o += 2 * UNIT
        def small(name, *shape):
            nonlocal o
            words = int(np.prod(shape))
            x = place(name, 0, o, shape=list(shape)); o += words + (-words) % 8
            return x
        mods = small("mods", NMOD, KT, 2)
        gains = small("gains", 4, KT)
        cond = small("cond", KT, 2)
        acol = small("acol", 3, KT, 2)
        atmp = small("atmp", KT, 2)
        ghalf = small("ghalf", 2, KT, 2)
        lg = small("lg", 2, H)
        pvec = small("pvec", 2)
        zeta = small("zeta", 2, H)
        dcs = small("dcs", H)
        stats = small("stats", 2 * H, 6)
        mv = small("mv", 2 * H, 2)
        rs = small("rs", 2 * H)
        nmr = small("nmr", 2 * H)
        ones = small("ones", P)
        ident = small("ident", P)
        O_ROPE = o
        rope = small("rope", NCH, 2, DK // 2)
        rtmp = small("rtmp", 2, 2 * H, DK // 2)
        O_LAST = o
        chan = small("chan", 2 * FC)
        b_mod = small("b_mod", NMOD * KT)
        assert max(o, O_LAST + 512) <= WORDS, o
        mod_acc_lat = place("mod_acc_lat", 0, O_ROPE, shape=[D])

        mod_pre = place("mod_pre", 0, O_X, shape=[2 * KT, UNIT])
        qk = place("qk", 0, O_R, shape=[NCH, HALF])
        ab_out = place("ab_out", 0, O_R, shape=[4, UNIT])
        kc = place("kc", 0, O_R + 4096, shape=[NCC, H * DK])
        v = place("v", 0, O_R + 4608, shape=[NCH + NCC, HALF])
        ut = place("ut", 0, O_R + 4608, shape=[FG, SEQ])
        gbuf_a = place("gbuf_a", 0, O_R + 9728, shape=[2, HALF])
        gbuf_b = place("gbuf_b", 0, O_HCTX, shape=[4, HALF])
        q = O_X
        ret_hi = place("ret_hi", 0, q, F32R, [H, SEQ]); q += H * SEQ
        ret_lo = place("ret_lo", 0, q, F32R, [H, SEQ]); q += H * SEQ
        O_TMP = q
        ust = place("ust", 0, q, shape=[NCH + NCC, H * DV]); q += (NCH + NCC) * H * DV
        qq = place("qq", 0, q, shape=[H, 2, DK]); q += 512
        qxT = place("qxT", 0, q, shape=[2, H, CH]); q += 1024
        xiT = place("xiT", 0, q, shape=[H, CH]); q += 512
        pr = place("pr", 0, q, shape=[2, H, CH])
        masks = place("masks", 0, q, shape=[5, CH]); q += 1024
        on = place("on", 0, q, shape=[2, 2, H, DV])
        kz = place("kz", 0, q, shape=[2, H, P]); q += 2048
        gin = place("gin", 0, q, shape=[2, 2, HALF]); q += 2048
        assert q <= O_X + 2 * KT * TOK
        qT = place("qT", 0, O_HCTX, shape=[H, CH])
        kT = place("kT", 0, O_HCTX + 512, shape=[H, CH])
        y = place("y", 0, O_HCTX + 1024, shape=[2, H, DV])
        dm = place("dm", 0, O_R + 9728, shape=[2, H, CH])
        df_hi = place("df_hi", 0, O_W, F32R, [4, UNIT])
        df_lo01 = place("df_lo01", 0, O_W + 4096, F32R, [2, UNIT])
        df_lo23 = place("df_lo23", 0, O_R, F32R, [2, UNIT])
        df_lo = [(df_lo01 if u < 2 else df_lo23)[:, u % 2, :] for u in range(4)]
        q = O_TMP
        z_hi = place("z_hi", 0, q, F32R, [4, 2, 2, FC]); q += 2048
        z_lo = place("z_lo", 0, q, F32R, [4, 2, 2, FC]); q += 2048
        abuf = [place("abuf0", 0, O_R + 2048, shape=[4, 2, 2, FC]), place("abuf1", 0, q, shape=[4, 2, 2, FC])]; q += 2048
        out_hi = place("out_hi", 0, q, F32R, [SLOTS, UNIT]); q += SLOTS * UNIT
        out_lo = place("out_lo", 0, q, F32R, [SLOTS, UNIT]); q += SLOTS * UNIT
        assert q <= O_X + 2 * KT * TOK
        four_hi = place("four_hi", 0, O_R + 4096, F32R, [FG, SEQ])
        four_lo = [place(f"four_lo{fg}", 0, at, F32R, [SEQ]) for fg, at in enumerate((O_R + 8192, O_R + 9216, O_HCTX, O_HCTX + 1024))]
        ebuf = [[place(f"ebuf{n}{j}", 0, at, shape=[2, 2, FC]) for j, at in enumerate(ats)]
                for n, ats in enumerate(((O_ROPE, O_ROPE + 512), (O_R + 10240, O_LAST)))]

        ps = ctx.enter_context(nc.psum_tensor("ps", [P, 8, HALF], F32))
        ab_dram = nc.dram_tensor("ab_dram", (NCH, P, UNIT), F32).ap()
        gate_dram = nc.dram_tensor("gate_dram", (NCH, P, 2, HALF), F32).ap()

        stage_in = [sem(f"stage_in{i}") for i in range(SLOTS)]
        hi_done, lo_done, mix_unit = sem("hi_done"), sem("lo_done"), sem("mix_unit")
        mod_in = [sem(f"mod_in{i}") for i in range(2)]
        mod_mm, mod_ready = sem("mod_mm"), sem("mod_ready")
        gate_ready = sem("gate_ready")
        mod_chain = sem("mod_chain")
        ctx_in, x_in, small_in, cond_ready, ones_set = (sem(n) for n in ("ctx_in", "x_in", "small_in", "cond_ready", "ones_set"))
        pre_in = [sem(f"pre_in{i}") for i in range(4)]
        rope_in = sem("rope_in")
        dve_step, act_prep = sem("dve_step"), sem("act_prep")

        FFN = [Ffn("1", U_FFN1, ALL, 0, True), Ffn("2", U_FFN2, LAT, 1, False)]
        for f in FFN:
            f.up_done, f.silu_done, f.mult_done, f.ghi_done, f.glo_done, f.down_done, f.acc_done = (
                sem(n + f.tag) for n in ("up_done", "silu_done", "mult_done", "ghi_done", "glo_done", "down_done", "acc_done"))

        O_G = O_R
        SPOTS = {"a": ((O_G, O_G + 512), (O_G + 1024, O_G + 1536, O_G + 2048), (O_G + 2304, O_G + 2816, O_G + 3328)),
                 "m": ((O_SCR + 2560, O_SCR + 3072), (O_MS, O_MS + 512, O_MS + 1024), (O_MS + 1280, O_ROPE, O_ROPE + 512)),
                 "b": ((O_G, O_G + 512), (O_G + 1024, O_G + 1536), (O_G + 2048, O_G + 2560, O_G + 3072)),
                 "f": ((O_HCTX, O_HCTX + 512), (O_MS, O_MS + 512), (O_MS + 1024, O_HCTX + 1024, O_HCTX + 1536))}
        NORM = {}
        for tag, chunks, shift, scale, gain in (("a", ALL, 0, 1, 0), ("m", ALL, 3, 4, 1), ("b", LAT, 6, 7, 2), ("f", LAT, None, None, 3)):
            n = Norm(tag, chunks, shift, scale, gain)
            squares, sums, scaled = SPOTS[tag]
            n.square = [place(f"square{j}_{tag}", 0, at, shape=[HALF]) for j, at in enumerate(squares)]
            n.total = [place(f"total{c}_{tag}", 0, at, shape=[chunks[c][1]]) for c, at in enumerate(sums)]
            n.scaled = [place(f"scaled{j}_{tag}", 0, at, shape=[HALF]) for j, at in enumerate(scaled)]
            n.sq, n.add, n.stat, n.var, n.root, n.rec, n.t, n.hi, n.lo = (
                sem(s + "_" + tag) for s in ("n_sq", "n_add", "n_stat", "n_var", "n_root", "n_rec", "n_t", "n_hi", "n_lo"))
            NORM[tag] = n

        mix_mm, mix_act, mix_dve = sem("mix_mm"), sem("mix_act"), sem("mix_dve")
        ab_spill = [sem(f"ab_spill{i}") for i in range(4)]
        gate_spill = [sem(f"gate_spill{i}") for i in range(6)]
        rope_done = sem("rope_done")
        mask_in, dm_exp, dm_done = sem("mask_in"), sem("dm_exp"), sem("dm_done")
        kz_done, u_mm, u_ev, rec_done = sem("kz_done"), sem("u_mm"), sem("u_ev"), sem("rec_done")
        qq_done, t_mm, t_act, t_dve = sem("qq_done"), sem("t_mm"), sem("t_act"), sem("t_dve")
        s_mm, p_done, o_mm, var_done, root_done, rs_done = (sem(n) for n in ("s_mm", "p_done", "o_mm", "var_done", "root_done", "rs_done"))
        xi_done, gated, q_turned = sem("xi_done"), sem("gated"), sem("q_turned")
        on_done, y_done, y_mm, yhi_done, ylo_done = (sem(n) for n in ("on_done", "y_done", "y_mm", "yhi_done", "ylo_done"))
        gate_in = [sem(f"gate_in{i}") for i in range(2)]
        ab_in = [sem(f"ab_in{i}") for i in range(2)]
        z_done, zhi_done, zlo_done, f_mm, fhi_done, flo_done = (
            sem(n) for n in ("z_done", "zhi_done", "zlo_done", "f_mm", "fhi_done", "flo_done"))
        out_mm, out_acc = sem("out_mm"), sem("out_acc")
        fin_done, stored = sem("fin_done"), sem("stored")

        block = ctx.enter_context(nc.Block())

        def h_of(m, chunk):
            start, n, which = chunk
            return h_ctx[:, m, :] if which else h_lat[:, m, start:start + n]

        outs = []
        for name, _ in MIX_GROUPS:
            if name == "fu":
                outs += [("fu", n, (n,), "ad"[n % 2 == 0]) for n in range(8)]
            elif name == "kc":
                outs += [("kc", n, (n,), "a") for n in range(NCC)]
            elif name == "vc":
                outs += [("vc", n, (2 + n,), "da"[n]) for n in range(NCC)]
                outs += [("ab", n, (4 + 2 * (n % 2), 5 + 2 * (n % 2)), "a") for n in range(NCH)]
            else:
                outs += [(name, n, (n,), "a" if name in ("gf", "gb") else "ad"[n % 2 == 0]) for n in range(NCH)]
        order = {}
        counts = {"a": 0, "d": 0}
        last_in_bank = {}
        for n, (kind, i, banks, who) in enumerate(outs):
            counts[who] += 1
            before = [last_in_bank[b] for b in banks if b in last_in_bank]
            order[kind, i] = (n + 1, who, counts[who], before)
            for b in banks:
                last_in_bank[b] = (who, counts[who])
        MIX_A, MIX_D = counts["a"], counts["d"]

        def halves(u):
            if U_DFT <= u < U_OUT:
                return df_hi[:, u - U_DFT, :], df_lo[u - U_DFT]
            s_ = ring(u) % SLOTS
            if U_OUT <= u < U_FFN2:
                return out_hi[:, s_, :], out_lo[:, s_, :]
            return w_hi[:, s_, :], w_lo[:, s_, :]

        def z_of(n):
            fg, j = divmod(n, 4)
            return abuf[fg % 2][:, j, :, :, :] if j < 2 else ebuf[fg % 2][j - 2][:, :, :, :]

        def wait_copied(e, who, count):
            e.wait_ge(mix_act if who == "a" else mix_dve, count)

        def mm3(pe, out, wh, wl, xh, xl, start, stop):
            pe.matmul(out, wl, xh, start=start, stop=False)
            pe.matmul(out, wh, xl, start=False, stop=False)
            return pe.matmul(out, wh, xh, start=False, stop=stop)

        @block.sync
        def _(sp):
            def unit(u, src, more=0):
                s = u % SLOTS
                sp.wait_ge(lo_done, more + (u - SLOTS + 1 + LO_BIAS))
                sp.dma_start(stage[:, s, :], src).then_inc(stage_in[s], 16)

            sp.dma_start(cond[:, :, :], t["cond"]).then_inc(small_in, 16)
            sp.dma_start(b_mod[:, :], t["b_mod"]).then_inc(small_in, 16)
            sp.dma_start(gains[:, :, :], t["gains"]).then_inc(small_in, 16)
            for dst, name in ((ident[:, :], "ident"), (chan[:, :], "chan"), (pvec[:, :], "pvec")):
                sp.dma_start(dst, t[name]).then_inc(small_in, 16)
            sp.dma_start(lg[:, :, :], t["lg"]).then_inc(small_in, 16)
            for m in range(0, KT, 2):
                sp.dma_start(h_lat[:, m:m + 2, :], t["x"][m:m + 2].rearrange("m p c -> p m c")).then_inc(x_in, 16)
            sp.dma_start(h_ctx[:, :, :], t["ctx"].rearrange("m p c -> p m c")).then_inc(ctx_in, 16)
            for n in range(4):
                sp.dma_start(mod_pre[:, 4 * n:4 * n + 4, :],
                             t["w_mod01"][4 * n:4 * n + 4].rearrange("n p c -> p n c")).then_inc(pre_in[n], 16)

            def mod_row(group, k):
                sp.wait_ge(mod_chain, KT * group + (k + 1))
                sp.dma_start(mod_stage[:, k % 2, :], t["w_mod"][bass.ds(KT * group + k, 1)].rearrange("o p c -> (o p) c"))\
                    .then_inc(mod_in[k % 2], 16)

            def ffn_units(f, w13, w2):
                def body(i, other_rows, first_rows):
                    for u in range(UP_UNITS):
                        src = w13[bass.ds(4 * i + u, 1)] if u < 4 else w2[bass.ds(2 * i + (u - 4), 1)]
                        unit(f.u0 + u, src.rearrange("o p c -> (o p) c"), UP_UNITS * i)
                        if other_rows and u == 1:
                            for k in range(2, KT):
                                mod_row(i - 1, k)
                    if first_rows:
                        for k in range(2):
                            mod_row(i, k)
                if not f.with_mods:
                    with sp.Fori(0, GROUPS) as i:
                        body(i, False, False)
                    return
                body(0, False, True)
                with sp.Fori(1, NMOD - 2) as i:
                    body(i, True, True)
                body(NMOD - 2, True, False)
                with sp.Fori(NMOD - 1, GROUPS) as i:
                    body(i, False, False)

            ffn_units(FFN[0], t["w13_1"], t["w2_1"])
            for g, (name, cols) in enumerate(MIX_GROUPS):
                for u in range(4):
                    unit(U_MIX + 4 * g + u, t["w_in"][cols, u])
                if g == 0:
                    sp.wait_ge(NORM["m"].lo, KT * 3)
                    sp.dma_start(rope[:, :, :, :], t["rope"]).then_inc(rope_in, 16)
            for u in range(3):
                unit(U_DFT + u, t["dft"][u])
            sp.wait_ge(mix_mm, len(outs))
            sp.dma_start(masks[:, :], t["masks"]).then_inc(mask_in, 16)
            for n in range(6):
                sp.wait_ge(gate_spill[n], 16 * len(range(n, 2 * NCH, 6)))
            def group_in(fg):
                if fg == 0:
                    for n in range(4):
                        sp.wait_ge(ab_spill[n], 16 * 2)
                    sp.wait_ge(t_mm, NCH)
                elif fg == 1:
                    sp.wait_ge(o_mm, NCH)
                    sp.wait_ge(t_dve, NCH)
                else:
                    sp.wait_ge(z_done, 4 * (fg - 1))
                    sp.wait_ge(zlo_done, 4 * (fg - 2) + 2)
                sp.dma_start(abuf[fg % 2][:, :, :, :, :].rearrange("p j t a c -> p (j t) (a c)"),
                             ab_dram[:, :, fg * 2 * FC:(fg + 1) * 2 * FC].rearrange("t p c -> p t c")).then_inc(ab_in[fg % 2], 16)

            for i in range(NCH):
                if i == NCH - 1:
                    group_in(0)
                if i >= 2:
                    sp.wait_ge(y_done, i - 1)
                sp.dma_start(gin[:, i % 2, :, :], gate_dram[i]).then_inc(gate_in[i % 2], 16)
                if i == 3:
                    unit(U_DFT + 3, t["dft"][3])
            for n in range(3):
                group_in(n + 1)
                unit(U_OUT + n, t["w_out"][n])
            for u in range(3, KT):
                unit(U_OUT + u, t["w_out"][u])
            ffn_units(FFN[1], t["w13_2"], t["w2_2"])
            for c in range(2):
                for m in range(KT):
                    sp.wait_ge(fin_done, c * KT + m + 1)
                    sp.dma_start(t["out"][m, :, c * HALF:(c + 1) * HALF], h_lat[:, m, c * HALF:(c + 1) * HALF]).then_inc(stored, 16)
            sp.wait_ge(stored, 16 * 2 * KT)

        @block.tensor
        def _(pe):
            def sum_partitions(n, c):
                size = n.chunks[c][1]
                pe.wait_ge(n.add, n.added[c])
                if c >= 2:
                    pe.wait_ge(n.var, c - 1)
                pe.matmul(ps[:, 7 - c % 2, 0:size], ones[:, :], n.total[c][:, :], start=True, stop=True).then_inc(n.stat, 1)

            def mod_tile(w, col):
                for k in range(KT):
                    mm = pe.matmul(col, w[:, k * P:(k + 1) * P], cond[:, k, :], start=(k == 0), stop=(k == KT - 1))
                return mm

            def ffn(f, n, behind):
                C = f.C

                def down(i, c, m):
                    start, size, _ = f.chunks[c]
                    s4, s5 = (ring(f.u0 + u) % SLOTS for u in (4, 5))
                    step = c * KT + m
                    b = step % (2 * C)
                    if m == 0:
                        pe.wait_ge(f.glo_done, 2 * C * i + (2 * C + c + 1))
                    if step < C:
                        pe.wait_ge(f.silu_done, 2 * C * i + (C + step + 1))
                    elif step < 2 * C:
                        pe.wait_ge(f.mult_done, 2 * C * i + (step + 1))
                    else:
                        pe.wait_ge(f.acc_done, KT * C * i + (step + 1))
                    w = slice(m * P, (m + 1) * P)
                    for j, s in enumerate((s4, s5)):
                        mm = mm3(pe, ps[:, b, 0:size], w_hi[:, s, w], w_lo[:, s, w],
                                 g_hi[:, j, start:start + size], g_lo[:, j, start:start + size], j == 0, j == 1)
                    mm.then_inc(f.down_done, 1)

                def body(i, mod, last=False):
                    for u in range(4):
                        s = ring(f.u0 + u) % SLOTS
                        pe.wait_ge(lo_done, UP_UNITS * i + (f.u0 + u + 1 + LO_BIAS))
                        for c, (start, size, _) in enumerate(f.chunks):
                            b = (u % 2) * C + c
                            if u < 2:
                                pe.wait_ge(f.acc_done, KT * C * i + (b + 1))
                            elif u == 2:
                                pe.wait_ge(f.silu_done, 2 * C * i + (c + 1))
                            else:
                                pe.wait_ge(f.mult_done, 2 * C * i + (c + 1))
                            for k in range(KT):
                                if u == 0:
                                    pe.wait_ge(n.lo, KT * c + k + 1)
                                w = slice(k * P, (k + 1) * P)
                                mm = mm3(pe, ps[:, b, 0:size], w_hi[:, s, w], w_lo[:, s, w],
                                         x_hi[:, k, start:start + size], x_lo[:, k, start:start + size], k == 0, k == KT - 1)
                            mm.then_inc(f.up_done, 1)
                    if mod:
                        pe.wait_ge(mod_chain, KT * i + (KT + 2))
                        pe.wait_ge(mod_ready, i + 2)
                        for n_ in range(KT):
                            for which in range(mod):
                                acc = mod_acc_ctx if which else mod_acc_lat
                                mm = pe.matmul(ps[:, 6, 2 * n_ + which:2 * n_ + which + 1], acc[:, n_ * P:(n_ + 1) * P],
                                               ones[:, 0:1], start=True, stop=True)
                        mm.then_inc(mod_mm, 1)
                    pe.wait_ge(lo_done, UP_UNITS * i + (f.u0 + 6 + LO_BIAS))
                    if not last:
                        for c in range(C):
                            for m in range(KT):
                                down(i, c, m)
                        return
                    for what, c, m in last_pass(C):
                        if what == "d":
                            down(i, c, m)
                        elif what == "s":
                            sum_partitions(behind, c)

                for first, end, mod in f.spans:
                    with pe.Fori(first, end) as i:
                        body(i, mod)
                body(GROUPS - 1, 0, last=True)

            pe.wait_ge(cond_ready, 1)
            for n in range(2 * KT):
                if n % 4 == 0:
                    pe.wait_ge(pre_in[n // 4], 16)
                mm = mod_tile(mod_pre[:, n, :], ps[:, 4 + n // KT, 2 * (n % KT):2 * (n % KT) + 2])
                if n % KT == KT - 1:
                    mm.then_inc(mod_mm, 1)
                if n == 3:
                    pe.wait_ge(ones_set, 1)
                if n in (3, 7, 11):
                    sum_partitions(NORM["a"], n // 4)
            ffn(FFN[0], NORM["a"], NORM["m"])

            def banks_free(kind, i):
                for who, count in order[kind, i][3]:
                    wait_copied(pe, who, count)

            pe.wait_ge(FFN[0].acc_done, 2 * 3 + KT * 3 * GROUPS)
            for g, (name, _) in enumerate(MIX_GROUPS):
                for u in range(4):
                    U = U_MIX + 4 * g + u
                    s = ring(U) % SLOTS
                    pe.wait_ge(lo_done, U + 1 + LO_BIAS)
                    for kk in range(2):
                        k = 2 * u + kk
                        n_out = NCC if name in ("kc", "vc") else 8
                        if g == 0:
                            pe.wait_ge(NORM["m"].lo, KT + k + 1)
                            if k == 0:
                                pe.wait_ge(NORM["m"].var, 3)
                        elif g == 1 and k == 0:
                            pe.wait_ge(NORM["m"].lo, KT * 3)
                        for n in range(n_out):
                            if k == 0:
                                banks_free(name, n)
                            w0 = kk * HALF
                            if name == "fu":
                                fg, c = n // 2, n % 2
                                w = slice(w0 + fg * FC, w0 + (fg + 1) * FC)
                                mm = mm3(pe, ps[:, n, :], w_hi[:, s, w], w_lo[:, s, w],
                                         x_hi[:, k, c * HALF:(c + 1) * HALF], x_lo[:, k, c * HALF:(c + 1) * HALF], k == 0, k == KT - 1)
                            else:
                                tok = slice(n * P, (n + 1) * P) if n_out == 8 else slice(SEQ + n * P, SEQ + (n + 1) * P)
                                w = slice(w0 + H * DK, w0 + HALF) if name == "kc" else slice(w0, w0 + HALF)
                                bank = n + (NCC if name == "vc" else 0)
                                mm = mm3(pe, ps[:, bank, 0:w.stop - w.start], x_hi[:, k, tok], x_lo[:, k, tok],
                                         w_hi[:, s, w], w_lo[:, s, w], k == 0, k == KT - 1)
                            if k == KT - 1:
                                mm.then_inc(mix_mm, 1)
                    if u < 3:
                        mm.then_inc(mix_unit, 1)
                if name == "vc":
                    for kind_i in range(8):
                        _, who, count, _ = order["fu", kind_i]
                        wait_copied(pe, who, count)
                    for n in range(NCH):
                        banks_free("ab", n)
                        for fg in range(FG):
                            mm = pe.matmul(ps[:, 4 + 2 * (n % 2) + fg // 2, (fg % 2) * 2 * FC:(fg % 2 + 1) * 2 * FC],
                                           ut[:, fg, n * P:(n + 1) * P], chan[:, :], start=True, stop=True)
                        mm.then_inc(mix_mm, 1)

            pe.wait_ge(mix_act, MIX_A)
            pe.wait_ge(mix_dve, MIX_D)
            for n, st in enumerate(STATES):
                pe.wait_ge(kz_done, n + 1)
                if n >= 2:
                    pe.wait_ge(u_ev, n - 1)
                for hd in range(H):
                    mm = pe.matmul(ps[:, 4 + n % 2, hd * DV:(hd + 1) * DV], kz[:, n % 2, hd, :],
                                   v[:, (NCH + st) if st < NCC else st - NCC, hd * DV:(hd + 1) * DV], start=True, stop=True)
                mm.then_inc(u_mm, 1)

            def turn(i):
                pe.wait_ge(qq_done, i + 1)
                if i:
                    pe.wait_ge(t_act, i)
                for hd in range(H):
                    pe.transpose(ps[:, 0, hd * CH:(hd + 1) * CH], qq[:, hd, :, :].rearrange("p s c -> p (s c)"), ident[:, :])
                for hd in range(H):
                    mm = pe.transpose(ps[0:DK, 1, hd * CH:(hd + 1) * CH], qk[:, i, (H + hd) * DK:(H + hd + 1) * DK], ident[:, :])
                mm.then_inc(t_mm, 1)

            def turn_y(i):
                pe.wait_ge(y_done, i + 1)
                if i:
                    pe.wait_ge(ylo_done, i)
                for hd in range(H):
                    mm = pe.transpose(ps[:, 3, hd * DV:(hd + 1) * DV], y[:, i % 2, hd, :], ident[:, :])
                mm.then_inc(y_mm, 1)

            pe.wait_ge(rope_done, NCH)
            turn(0)
            for i in range(NCH):
                pe.wait_ge(t_act, i + 1)
                if i:
                    pe.wait_ge(p_done, i)
                for hd in range(H):
                    mm = pe.matmul(ps[:, 2, hd * CH:(hd + 1) * CH], kT[0:DK, hd, :], qT[0:DK, hd, :], start=True, stop=True)
                mm.then_inc(s_mm, 1)
                if i < NCH - 1:
                    turn(i + 1)
                pe.wait_ge(p_done, i + 1)
                pe.wait_ge(t_dve, i + 1)
                if i >= 2:
                    pe.wait_ge(on_done, i - 1)
                elif i == 0:
                    pe.wait_ge(rec_done, NCH)
                for d in range(2):
                    rows = slice(d * DK, (d + 1) * DK)
                    prev = 1 + (i if d == 0 else NCH - 1 - i)
                    for hd in range(H):
                        o_ = ps[:, 4 + 2 * (i % 2) + d, hd * DV:(hd + 1) * DV]
                        pe.matmul(o_, pr[:, d, hd, :], v[:, i, hd * DV:(hd + 1) * DV], start=True, stop=False)
                        mm = pe.matmul(o_, qxT[rows, i % 2, hd, :], ust[rows, prev, hd * DV:(hd + 1) * DV], start=False, stop=True)
                mm.then_inc(o_mm, 1)
                if i >= 2:
                    turn_y(i - 2)

            pe.wait_ge(lo_done, U_DFT + 4 + LO_BIAS)
            pe.wait_ge(on_done, NCH - 1)
            for n in range(4 * FG):
                s = BRANCHES[n % 4]
                pe.wait_ge(zlo_done, n + 1)
                if n >= 4:
                    pe.wait_ge(flo_done, n - 3)
                for ta in range(4):
                    w = z_hi[:, n % 4, ta // 2, ta % 2, :], z_lo[:, n % 4, ta // 2, ta % 2, :]
                    cols = slice(s * NQ, (s + 1) * NQ)
                    mm = mm3(pe, ps[:, FOUR_BANKS[n % 4], 0:NQ], *w, df_hi[:, ta, cols], df_lo[ta][:, cols], ta == 0, ta == 3)
                mm.then_inc(f_mm, 1)
                if n in (1, 5):
                    turn_y(NCH - 2 + n // 4)

            pe.wait_ge(flo_done, 4 * FG)
            pe.wait_ge(ylo_done, NCH)
            for m in range(KT):
                U = U_OUT + m
                s = ring(U) % SLOTS
                pe.wait_ge(lo_done, U + 1 + LO_BIAS)
                for c in range(2):
                    n = 2 * m + c
                    if n >= 4:
                        pe.wait_ge(out_acc, n - 3)
                    cols = slice(c * HALF, (c + 1) * HALF)
                    for k in range(KT):
                        xh, xl = (ret_hi[:, k, cols], ret_lo[:, k, cols]) if k < H else (four_hi[:, k - H, cols], four_lo[k - H][:, cols])
                        w = slice(k * P, (k + 1) * P)
                        mm = mm3(pe, ps[:, n % 4, :], out_hi[:, s, w], out_lo[:, s, w], xh, xl, k == 0, k == KT - 1)
                    mm.then_inc(out_mm, 1)
            for c in range(2):
                sum_partitions(NORM["b"], c)
            ffn(FFN[1], NORM["b"], NORM["f"])

        @block.scalar
        def _(act):
            def hi(u, i=None):
                s = u % SLOTS
                landed = 16 * (u // SLOTS + 1)
                act.wait_ge(stage_in[s], landed if i is None else i * (16 * UP_UNITS // SLOTS) + landed)
                act.activation(halves(u)[0], stage[:, s, :], ACT.Copy).then_inc(hi_done, 1)

            def square(n, c, m):
                if m == 0:
                    dst = n.total[c][:, :]
                else:
                    r = n.add_at[c, m]
                    if r >= 2:
                        act.wait_ge(n.add, r - 1)
                    dst = n.square[r % 2][:, 0:n.chunks[c][1]]
                act.activation(dst, h_of(m, n.chunks[c]), ACT.Square).then_inc(n.sq, 1)

            def root(n, c):
                act.wait_ge(n.var, c + 1)
                act.activation(n.total[c][:, :], n.total[c][:, :], ACT.Sqrt).then_inc(n.root, 1)

            def normed_hi(n, c, m):
                if n.shift is None:
                    return
                q = c * KT + m
                start, size, which = n.chunks[c]
                act.wait_ge(n.t, q + 1)
                act.activation(x_hi[:, m, start:start + size], n.scaled[q % 3][:, 0:size], ACT.Identity,
                               bias=mods[:, n.shift, m, which:which + 1]).then_inc(n.hi, 1)

            def ffn(f, behind):
                C = f.C
                end = f.u0 + UP_UNITS * GROUPS == U_END

                def body(i, last):
                    for u in range(4):
                        for c, (start, size, _) in enumerate(f.chunks):
                            if u % 2 == 0:
                                act.wait_ge(f.up_done, 4 * C * i + (u * C + c + 1))
                                if u == 2:
                                    act.wait_ge(f.mult_done, 2 * C * i + (c + 1))
                                act.activation(silu_a[c][:, :], ps[:, c, 0:size], ACT.Silu).then_inc(f.silu_done, 1)
                            else:
                                act.wait_ge(f.mult_done, 2 * C * i + ((u // 2) * C + c + 1))
                                act.activation(g_hi[:, u // 2, start:start + size], prod[c][:, :], ACT.Copy)\
                                    .then_inc(f.ghi_done, 1)
                        if last and end and u + SLOTS >= UP_UNITS:
                            continue
                        act.wait_ge(f.up_done, 4 * C * i + (u + 1) * C)
                        hi(f.u0 + u + SLOTS, i)
                    if last:
                        for what, c, m in last_pass(C):
                            if what == "d":
                                act.wait_ge(f.acc_done, KT * C * i + (2 * C + c * KT + m + 1))
                                square(behind, c, m)
                            elif what == "s":
                                root(behind, c)
                            else:
                                normed_hi(behind, c, m)
                            if (what, c, m) == ("n", 1, KT - 1) and not end:
                                act.wait_ge(f.down_done, KT * C * i + KT * C)
                                hi(f.u0 + 4 + SLOTS, i)
                                hi(f.u0 + 5 + SLOTS, i)
                        return
                    act.wait_ge(f.down_done, KT * C * i + KT * C)
                    hi(f.u0 + 4 + SLOTS, i)
                    hi(f.u0 + 5 + SLOTS, i)

                with act.Fori(0, GROUPS - 1) as i:
                    body(i, False)
                body(GROUPS - 1, True)

            act.wait_ge(small_in, 16 * 7)
            act.activation(cond[:, :, :], cond[:, :, :], ACT.Silu).then_inc(cond_ready, 1)
            act.wait_ge(dve_step, 1)
            act.activation(zeta[:, :, :], zeta[:, :, :], ACT.Exp).then_inc(act_prep, 1)
            for d in range(2):
                rows = slice(d * DK, (d + 1) * DK)
                act.activation(dcs[rows, :], lg[rows, d, :], ACT.Exp, scale=float(CH)).then_inc(act_prep, 1)

            n = NORM["a"]
            act.wait_ge(x_in, 16 * KT // 2)
            for c in range(2):
                for m in range(KT):
                    square(n, c, m)
                root(n, c)
            act.wait_ge(ctx_in, 16)
            for m in range(KT):
                square(n, 2, m)
            root(n, 2)
            for u in range(SLOTS):
                hi(u)
            for c in range(3):
                for m in range(KT):
                    normed_hi(n, c, m)
            ffn(FFN[0], NORM["m"])

            def copy_out(kind, i):
                mm, who, _, _ = order[kind, i]
                if who != "a":
                    return
                act.wait_ge(mix_mm, mm)
                if kind == "fu":
                    act.activation(ut[:, i // 2, (i % 2) * HALF:(i % 2 + 1) * HALF], ps[:, i, :], ACT.Copy).then_inc(mix_act, 1)
                elif kind == "kc":
                    act.activation(kc[:, i, :], ps[:, i, 0:H * DK], ACT.Copy, scale=DK ** -0.5).then_inc(mix_act, 1)
                elif kind == "vc":
                    act.activation(v[:, NCH + i, :], ps[:, 2 + i, :], ACT.Copy).then_inc(mix_act, 1)
                elif kind == "ab":
                    if i >= 4:
                        act.wait_ge(ab_spill[i % 4], 16 * (i // 4))
                    b = 4 + 2 * (i % 2)
                    act.activation(ab_out[:, i % 4, :].rearrange("p (b c) -> p b c", b=2), ps[:, b:b + 2, :], ACT.Copy).then_inc(mix_act, 1)
                    act.wait_ge(mix_act, order[kind, i][2])
                    act.dma_start(ab_dram[i], ab_out[:, i % 4, :]).then_inc(ab_spill[i % 4], 16)
                elif kind == "qk":
                    if i == 1:
                        for n in range(4):
                            act.wait_ge(ab_spill[n], 32)
                    act.activation(qk[:, i, 0:H * DK], ps[:, i, 0:H * DK], ACT.Copy)
                    act.activation(qk[:, i, H * DK:HALF], ps[:, i, H * DK:HALF], ACT.Copy, scale=DK ** -0.5).then_inc(mix_act, 1)
                elif kind == "v":
                    act.activation(v[:, i, :], ps[:, i, :], ACT.Copy).then_inc(mix_act, 1)
                else:
                    n = i + (NCH if kind == "gb" else 0)
                    if n >= 6:
                        act.wait_ge(gate_spill[n % 6], 16 * (n // 6))
                    gb = gbuf_a[:, n % 6, :] if n % 6 < 2 else gbuf_b[:, n % 6 - 2, :]
                    act.activation(gb, ps[:, i, :], ACT.Silu).then_inc(mix_act, 1)
                    act.wait_ge(mix_act, order[kind, i][2])
                    act.dma_start(gate_dram[i, :, n // NCH, :], gb).then_inc(gate_spill[n % 6], 16)

            for g, (name, _) in enumerate(MIX_GROUPS):
                n_out = NCC if name in ("kc", "vc") else 8
                U = U_MIX + 4 * g + SLOTS
                for u in range(3):
                    if U + u < U_DFT:
                        act.wait_ge(mix_unit, 3 * g + u + 1)
                        hi(U + u)
                for i in range(n_out):
                    copy_out(name, i)
                if U + 3 < U_DFT:
                    act.wait_ge(mix_mm, order[name, n_out - 1][0])
                    hi(U + 3)
                if name == "vc":
                    for i in range(NCH):
                        copy_out("ab", i)

            for n, st in enumerate(STATES):
                fw = st
                bw = NCC - 1 - st if st < NCC else NCC + NCH - 1 - (st - NCC)
                act.wait_ge(u_mm, n + 1)
                act.activation(ust[0:DK, fw, :], ps[0:DK, 4 + n % 2, :], ACT.Copy)
                act.activation(ust[DK:P, bw, :], ps[DK:P, 4 + n % 2, :], ACT.Copy).then_inc(u_ev, 1)
                if n == 1:
                    act.wait_ge(mask_in, 16)
                    for n_ in range(6):
                        act.wait_ge(gate_spill[n_], 16 * len(range(n_, 2 * NCH, 6)))
                if n >= 2:
                    d, hd = divmod(n - 2, H)
                    act.activation(dm[:, d, hd, :], masks[:, d, :], ACT.Exp, scale=lg[:, d, hd:hd + 1]).then_inc(dm_exp, 1)
            for d in range(2):
                rows = slice(d * DK, (d + 1) * DK)
                for hd in range(H):
                    act.activation(xiT[rows, hd, :], masks[rows, 4, :], ACT.Exp, scale=lg[rows, d, hd:hd + 1]).then_inc(xi_done, 1)

            def turned(i):
                act.wait_ge(t_mm, i + 1)
                if i:
                    act.wait_ge(t_dve, i)
                act.activation(qT[:, :, :], ps[:, 0, :].rearrange("p (h c) -> p h c", h=H), ACT.Copy).then_inc(q_turned, 1)
                act.activation(kT[0:DK, :, :], ps[0:DK, 1, :].rearrange("p (h c) -> p h c", h=H), ACT.Copy).then_inc(t_act, 1)

            def normalise(i):
                act.wait_ge(var_done, i + 1)
                act.activation(rs[:, :], rs[:, :], ACT.Sqrt).then_inc(root_done, 1)
                act.wait_ge(rs_done, i + 1)
                if i >= 2:
                    act.wait_ge(y_done, i - 1)
                for d in range(2):
                    for hd in range(H):
                        n = d * H + hd
                        a = act.activation(on[:, i % 2, d, hd, :], ps[:, 4 + 2 * (i % 2) + d, hd * DV:(hd + 1) * DV], ACT.Identity,
                                           scale=rs[:, n:n + 1], bias=nmr[:, n:n + 1])
                a.then_inc(on_done, 1)

            def y_hi(i):
                act.wait_ge(y_mm, i + 1)
                act.activation(ret_hi[:, :, i * CH:(i + 1) * CH], ps[:, 3, :].rearrange("p (h c) -> p h c", h=H), ACT.Copy)\
                    .then_inc(yhi_done, 1)

            turned(0)
            for i in range(NCH):
                if i < NCH - 1:
                    turned(i + 1)
                if i >= 1:
                    normalise(i - 1)
                if i >= 2:
                    y_hi(i - 2)
                if i < 4:
                    hi(U_DFT + i)

            def z_hi_of(n):
                act.wait_ge(z_done, n + 1)
                if n >= 4:
                    act.wait_ge(f_mm, n - 3)
                else:
                    act.wait_ge(o_mm, NCH)
                act.activation(z_hi[:, n % 4, :, :, :], z_of(n), ACT.Copy).then_inc(zhi_done, 1)

            for n in range(4):
                z_hi_of(n)
            normalise(NCH - 1)
            for n in range(4 * FG):
                act.wait_ge(f_mm, n + 1)
                act.activation(four_hi[:, n // 4, BRANCHES[n % 4]:SEQ:4], ps[:, FOUR_BANKS[n % 4], 0:NQ], ACT.Copy).then_inc(fhi_done, 1)
                if n < 4 * (FG - 1):
                    z_hi_of(n + 4)
                if n in (1, 5):
                    y_hi(NCH - 2 + n // 4)
                if n in (6, 8, 10):
                    hi(U_OUT + (n - 6) // 2)
            n = NORM["b"]
            for m in range(KT):
                act.wait_ge(out_mm, 2 * m + 2)
                hi(U_OUT + m + 3)
                for c in range(2):
                    act.wait_ge(out_acc, 2 * m + c + 1)
                    square(n, c, m)
            for c in range(2):
                root(n, c)
            for c in range(2):
                for m in range(KT):
                    normed_hi(n, c, m)
            ffn(FFN[1], NORM["f"])

        @block.gpsimd
        def _(pool):
            pool.memset(ones[:, :], 1.0).then_inc(ones_set, 1)

            def lo(u, i=None):
                s = u % SLOTS
                pool.wait_ge(hi_done, u + 1 if i is None else UP_UNITS * i + (u + 1))
                a, b = halves(u)
                pool.tensor_tensor(b, stage[:, s, :], a.bitcast(F32), ALU.subtract).then_inc(lo_done, 1)

            def add_square(n, c, m):
                if m == 0:
                    return
                r = n.add_at[c, m]
                pool.wait_ge(n.sq, n.at[c, m] + 1)
                if r:
                    pool.wait_ge(n.add, r)
                pool.tensor_tensor(n.total[c][:, :], n.total[c][:, :], n.square[r % 2][:, 0:n.chunks[c][1]], ALU.add).then_inc(n.add, 1)

            def ffn(f, behind):
                end = f.u0 + UP_UNITS * GROUPS == U_END
                with pool.Fori(0, GROUPS - 1) as i:
                    for u in range(UP_UNITS):
                        lo(f.u0 + u + SLOTS, i)
                for u in range(SLOTS if end else 4):
                    lo(f.u0 + u + SLOTS, GROUPS - 1)
                for c in range(f.C):
                    for m in range(KT):
                        add_square(behind, c, m)
                if not end:
                    for u in (4, 5):
                        lo(f.u0 + u + SLOTS, GROUPS - 1)

            for c in range(3):
                for m in range(KT):
                    add_square(NORM["a"], c, m)
            for u in range(SLOTS):
                lo(u)
            ffn(FFN[0], NORM["m"])
            for u in range(U_MIX + SLOTS, U_DFT):
                lo(u)
            def gate(i):
                pool.wait_ge(on_done, i + 1)
                pool.wait_ge(gate_in[i % 2], 16 * (i // 2 + 1))
                o2 = on[:, i % 2, :, :, :].rearrange("p d h c -> p d (h c)")
                pool.tensor_tensor(o2, o2, gin[:, i % 2, :, :], ALU.mult).then_inc(gated, 1)
                pool.wait_ge(gated, i + 1)
                if i >= 2:
                    pool.wait_ge(y_mm, i - 1)
                pool.tensor_tensor(y[:, i % 2, :, :], on[:, i % 2, 0, :, :], on[:, i % 2, 1, :, :], ALU.add).then_inc(y_done, 1)

            for i in range(NCH - 1):
                gate(i)
                if i < 2:
                    lo(U_DFT + i)
                elif i == 5:
                    pool.wait_ge(t_mm, NCH)
                    lo(U_DFT + 2)
                    lo(U_DFT + 3)
            for n in range(4 * FG):
                pool.wait_ge(zhi_done, n + 1)
                pool.tensor_tensor(z_lo[:, n % 4, :, :, :], z_of(n), z_hi[:, n % 4, :, :, :].bitcast(F32), ALU.subtract)\
                    .then_inc(zlo_done, 1)
                if n == 3:
                    gate(NCH - 1)
                if n in (11, 13, 15):
                    lo(U_OUT + (n - 11) // 2)
            for m in range(KT):
                lo(U_OUT + m + 3)
                for c in range(2):
                    add_square(NORM["b"], c, m)
            ffn(FFN[1], NORM["f"])

        @block.vector
        def _(dve):
            steps = [0]

            def step(ins):
                steps[0] += 1
                ins.then_inc(dve_step, 1)
                dve.wait_ge(dve_step, steps[0])

            def mods_add_bias(i, bank, conds=2):
                return dve.tensor_tensor(mods[:, bass.ds(i, 1), :, 0:conds].rearrange("p o k w -> p (o k) w"),
                                         ps[:, bank, 0:2 * KT].rearrange("p (k w) -> p k w", w=2)[:, :, 0:conds],
                                         b_mod[:, bass.ds(i * KT, KT)].unsqueeze(2).to_broadcast([P, KT, conds]), ALU.add)

            def columns_of(n):
                j = "amb".index(n.tag)
                conds = 1 + n.chunks[-1][2]
                step(dve.tensor_scalar(atmp[:, :, 0:conds], mods[:, n.scale, :, 0:conds], 1.0, None, ALU.add))
                step(dve.tensor_tensor(acol[:, j, :, 0:conds], atmp[:, :, 0:conds],
                                       gains[:, n.gain, :].unsqueeze(2).to_broadcast([P, KT, conds]), ALU.mult))

            def rsqrt(n, c):
                dve.wait_ge(n.stat, c + 1)
                r = n.total[c][:, :]
                dve.tensor_scalar(r, ps[:, 7 - c % 2, 0:n.chunks[c][1]], 1.0 / D, EPS, ALU.mult, ALU.add).then_inc(n.var, 1)
                dve.wait_ge(n.root, c + 1)
                dve.reciprocal(r, r).then_inc(n.rec, 1)

            def normed_lo(n, q):
                c, m = divmod(q, KT)
                start, size, which = n.chunks[c]
                dve.wait_ge(n.hi, q + 1)
                x = slice(start, start + size)
                dve.scalar_tensor_tensor(x_lo[:, m, x], n.scaled[q % 3][:, 0:size], mods[:, n.shift, m, which:which + 1],
                                         x_hi[:, m, x].bitcast(F32), ALU.add, ALU.subtract).then_inc(n.lo, 1)

            def normed(n, c, m):
                chunk = n.chunks[c]
                if m == 0:
                    dve.wait_ge(n.rec, c + 1)
                if n.shift is None:
                    dve.scalar_tensor_tensor(h_of(m, chunk), h_of(m, chunk), gains[:, n.gain, m:m + 1], n.total[c][:, :], ALU.mult, ALU.mult)\
                        .then_inc(fin_done, 1)
                    return
                q = c * KT + m
                if q >= 3:
                    dve.wait_ge(n.lo, q - 2)
                j = "amb".index(n.tag)
                dve.scalar_tensor_tensor(n.scaled[q % 3][:, 0:chunk[1]], h_of(m, chunk), acol[:, j, m, chunk[2]:chunk[2] + 1],
                                         n.total[c][:, :], ALU.mult, ALU.mult).then_inc(n.t, 1)
                if m >= 2:
                    normed_lo(n, q - 2)
                if m == KT - 1:
                    normed_lo(n, q - 1)
                    normed_lo(n, q)

            def ffn(f, behind):
                C = f.C

                def mod_rows(i, k, mod):
                    dve.wait_ge(mod_in[k % 2], 16 * 4 * i + 16 * (k // 2 + 1))
                    if k:
                        dve.wait_ge(mod_chain, KT * i + (k + 2))
                    for which in range(mod):
                        acc = mod_acc_ctx if which else mod_acc_lat
                        w = mod_stage[:, k % 2, :]
                        s_ = cond[:, k, which:which + 1]
                        if k == 0:
                            a = dve.tensor_scalar(acc[:, :], w, s_, None, ALU.mult)
                        else:
                            a = dve.scalar_tensor_tensor(acc[:, :], w, s_, acc[:, :], ALU.mult, ALU.add)
                    a.then_inc(mod_chain, 1)

                def acc_step(i, c, m):
                    s = c * KT + m
                    chunk = f.chunks[c]
                    dve.wait_ge(f.down_done, KT * C * i + (s + 1))
                    hh = h_of(m, chunk)
                    dve.scalar_tensor_tensor(hh, ps[:, s % (2 * C), 0:chunk[1]], ghalf[:, f.gate, m, chunk[2]:chunk[2] + 1], hh,
                                             ALU.mult, ALU.add).then_inc(f.acc_done, 1)

                def body(i, mod, last=False):
                    for j in range(2):
                        def product(c):
                            start, size, _ = f.chunks[c]
                            dve.wait_ge(f.up_done, 4 * C * i + ((2 * j + 1) * C + c + 1))
                            dve.wait_ge(f.silu_done, 2 * C * i + (j * C + c + 1))
                            dve.wait_ge(f.glo_done, 2 * C * i + (j * C + c + 1))
                            dve.tensor_tensor(prod[c][:, :], silu_a[c][:, :], ps[:, C + c, 0:size], ALU.mult)\
                                .then_inc(f.mult_done, 1)

                        def rest(c):
                            start, size, _ = f.chunks[c]
                            dve.wait_ge(f.ghi_done, 2 * C * i + (j * C + c + 1))
                            g = slice(start, start + size)
                            dve.tensor_tensor(g_lo[:, j, g], prod[c][:, :], g_hi[:, j, g].bitcast(F32), ALU.subtract)\
                                .then_inc(f.glo_done, 1)

                        product(0)
                        for c in range(1, C):
                            product(c)
                            rest(c - 1)
                        rest(C - 1)
                        if mod and j == 0:
                            for k in range(KT):
                                mod_rows(i, k, mod)
                    if mod:
                        dve.wait_ge(mod_mm, i + 3)
                        mods_add_bias(i + 2, 6, mod).then_inc(mod_ready, 1)
                        dve.wait_ge(mod_ready, i + 3)
                        dve.tensor_scalar(ghalf[:, 0, :, :], mods[:, 2, :, :], 0.5, None, ALU.mult).then_inc(gate_ready, 1)
                        dve.wait_ge(gate_ready, i + 1)
                    if not last:
                        for c in range(C):
                            for m in range(KT):
                                acc_step(i, c, m)
                        return
                    if behind.shift is not None:
                        columns_of(behind)
                    for what, c, m in last_pass(C):
                        if what == "d":
                            acc_step(i, c, m)
                        elif what == "s":
                            rsqrt(behind, c)
                        else:
                            normed(behind, c, m)

                for first, end, mod in f.spans:
                    with dve.Fori(first, end) as i:
                        body(i, mod)
                body(GROUPS - 1, 0, last=True)

            dve.memset(rtmp[:, 0, 0, 0:1], 0.0).then_inc(lo_done, LO_BIAS)
            dve.memset(rtmp[:, 0, 0, 1:2], 0.0).then_inc(mod_chain, 2)
            dve.memset(rtmp[:, 0, 0, 2:3], 0.0).then_inc(FFN[0].acc_done, 2 * 3)
            dve.memset(rtmp[:, 0, 0, 3:4], 0.0).then_inc(FFN[1].acc_done, 2 * 2)
            dve.memset(rtmp[:, 0, 0, 4:5], 0.0).then_inc(FFN[0].glo_done, 3)
            dve.memset(rtmp[:, 0, 0, 5:6], 0.0).then_inc(FFN[1].glo_done, 2)

            dve.wait_ge(small_in, 16 * 7)
            for d in range(2):
                zz = dve.tensor_scalar(zeta[:, d, :], lg[:, d, :], pvec[:, d:d + 1], None, ALU.mult)
            step(zz)
            n = NORM["a"]
            for c in range(3):
                rsqrt(n, c)
            for i in range(2):
                dve.wait_ge(mod_mm, i + 1)
                mods_add_bias(i, 4 + i).then_inc(mod_ready, 1)
            dve.wait_ge(mod_ready, 2)
            columns_of(n)
            for c in range(3):
                for m in range(KT):
                    normed(n, c, m)
            ffn(FFN[0], NORM["m"])

            def copy_out(kind, i):
                mm, who, _, _ = order[kind, i]
                if who != "d":
                    return
                dve.wait_ge(mix_mm, mm)
                if kind == "fu":
                    dve.tensor_copy(ut[:, i // 2, (i % 2) * HALF:(i % 2 + 1) * HALF], ps[:, i, :]).then_inc(mix_dve, 1)
                elif kind == "vc":
                    dve.tensor_copy(v[:, NCH + i, :], ps[:, 2 + i, :]).then_inc(mix_dve, 1)
                elif kind == "qk":
                    if i == 0:
                        for n in range(4):
                            dve.wait_ge(ab_spill[n], 32)
                    dve.tensor_copy(qk[:, i, 0:H * DK], ps[:, i, 0:H * DK])
                    dve.tensor_scalar(qk[:, i, H * DK:HALF], ps[:, i, H * DK:HALF], DK ** -0.5, None, ALU.mult).then_inc(mix_dve, 1)
                elif kind == "v":
                    dve.tensor_copy(v[:, i, :], ps[:, i, :]).then_inc(mix_dve, 1)

            def rotate(i):
                _, who, count, _ = order["qk", i]
                wait_copied(dve, who, count)
                heads = qk[:, i, :].rearrange("p (n s c) -> p n s c", n=2 * H, s=2)
                cos = rope[:, i, 0, :].unsqueeze(1).to_broadcast([P, 2 * H, DK // 2])
                sin = rope[:, i, 1, :].unsqueeze(1).to_broadcast([P, 2 * H, DK // 2])
                dve.tensor_tensor(rtmp[:, 0, :, :], heads[:, :, 1, :], sin, ALU.mult)
                step(dve.tensor_tensor(rtmp[:, 1, :, :], heads[:, :, 0, :], sin, ALU.mult))
                dve.tensor_tensor(heads[:, :, 0, :], heads[:, :, 0, :], cos, ALU.mult)
                step(dve.tensor_tensor(heads[:, :, 1, :], heads[:, :, 1, :], cos, ALU.mult))
                dve.tensor_tensor(heads[:, :, 0, :], heads[:, :, 0, :], rtmp[:, 0, :, :], ALU.subtract)
                dve.tensor_tensor(heads[:, :, 1, :], heads[:, :, 1, :], rtmp[:, 1, :, :], ALU.add).then_inc(rope_done, 1)
                dve.wait_ge(rope_done, i + 1)

            for g, (name, _) in enumerate(MIX_GROUPS):
                if name in ("gf", "gb"):
                    continue
                for i in range(NCC if name in ("kc", "vc") else 8):
                    copy_out(name, i)
                if name == "qk":
                    dve.wait_ge(rope_in, 16)
                    for i in range(NCH):
                        rotate(i)

            dve.wait_ge(act_prep, 3)
            dve.wait_ge(mix_act, MIX_A)
            dve.wait_ge(mix_mm, len(outs))

            def state(j):
                if j:
                    dve.wait_ge(rec_done, j)
                for hd in range(H):
                    e = slice(hd * DV, (hd + 1) * DV)
                    a = dve.scalar_tensor_tensor(ust[:, j + 1, e], ust[:, j, e], dcs[:, hd:hd + 1], ust[:, j + 1, e], ALU.mult, ALU.add)
                a.then_inc(rec_done, 1)

            def twice(i):
                if i:
                    dve.wait_ge(t_mm, i)
                q_ = qk[:, i, 0:H * DK].rearrange("p (h c) -> p h c", h=H)
                dve.tensor_copy(qq[:, :, 0, :], q_)
                dve.tensor_copy(qq[:, :, 1, :], q_).then_inc(qq_done, 1)

            for n, st in enumerate(STATES):
                k = (kc[:, st, :] if st < NCC else qk[:, st - NCC, H * DK:HALF]).rearrange("p (h c) -> p h c", h=H)
                if n >= 2:
                    dve.wait_ge(u_mm, n - 1)
                for d in range(2):
                    kk = dve.tensor_tensor(kz[:, n % 2, :, d * DK:(d + 1) * DK], k,
                                           zeta[:, d, :].unsqueeze(2).to_broadcast([P, H, DK]), ALU.mult)
                kk.then_inc(kz_done, 1)
            twice(0)
            for d in range(2):
                dve.wait_ge(dm_exp, H * (d + 1))
                dve.tensor_tensor(dm[:, d, :, :], dm[:, d, :, :], masks[:, 2 + d, :].unsqueeze(1).to_broadcast([P, H, CH]), ALU.mult)\
                    .then_inc(dm_done, 1)
            dve.wait_ge(u_ev, NCC + NCH)
            for j in range(NCH):
                state(j)

            def turned(i):
                dve.wait_ge(q_turned, i + 1)
                if i >= 2:
                    dve.wait_ge(o_mm, i - 1)
                dve.tensor_tensor(qxT[:, i % 2, :, :], qT[:, :, :], xiT[:, :, :], ALU.mult)\
                    .then_inc(t_dve, 1)

            def decayed(i):
                dve.wait_ge(s_mm, i + 1)
                if i:
                    dve.wait_ge(o_mm, i)
                for d in range(2):
                    a = dve.tensor_tensor(pr[:, d, :, :], ps[:, 2, :].rearrange("p (h c) -> p h c", h=H), dm[:, d, :, :], ALU.mult)
                a.then_inc(p_done, 1)

            def moments(i):
                dve.wait_ge(o_mm, i + 1)
                if i:
                    dve.wait_ge(on_done, i)
                for n in range(2 * H):
                    a = dve.bn_stats(stats[:, n, :], ps[:, 4 + 2 * (i % 2) + n // H, (n % H) * DV:(n % H + 1) * DV])
                step(a)
                for n in range(2 * H):
                    a = dve.bn_aggr(mv[:, n, :], stats[:, n, :])
                step(a)
                dve.tensor_scalar(rs[:, :], mv[:, :, 1], EPS, None, ALU.add).then_inc(var_done, 1)
                dve.wait_ge(root_done, i + 1)
                step(dve.reciprocal(rs[:, :], rs[:, :]))
                dve.scalar_tensor_tensor(nmr[:, :], mv[:, :, 0], -1.0, rs[:, :], ALU.mult, ALU.mult).then_inc(rs_done, 1)

            def y_lo(i):
                dve.wait_ge(yhi_done, i + 1)
                cc = slice(i * CH, (i + 1) * CH)
                dve.tensor_tensor(ret_lo[:, :, cc], ps[:, 3, :].rearrange("p (h c) -> p h c", h=H), ret_hi[:, :, cc].bitcast(F32), ALU.subtract)\
                    .then_inc(ylo_done, 1)

            dve.wait_ge(dm_done, 2)
            dve.wait_ge(xi_done, 2 * H)
            turned(0)
            twice(1)
            for i in range(NCH):
                decayed(i)
                if i >= 1:
                    moments(i - 1)
                if i < NCH - 1:
                    turned(i + 1)
                if i < NCH - 2:
                    twice(i + 2)
                if i >= 3:
                    y_lo(i - 3)
            y_lo(NCH - 3)

            def butterflies(fg):
                x, e = [abuf[fg % 2][:, j, :, :, :] for j in range(4)], [eb[:, :, :, :] for eb in ebuf[fg % 2]]
                dve.wait_ge(ab_in[fg % 2], 16 * (fg // 2 + 1))
                if fg >= 2:
                    dve.wait_ge(zlo_done, 4 * (fg - 1))
                for j in range(2):
                    dve.tensor_tensor(e[j], x[j], x[2 + j], ALU.add)
                for j in range(2):
                    a = dve.tensor_tensor(x[2 + j], x[j], x[2 + j], ALU.subtract)
                step(a)
                dve.tensor_tensor(x[0], e[0], e[1], ALU.add).then_inc(z_done, 1)
                dve.tensor_tensor(x[1], e[0], e[1], ALU.subtract).then_inc(z_done, 1)
                dve.wait_ge(z_done, 4 * fg + 2)
                d0, d1 = x[2], x[3]
                dve.tensor_tensor(e[0][:, :, 0, :], d0[:, :, 0, :], d1[:, :, 1, :], ALU.subtract)
                dve.tensor_tensor(e[0][:, :, 1, :], d0[:, :, 1, :], d1[:, :, 0, :], ALU.add).then_inc(z_done, 1)
                dve.tensor_tensor(e[1][:, :, 0, :], d0[:, :, 0, :], d1[:, :, 1, :], ALU.add)
                dve.tensor_tensor(e[1][:, :, 1, :], d0[:, :, 1, :], d1[:, :, 0, :], ALU.subtract).then_inc(z_done, 1)

            butterflies(0)
            moments(NCH - 1)
            for n in range(4 * FG):
                fg, s = n // 4, BRANCHES[n % 4]
                if n % 4 == 0 and fg < FG - 1:
                    butterflies(fg + 1)
                dve.wait_ge(fhi_done, n + 1)
                dve.tensor_tensor(four_lo[fg][:, s:SEQ:4], ps[:, FOUR_BANKS[n % 4], 0:NQ], four_hi[:, fg, s:SEQ:4].bitcast(F32), ALU.subtract)\
                    .then_inc(flo_done, 1)
                if n in (1, 5):
                    y_lo(NCH - 2 + n // 4)

            step(dve.tensor_scalar(ghalf[:, 1, :, 0:1], mods[:, 8, :, 0:1], 0.5, None, ALU.mult))
            for m in range(KT):
                for c in range(2):
                    n = 2 * m + c
                    dve.wait_ge(out_mm, n + 1)
                    hh = h_lat[:, m, c * HALF:(c + 1) * HALF]
                    dve.scalar_tensor_tensor(hh, ps[:, n % 4, :], mods[:, 5, m, 0:1], hh, ALU.mult, ALU.add).then_inc(out_acc, 1)
            n = NORM["b"]
            columns_of(n)
            for c in range(2):
                rsqrt(n, c)
            for c in range(2):
                for m in range(KT):
                    normed(n, c, m)
            ffn(FFN[1], NORM["f"])


def constants():
    f = np.float32
    pos = np.arange(CH, dtype=np.float64)
    n_freq = DK // 4
    inv = (f(10000.0) ** (-np.arange(n_freq, dtype=f) / f(n_freq))).astype(f)
    tok = np.arange(SEQ)
    ang = np.concatenate([(tok // 64).astype(f)[:, None] * inv, (tok % 64).astype(f)[:, None] * inv], axis=-1).astype(np.float64)
    rope = np.stack([np.cos(ang), np.sin(ang)], 1).astype(f)
    diff = pos[None, :] - pos[:, None]
    xi = np.concatenate([np.tile(pos + 1, (DK, 1)), np.tile(CH - pos, (DK, 1))])
    masks = np.stack([np.maximum(diff, 0), np.maximum(-diff, 0), diff >= 0, diff <= 0, xi], 1).astype(f)
    pvec = np.stack([CH - 1 - pos, pos], 1).astype(f)
    a = 2 * np.pi * np.outer(np.arange(FC), np.arange(FC)) / FC
    chan = np.concatenate([np.cos(a), np.sin(a)], 1) / np.sqrt(SEQ * FC)
    n = np.arange(NQ)[:, None, None]
    k = 4 * np.arange(NQ)[None, None, :] + np.arange(4)[None, :, None]
    a = 2 * np.pi * (n * k % SEQ) / SEQ
    dft = np.stack([np.cos(a), -np.sin(a)], 0).reshape(2, 2, P, 4 * NQ).transpose(1, 0, 2, 3).reshape(4, P, 4 * NQ)
    return {
        "ident": np.eye(P, dtype=f),
        "chan": chan.astype(f),
        "pvec": pvec,
        "rope": np.ascontiguousarray(rope.reshape(NCH, P, 2, DK // 2).transpose(1, 0, 2, 3)),
        "masks": masks,
        "dft": np.ascontiguousarray(dft.astype(f)),
    }


def kernel(x, c, ctx, c_ctx, w_mod, b_mod, norm_ffn1, w13_ffn1, w2_ffn1, norm_mix, w_in, ret_log_decay, w_out,
           norm_ffn2, w13_ffn2, w2_ffn2, norm_final):
    import concourse.bacc as bacc
    from concourse.bass_utils import run_bass_kernel_spmd

    A = lambda a: np.asarray(a)
    tiles = lambda a: A(a).reshape(KT, P, -1)
    columns = lambda a: A(a).reshape(-1, P).T

    def w13(a):
        return A(a)[0].reshape(KT, P, 2, FT, P).transpose(3, 2, 1, 0, 4).reshape(2 * FT, P, UNIT)

    arrays = {
        "x": tiles(A(x)[0].T), "ctx": tiles(A(ctx)[0].T),
        "cond": np.stack([columns(A(c)[0]), columns(c_ctx)], 2),
        "w_mod01": A(w_mod)[0][:, :2 * D].reshape(KT, P, 2 * KT, P).transpose(2, 1, 0, 3).reshape(2 * KT, P, UNIT),
        "w_mod": A(w_mod)[0][:, 2 * D:].reshape(KT, P, NMOD - 2, D).transpose(2, 0, 1, 3).reshape((NMOD - 2) * KT, P, D),
        "b_mod": columns(A(b_mod)[0]),
        "gains": np.stack([columns(A(g).reshape(-1)) for g in (norm_ffn1, norm_mix, norm_ffn2, norm_final)], 1),
        "w13_1": w13(w13_ffn1), "w2_1": A(w2_ffn1)[0].reshape(FT, P, D),
        "w13_2": w13(w13_ffn2), "w2_2": A(w2_ffn2)[0].reshape(FT, P, D),
        "w_in": A(w_in)[0].reshape(4, 2, P, 5, HALF).transpose(3, 0, 2, 1, 4).reshape(5, 4, P, UNIT),
        "lg": A(ret_log_decay)[0],
        "w_out": A(w_out)[0].reshape(KT, P, KT, P).transpose(2, 1, 0, 3).reshape(KT, P, UNIT),
        **constants(),
    }
    arrays = {"in_" + k: np.ascontiguousarray(a) for k, a in arrays.items()}
    nc = bacc.Bacc("TRN2", target_bir_lowering=False, num_devices=1)
    t = {k[3:]: nc.dram_tensor(k, a.shape, F32, kind="ExternalInput").ap() for k, a in arrays.items()}
    t["lg"] = t["lg"].partition_broadcast(P)
    t["out"] = nc.dram_tensor("out", (KT, P, SEQ), F32, kind="ExternalOutput").ap()
    build(nc, t)
    got = run_bass_kernel_spmd(nc, [arrays], core_ids=[0]).results[0]["out"]
    return np.ascontiguousarray(got.reshape(D, SEQ).T)[None]
```

```python
from contextlib import ExitStack

import numpy as np

import concourse.bass as bass
from concourse import mybir
from concourse.alu_op_type import AluOpType as ALU

F32 = mybir.dt.float32
F32R = mybir.dt.float32r
ACT = mybir.ActivationFunctionType

P = 128
D = 1024
KT = D // P
SEQ, CTX = 1024, 256
TOK = SEQ + CTX
FF = 2816
FT = FF // P
GROUPS = FT // 2
NMOD = 9
PRE = KT // 2
H, DK, DV = 4, 64, 128
FG, FC = 4, 128
CH = 128
NCH, NCC = SEQ // CH, CTX // CH
EPS = 1e-6
SLOTS = 3
UNIT = 1024
HALF = 512
NQ = SEQ // 4

UP_UNITS = 6
U_FFN1 = 0
U_MIX = U_FFN1 + UP_UNITS * GROUPS
MIX_GROUPS = (("fu", 4), ("kc", 0), ("vc", 1), ("qk", 0), ("v", 1), ("gf", 2), ("gb", 3))
U_DFT = U_MIX + 4 * len(MIX_GROUPS)
U_OUT = U_DFT + 4
U_FFN2 = U_OUT + KT
U_END = U_FFN2 + UP_UNITS * GROUPS
STATES = tuple(range(NCC)) + tuple(NCC + c for j in range(NCH // 2) for c in (j, NCH - 1 - j))
WORDS = 53208
BRANCHES = (0, 2, 1, 3)
FOUR_BANKS = (0, 1, 2, 4)
LO_BIAS = SLOTS


def ring(u):
    return u if u < U_DFT else u - 4


class Ffn:

    def __init__(self, tag, u0, chunks, gate, with_mods):
        self.tag, self.u0, self.chunks, self.gate, self.with_mods = tag, u0, chunks, gate, with_mods
        self.C = len(chunks)
        self.spans = ((0, 3, 2), (3, NMOD - 2, 1), (NMOD - 2, GROUPS - 1, 0)) if with_mods else ((0, GROUPS - 1, 0),)


OUT_ORDER = tuple((m, c) for m in range(KT - SLOTS) for c in range(2)) + tuple((m, c) for c in range(2) for m in range(KT - SLOTS, KT))


UNIT_AT = {2 * m + 1: U_OUT + SLOTS + m for m in range(KT - SLOTS)}
UNIT_AT.update({2 * (KT - SLOTS) + n: U_FFN2 + n for n in range(SLOTS)})


class Norm:

    def __init__(self, tag, chunks, shift, scale, gain):
        self.tag, self.chunks, self.shift, self.scale, self.gain = tag, chunks, shift, scale, gain
        C = len(chunks)
        by_chunk = [(c, m) for c in range(C) for m in range(KT)]
        if tag == "a":
            tiles = [(c, m) for m in range(KT) for c in range(2)] + [(2, m) for m in range(KT)]
        elif tag == "b":
            tiles = [(c, m) for m, c in OUT_ORDER]
        else:
            tiles = by_chunk
        self.squares = tiles
        self.at = {x: n for n, x in enumerate(tiles)}
        self.adder = {c: int(tag == "a" and c == 1) for c in range(C)}
        adds = [[x for x in tiles if x[1] and self.adder[x[0]] == who] for who in range(2)]
        self.add_at = {x: n for l in adds for n, x in enumerate(l)}
        self.added = {c: self.add_at[c, KT - 1] + 1 for c in range(C)}
        self.bank = (7, 6, 5)
        self.kept = (1, 2) if tag == "m" else ()
        self.groups = [[(c, 2 * g + m) for c in range(2) for m in range(2)] for g in range(PRE)] + [[(2, m) for m in range(KT)]]
        self.tiles = [x for group in self.groups for x in group] if tag == "a" else by_chunk
        self.tile_at = {x: n for n, x in enumerate(self.tiles)}
        self.catch_up = {len(self.tiles) - 1} if tag == "a" else {c * KT + KT - 1 for c in range(C)}


def last_pass(C):
    plan = [("d", 0, m) for m in range(KT)] + [("d", 1, m) for m in range(3)] + [("s", 0, 0)]
    plan += [("d", 1, 3), ("d", 1, 4), ("f", 0, 0)]
    for m in range(3):
        plan += [("d", 1, 5 + m), ("n", 0, m)]
    return plan + [("d", 2, m) for m in range(KT) if C == 3]


def behind_pass(C):
    plan = [("n", 0, 3), ("n", 0, 4), ("s", 1, 0), ("n", 0, 5), ("n", 0, 6), ("n", 0, 7)]
    if C == 2:
        return plan + [("n", 1, m) for m in range(KT)]
    return plan + [("s", 2, 0), ("k", 1, 0), ("n", 1, 0), ("n", 1, 1), ("k", 2, 0)] + [("n", 1, m) for m in range(2, KT)]\
        + [("n", 2, m) for m in range(KT)]


LAT = ((0, 512, 0), (512, 512, 0))
ALL = LAT + ((1024, 256, 1),)


def slab_offset(nc, slab):
    return nc.lookup_mloc(slab.name).addr


def build(nc, t):
    ctx = ExitStack()
    with ctx:
        sem = lambda name: ctx.enter_context(nc.semaphore(name))

        slab = ctx.enter_context(nc.sbuf_tensor("slab", [P, WORDS], F32))
        base = slab_offset(nc, slab)

        def place(name, words, offset, dtype=F32, shape=None):
            return nc.alloc_sbuf_tensor_at(name, [P, words] if shape is None else [P, *shape], dtype,
                                           offset=base + 4 * offset)

        o = 0
        h_lat = place("h_lat", 0, o, shape=[KT, SEQ]); o += KT * SEQ
        O_HCTX = o
        h_ctx = place("h_ctx", 0, o, shape=[KT, CTX]); o += KT * CTX
        O_X = o
        x_hi = place("x_hi", 0, o, F32R, [KT, TOK]); o += KT * TOK
        x_lo = place("x_lo", 0, o, F32R, [KT, TOK]); o += KT * TOK
        O_W = o
        w_hi = place("w_hi", 0, o, F32R, [SLOTS, UNIT]); o += SLOTS * UNIT
        w_lo = place("w_lo", 0, o, F32R, [SLOTS, UNIT]); o += SLOTS * UNIT
        stage = place("stage", 0, o, shape=[SLOTS, UNIT]); o += SLOTS * UNIT
        O_R = o
        g_hi = place("g_hi", 0, o, F32R, [2, TOK]); o += 2 * TOK
        g_lo = place("g_lo", 0, o, F32R, [2, TOK]); o += 2 * TOK
        O_SCR = o
        silu_a = [place(f"silu_a{c}", 0, o + at, shape=[HALF // (1 + (c == 2))]) for c, at in enumerate((0, 512, 2048))]
        prod = [place(f"prod{c}", 0, o + at, shape=[HALF // (1 + (c == 2))]) for c, at in enumerate((1024, 1536, 2304))]
        mod_acc_ctx = place("mod_acc_ctx", 0, o + 2560, shape=[D]); o += 3584
        O_MS = o
        mod_stage = place("mod_stage", 0, o, shape=[2, UNIT]); o += 2 * UNIT
        def small(name, *shape):
            nonlocal o
            words = int(np.prod(shape))
            x = place(name, 0, o, shape=list(shape)); o += words + (-words) % 8
            return x
        mods = small("mods", NMOD, KT, 2)
        gains = small("gains", 4, KT)
        cond = small("cond", KT, 2)
        acol = small("acol", 3, KT, 2)
        ghalf = small("ghalf", 2, KT, 2)
        lg = small("lg", 2, H)
        pvec = small("pvec", 2)
        zeta = small("zeta", 2, H)
        dcs = small("dcs", H)
        stats = small("stats", 2 * H, 6)
        mv = small("mv", 2 * H, 2)
        rs = small("rs", 2 * H)
        nmr = small("nmr", 2 * H)
        rt = small("rt", 3, 4)
        ones = small("ones", P)
        ident = small("ident", P)
        O_ROPE = o
        rope = small("rope", NCH, 2, DK // 2)
        rtmp = small("rtmp", 2, 2 * H, DK // 2)
        O_LAST = o
        chan = small("chan", 2 * FC)
        b_mod = small("b_mod", NMOD * KT)
        assert max(o, O_LAST + 512) <= WORDS, o
        mod_acc_lat = place("mod_acc_lat", 0, O_ROPE, shape=[D])

        spots = [O_X + 2 * KT * TOK - 4 * UNIT + n * UNIT for n in range(4)] + [O_R + 3840 + n * UNIT for n in range(6)]\
            + [O_W + (s_ + i * SLOTS) * UNIT for s_ in range(SLOTS) for i in range(2)]
        mod_pre = [place(f"mod_pre{n}", 0, at, shape=[UNIT]) for n, at in enumerate(spots)]
        mod_flat = [place(f"mod_flat{n}", 0, at, shape=[HALF]) for n, at in enumerate((O_R + 9984, O_ROPE))]
        qk = place("qk", 0, O_R, shape=[NCH, HALF])
        ab_out = place("ab_out", 0, O_R, shape=[4, UNIT])
        kc = place("kc", 0, O_R + 4096, shape=[NCC, H * DK])
        v = place("v", 0, O_R + 4608, shape=[NCH + NCC, HALF])
        ut = place("ut", 0, O_R + 4608, shape=[FG, SEQ])
        gbuf_a = place("gbuf_a", 0, O_R + 9728, shape=[2, HALF])
        gbuf_b = place("gbuf_b", 0, O_HCTX, shape=[4, HALF])
        q = O_X
        ret_hi = place("ret_hi", 0, q, F32R, [H, SEQ]); q += H * SEQ
        ret_lo = place("ret_lo", 0, q, F32R, [H, SEQ]); q += H * SEQ
        O_TMP = q
        ust = place("ust", 0, q, shape=[NCH + NCC, H * DV]); q += (NCH + NCC) * H * DV
        qq = place("qq", 0, q, shape=[H, 2, DK]); q += 512
        qxT = place("qxT", 0, q, shape=[2, H, CH]); q += 1024
        pr = place("pr", 0, q, shape=[2, H, CH])
        q += 1024
        on = place("on", 0, q, shape=[2, 2, H, DV])
        kz = place("kz", 0, q, shape=[2, H, P]); q += 2048
        gin = place("gin", 0, q, shape=[2, 2, HALF]); q += 2048
        assert q <= O_X + 2 * KT * TOK
        qT = place("qT", 0, O_HCTX, shape=[H, CH])
        kT = place("kT", 0, O_HCTX + 512, shape=[H, CH])
        y = place("y", 0, O_HCTX + 1024, shape=[2, H, DV])
        masks = place("masks", 0, O_ROPE, shape=[5, CH])
        xiT = place("xiT", 0, O_LAST, shape=[H, CH])
        dm = place("dm", 0, O_R + 9728, shape=[2, H, CH])
        df_hi = place("df_hi", 0, O_W, F32R, [4, UNIT])
        df_lo01 = place("df_lo01", 0, O_W + 4096, F32R, [2, UNIT])
        df_lo23 = place("df_lo23", 0, O_R, F32R, [2, UNIT])
        df_lo = [(df_lo01 if u < 2 else df_lo23)[:, u % 2, :] for u in range(4)]
        q = O_TMP
        z_hi = place("z_hi", 0, q, F32R, [4, 2, 2, FC]); q += 2048
        z_lo = place("z_lo", 0, q, F32R, [4, 2, 2, FC]); q += 2048
        abuf = [place("abuf0", 0, O_R + 2048, shape=[4, 2, 2, FC]), place("abuf1", 0, q, shape=[4, 2, 2, FC])]; q += 2048
        out_hi = place("out_hi", 0, q, F32R, [SLOTS, UNIT]); q += SLOTS * UNIT
        out_lo = place("out_lo", 0, q, F32R, [SLOTS, UNIT]); q += SLOTS * UNIT
        assert q <= O_X + 2 * KT * TOK
        four_hi = place("four_hi", 0, O_R + 4096, F32R, [FG, SEQ])
        four_lo = [place(f"four_lo{fg}", 0, at, F32R, [SEQ]) for fg, at in enumerate((O_R + 8192, O_R + 9216, O_HCTX, O_HCTX + 1024))]
        ebuf = [[place(f"ebuf{n}{j}", 0, at, shape=[2, 2, FC]) for j, at in enumerate(ats)]
                for n, ats in enumerate(((O_ROPE, O_ROPE + 512), (O_R + 10240, O_LAST)))]

        ps = ctx.enter_context(nc.psum_tensor("ps", [P, 8, HALF], F32))
        ab_dram = nc.dram_tensor("ab_dram", (NCH, P, UNIT), F32).ap()
        gate_dram = nc.dram_tensor("gate_dram", (NCH, P, 2, HALF), F32).ap()

        stage_in = [sem(f"stage_in{i}") for i in range(SLOTS)]
        hi_done, lo_done, mix_unit = sem("hi_done"), sem("lo_done"), sem("mix_unit")
        mod_in = [sem(f"mod_in{i}") for i in range(2)]
        mod_mm, mod_ready = sem("mod_mm"), sem("mod_ready")
        mod_row_mm, mod_flat_done = sem("mod_row_mm"), sem("mod_flat_done")
        gate_ready = sem("gate_ready")
        mod_chain = sem("mod_chain")
        ctx_in, small_in, cond_ready, ones_set = (sem(n) for n in ("ctx_in", "small_in", "cond_ready", "ones_set"))
        pre_in = [sem(f"pre_in{i}") for i in range(KT)]
        x_in = [sem(f"x_in{i}") for i in range(KT // 2)]
        rope_in = sem("rope_in")
        dve_step, act_prep = sem("dve_step"), sem("act_prep")

        FFN = [Ffn("1", U_FFN1, ALL, 0, True), Ffn("2", U_FFN2, LAT, 1, False)]
        for f in FFN:
            f.up_done, f.silu_done, f.mult_done, f.ghi_done, f.glo_done, f.down_done, f.acc_done = (
                sem(n + f.tag) for n in ("up_done", "silu_done", "mult_done", "ghi_done", "glo_done", "down_done", "acc_done"))

        O_G = O_R
        SPOTS = {"a": ((O_G, O_G + 512), (O_G + 1024, O_G + 1536, O_G + 2048), (O_G + 2304, O_G + 2816, O_G + 3328)),
                 "m": ((O_SCR + 2560, O_SCR + 3072), (O_MS, O_MS + 512, O_MS + 1024), (O_MS + 1280, O_ROPE, O_ROPE + 512)),
                 "b": ((O_G, O_G + 512), (O_G + 1024, O_G + 1536), (O_G + 2048, O_G + 2560, O_G + 3072)),
                 "f": ((O_HCTX, O_HCTX + 512), (O_MS, O_MS + 512), (O_MS + 1024, O_HCTX + 1024, O_HCTX + 1536))}
        NORM = {}
        for tag, chunks, shift, scale, gain in (("a", ALL, 0, 1, 0), ("m", ALL, 3, 4, 1), ("b", LAT, 6, 7, 2), ("f", LAT, None, None, 3)):
            n = Norm(tag, chunks, shift, scale, gain)
            squares, sums, scaled = SPOTS[tag]
            n.square = [[place(f"square{who}{j}_{tag}", 0, at, shape=[HALF]) for j, at in enumerate(ats)]
                        for who, ats in enumerate((squares, (O_ROPE, O_ROPE + 512) if tag == "a" else ()))]
            n.total = [place(f"total{c}_{tag}", 0, at, shape=[chunks[c][1]]) for c, at in enumerate(sums)]
            n.scaled = [place(f"scaled{j}_{tag}", 0, at, shape=[HALF]) for j, at in enumerate(scaled)]
            n.sq, n.stat, n.var, n.root, n.rec, n.diag, n.spread, n.t, n.hi, n.lo = (
                sem(s + "_" + tag) for s in ("n_sq", "n_stat", "n_var", "n_root", "n_rec", "n_diag", "n_spread", "n_t", "n_hi", "n_lo"))
            n.keep = sem("n_keep_" + tag)
            n.add = [sem(s + "_" + tag) for s in (("n_add", "n_add_dve") if tag == "a" else ("n_add",))]
            NORM[tag] = n

        mix_mm, mix_act, mix_dve = sem("mix_mm"), sem("mix_act"), sem("mix_dve")
        ab_spill = [sem(f"ab_spill{i}") for i in range(4)]
        gate_spill = [sem(f"gate_spill{i}") for i in range(6)]
        rope_done = sem("rope_done")
        mask_in, dm_exp, dm_done = sem("mask_in"), sem("dm_exp"), sem("dm_done")
        kz_done, u_mm, u_ev, rec_done = sem("kz_done"), sem("u_mm"), sem("u_ev"), sem("rec_done")
        qq_done, t_mm, t_act, t_dve = sem("qq_done"), sem("t_mm"), sem("t_act"), sem("t_dve")
        s_mm, p_done, o_mm, var_done, root_done, rs_done = (sem(n) for n in ("s_mm", "p_done", "o_mm", "var_done", "root_done", "rs_done"))
        xi_done, gated, q_turned = sem("xi_done"), sem("gated"), sem("q_turned")
        on_done, y_done, y_mm, yhi_done, ylo_done = (sem(n) for n in ("on_done", "y_done", "y_mm", "yhi_done", "ylo_done"))
        gate_in = [sem(f"gate_in{i}") for i in range(2)]
        ab_in = [sem(f"ab_in{i}") for i in range(2)]
        z_done, zhi_done, zlo_done, f_mm, fhi_done, flo_done = (
            sem(n) for n in ("z_done", "zhi_done", "zlo_done", "f_mm", "fhi_done", "flo_done"))
        out_mm, out_acc = sem("out_mm"), sem("out_acc")
        fin_done, stored = sem("fin_done"), sem("stored")

        block = ctx.enter_context(nc.Block())

        def h_of(m, chunk):
            start, n, which = chunk
            return h_ctx[:, m, :] if which else h_lat[:, m, start:start + n]

        outs = []
        for name, _ in MIX_GROUPS:
            if name == "fu":
                outs += [("fu", n, (n,), "ad"[n % 2 == 0]) for n in range(8)]
            elif name == "kc":
                outs += [("kc", n, (n,), "a") for n in range(NCC)]
            elif name == "vc":
                outs += [("vc", n, (2 + n,), "da"[n]) for n in range(NCC)]
                outs += [("ab", n, (4 + 2 * (n % 2), 5 + 2 * (n % 2)), "a") for n in range(NCH)]
            else:
                outs += [(name, n, (n,), "a" if name in ("gf", "gb") else "ad"[n % 2 == 0]) for n in range(NCH)]
        order = {}
        counts = {"a": 0, "d": 0}
        last_in_bank = {}
        for n, (kind, i, banks, who) in enumerate(outs):
            counts[who] += 1
            before = [last_in_bank[b] for b in banks if b in last_in_bank]
            order[kind, i] = (n + 1, who, counts[who], before)
            for b in banks:
                last_in_bank[b] = (who, counts[who])
        MIX_A, MIX_D = counts["a"], counts["d"]

        def halves(u):
            if U_DFT <= u < U_OUT:
                return df_hi[:, u - U_DFT, :], df_lo[u - U_DFT]
            s_ = ring(u) % SLOTS
            if U_OUT <= u < U_FFN2:
                return out_hi[:, s_, :], out_lo[:, s_, :]
            return w_hi[:, s_, :], w_lo[:, s_, :]

        def z_of(n):
            fg, j = divmod(n, 4)
            return abuf[fg % 2][:, j, :, :, :] if j < 2 else ebuf[fg % 2][j - 2][:, :, :, :]

        def wait_copied(e, who, count):
            e.wait_ge(mix_act if who == "a" else mix_dve, count)

        def mm3(pe, out, wh, wl, xh, xl, start, stop):
            pe.matmul(out, wl, xh, start=start, stop=False)
            pe.matmul(out, wh, xl, start=False, stop=False)
            return pe.matmul(out, wh, xh, start=False, stop=stop)

        @block.sync
        def _(sp):
            def unit(u, src, more=0):
                s = u % SLOTS
                sp.wait_ge(lo_done, more + (u - SLOTS + 1 + LO_BIAS))
                sp.dma_start(stage[:, s, :], src).then_inc(stage_in[s], 16)

            sp.dma_start(cond[:, :, :], t["cond"]).then_inc(small_in, 16)
            sp.dma_start(b_mod[:, :], t["b_mod"]).then_inc(small_in, 16)
            sp.dma_start(gains[:, :, :], t["gains"]).then_inc(small_in, 16)
            for dst, name in ((ident[:, :], "ident"), (chan[:, :], "chan"), (pvec[:, :], "pvec")):
                sp.dma_start(dst, t[name]).then_inc(small_in, 16)
            sp.dma_start(lg[:, :, :], t["lg"]).then_inc(small_in, 16)
            def mod_weights(j):
                for n in (2 * j, 2 * j + 1):
                    sp.dma_start(mod_pre[n][:, :], t["w_mod01"][n]).then_inc(pre_in[j], 16)

            mod_weights(0)
            mod_weights(1)
            for j in range(KT // 2):
                sp.dma_start(h_lat[:, 2 * j:2 * j + 2, :], t["x"][2 * j:2 * j + 2].rearrange("m p c -> p m c")).then_inc(x_in[j], 16)
            mod_weights(2)
            mod_weights(3)
            sp.dma_start(h_ctx[:, :, :], t["ctx"].rearrange("m p c -> p m c")).then_inc(ctx_in, 16)
            mod_weights(4)
            mod_weights(5)
            unit(0, t["w13_1"][0])
            mod_weights(6)
            mod_weights(7)

            def mod_row(group, k):
                sp.wait_ge(mod_chain, KT * group + (k + 1))
                sp.dma_start(mod_stage[:, k % 2, :], t["w_mod"][bass.ds(KT * group + k, 1)].rearrange("o p c -> (o p) c"))\
                    .then_inc(mod_in[k % 2], 16)

            def ffn_units(f, w13, w2):
                def body(i, other_rows, first_rows, first=0):
                    for u in range(first, UP_UNITS):
                        src = w13[bass.ds(4 * i + u, 1)] if u < 4 else w2[bass.ds(2 * i + (u - 4), 1)]
                        unit(f.u0 + u, src.rearrange("o p c -> (o p) c"), UP_UNITS * i)
                        if other_rows and u == 1:
                            for k in range(2, KT):
                                mod_row(i - 1, k)
                    if first_rows:
                        for k in range(2):
                            mod_row(i, k)
                if not f.with_mods:
                    with sp.Fori(0, GROUPS) as i:
                        body(i, False, False)
                    return
                body(0, False, True, first=1)
                with sp.Fori(1, NMOD - 2) as i:
                    body(i, True, True)
                body(NMOD - 2, True, False)
                with sp.Fori(NMOD - 1, GROUPS) as i:
                    body(i, False, False)

            ffn_units(FFN[0], t["w13_1"], t["w2_1"])
            for g, (name, cols) in enumerate(MIX_GROUPS):
                for u in range(4):
                    unit(U_MIX + 4 * g + u, t["w_in"][cols, u])
                if g == 0:
                    sp.wait_ge(NORM["m"].lo, KT * 3)
                    sp.dma_start(rope[:, :, :, :], t["rope"]).then_inc(rope_in, 16)
            sp.wait_ge(rope_done, NCH)
            sp.dma_start(masks[:, :], t["masks"]).then_inc(mask_in, 16)
            for u in range(3):
                unit(U_DFT + u, t["dft"][u])
            sp.wait_ge(mix_mm, len(outs))
            for n in range(6):
                sp.wait_ge(gate_spill[n], 16 * len(range(n, 2 * NCH, 6)))
            def group_in(fg):
                if fg == 0:
                    for n in range(4):
                        sp.wait_ge(ab_spill[n], 16 * 2)
                    sp.wait_ge(t_mm, NCH)
                elif fg == 1:
                    sp.wait_ge(o_mm, NCH)
                    sp.wait_ge(t_dve, NCH)
                else:
                    sp.wait_ge(z_done, 4 * (fg - 1))
                    sp.wait_ge(zlo_done, 4 * (fg - 2) + 2)
                sp.dma_start(abuf[fg % 2][:, :, :, :, :].rearrange("p j t a c -> p (j t) (a c)"),
                             ab_dram[:, :, fg * 2 * FC:(fg + 1) * 2 * FC].rearrange("t p c -> p t c")).then_inc(ab_in[fg % 2], 16)

            for i in range(NCH):
                if i == NCH - 1:
                    group_in(0)
                if i >= 2:
                    sp.wait_ge(y_done, i - 1)
                sp.dma_start(gin[:, i % 2, :, :], gate_dram[i]).then_inc(gate_in[i % 2], 16)
                if i == 3:
                    unit(U_DFT + 3, t["dft"][3])
            for n in range(3):
                group_in(n + 1)
                unit(U_OUT + n, t["w_out"][n])
            for u in range(3, KT):
                unit(U_OUT + u, t["w_out"][u])
            ffn_units(FFN[1], t["w13_2"], t["w2_2"])
            for c in range(2):
                for m in range(KT):
                    sp.wait_ge(fin_done, c * KT + m + 1)
                    sp.dma_start(t["out"][m, :, c * HALF:(c + 1) * HALF], h_lat[:, m, c * HALF:(c + 1) * HALF]).then_inc(stored, 16)
            sp.wait_ge(stored, 16 * 2 * KT)

        @block.tensor
        def _(pe):
            def sum_partitions(n, c):
                pe.wait_ge(n.add[n.adder[c]], n.added[c])
                for q in range(n.chunks[c][1] // P):
                    mm = pe.matmul(ps[:, n.bank[c], q:q + 1], n.total[c][:, q * P:(q + 1) * P], ones[:, 0:1], start=True, stop=True)
                mm.then_inc(n.stat, 1)

            def spread(n, c):
                pe.wait_ge(n.diag, c + 1)
                pe.matmul(ps[:, n.bank[c], 0:n.chunks[c][1]], ones[:, :], n.total[c][:, :], start=True, stop=True).then_inc(n.spread, 1)

            def mod_group(g, kpairs):
                if 0 in kpairs and g >= 2:
                    pe.wait_ge(mod_flat_done, g - 1)
                for q in kpairs:
                    if q % 2 == 0:
                        pe.wait_ge(pre_in[2 * g + q // 2], 16 * 2)
                    for kk in range(2):
                        k = 2 * q + kk
                        mm = pe.matmul(ps[0:2, g % 2, :], cond[:, k, :], mod_pre[4 * g + q][:, kk * HALF:(kk + 1) * HALF],
                                       start=(k == 0), stop=(k == KT - 1))
                if k == KT - 1:
                    mm.then_inc(mod_row_mm, 1)

            def turn_mods(g):
                pe.wait_ge(mod_flat_done, g + 1)
                if g >= 2:
                    pe.wait_ge(mod_ready, g - 1)
                for n in range(4):
                    mm = pe.matmul(ps[:, 2 + g % 2, 2 * n:2 * n + 2], mod_flat[g % 2][0:2, n * P:(n + 1) * P], ident[0:2, 0:2],
                                   start=True, stop=True)
                mm.then_inc(mod_mm, 1)

            def ffn(f, n, behind):
                C = f.C

                def down(i, c, m):
                    start, size, _ = f.chunks[c]
                    s4, s5 = (ring(f.u0 + u) % SLOTS for u in (4, 5))
                    step = c * KT + m
                    b = step % (2 * C)
                    if m == 0:
                        pe.wait_ge(f.glo_done, 2 * C * i + (2 * C + c + 1))
                    if step < C:
                        pe.wait_ge(f.silu_done, 2 * C * i + (C + step + 1))
                    elif step < 2 * C:
                        pe.wait_ge(f.mult_done, 2 * C * i + (step + 1))
                    else:
                        pe.wait_ge(f.acc_done, KT * C * i + (step + 1))
                    w = slice(m * P, (m + 1) * P)
                    for j, s in enumerate((s4, s5)):
                        mm = mm3(pe, ps[:, b, 0:size], w_hi[:, s, w], w_lo[:, s, w],
                                 g_hi[:, j, start:start + size], g_lo[:, j, start:start + size], j == 0, j == 1)
                    mm.then_inc(f.down_done, 1)

                def body(i, mod, last=False, first=False):
                    for u in range(4):
                        s = ring(f.u0 + u) % SLOTS
                        pe.wait_ge(lo_done, UP_UNITS * i + (f.u0 + u + 1 + LO_BIAS))
                        for c, (start, size, _) in enumerate(f.chunks):
                            b = (u % 2) * C + c
                            if u < 2:
                                pe.wait_ge(f.acc_done, KT * C * i + (b + 1))
                            elif u == 2:
                                pe.wait_ge(f.silu_done, 2 * C * i + (c + 1))
                            else:
                                pe.wait_ge(f.mult_done, 2 * C * i + (c + 1))
                            for k in range(KT):
                                if first and (u, c, k) == (0, 0, 2):
                                    sum_partitions(n, 1)
                                elif first and (u, c, k) == (0, 1, 0):
                                    spread(n, 1)
                                if u == 0:
                                    pe.wait_ge(n.lo, n.tile_at[c, k] + 1)
                                w = slice(k * P, (k + 1) * P)
                                mm = mm3(pe, ps[:, b, 0:size], w_hi[:, s, w], w_lo[:, s, w],
                                         x_hi[:, k, start:start + size], x_lo[:, k, start:start + size], k == 0, k == KT - 1)
                            mm.then_inc(f.up_done, 1)
                    if mod:
                        pe.wait_ge(mod_chain, KT * i + (KT + 2))
                        pe.wait_ge(mod_ready, i + PRE)
                        for n_ in range(KT):
                            for which in range(mod):
                                acc = mod_acc_ctx if which else mod_acc_lat
                                mm = pe.matmul(ps[:, 6, 2 * n_ + which:2 * n_ + which + 1], acc[:, n_ * P:(n_ + 1) * P],
                                               ones[:, 0:1], start=True, stop=True)
                        mm.then_inc(mod_mm, 1)
                    pe.wait_ge(lo_done, UP_UNITS * i + (f.u0 + 6 + LO_BIAS))
                    if not last:
                        for c in range(C):
                            for m in range(KT):
                                down(i, c, m)
                        return
                    for what, c, m in last_pass(C):
                        if what == "d":
                            down(i, c, m)
                        elif what == "s":
                            sum_partitions(behind, c)
                        elif what == "f":
                            spread(behind, c)

                if n.tag == "b":
                    body(0, 0, first=True)
                for first, end, mod in ((1, GROUPS - 1, 0),) if n.tag == "b" else f.spans:
                    with pe.Fori(first, end) as i:
                        body(i, mod)
                body(GROUPS - 1, 0, last=True)

            pe.wait_ge(ones_set, 1)
            pe.wait_ge(cond_ready, 1)
            n_ = NORM["a"]
            mod_group(0, range(4))
            turn_mods(0)
            for c in range(2):
                sum_partitions(n_, c)
            mod_group(1, range(1))
            for c in range(2):
                spread(n_, c)
            mod_group(1, range(1, 4))
            mod_group(2, range(2))
            turn_mods(1)
            mod_group(2, range(2, 4))
            sum_partitions(n_, 2)
            mod_group(3, range(2))
            turn_mods(2)
            mod_group(3, range(2, 4))
            turn_mods(3)
            spread(n_, 2)
            ffn(FFN[0], NORM["a"], NORM["m"])

            def banks_free(kind, i):
                for who, count in order[kind, i][3]:
                    wait_copied(pe, who, count)

            n_ = NORM["m"]
            sum_partitions(n_, 1)
            for c, u in [(c, u) for c in range(2) for u in range(3)] + [(c, 3) for c in range(2)]:
                U = U_MIX + u
                s = ring(U) % SLOTS
                pe.wait_ge(lo_done, U + 1 + LO_BIAS)
                if (c, u) == (0, 0):
                    pe.wait_ge(FFN[0].acc_done, 2 * 3 + KT * 3 * GROUPS)
                elif (c, u) == (1, 0):
                    pe.wait_ge(n_.t, KT)
                    pe.wait_ge(n_.keep, 2)
                for kk in range(2):
                    k = 2 * u + kk
                    pe.wait_ge(n_.lo, n_.tile_at[c, k] + 1)
                    for fg in range(FG):
                        w = slice(kk * HALF + fg * FC, kk * HALF + (fg + 1) * FC)
                        mm = mm3(pe, ps[:, c * FG + fg, :], w_hi[:, s, w], w_lo[:, s, w],
                                 x_hi[:, k, c * HALF:(c + 1) * HALF], x_lo[:, k, c * HALF:(c + 1) * HALF], k == 0, k == KT - 1)
                        if k == KT - 1:
                            mm.then_inc(mix_mm, 1)
                if c == 1 and u < 3:
                    mm.then_inc(mix_unit, 1)
                if (c, u) == (0, 0):
                    spread(n_, 1)
                    sum_partitions(n_, 2)
                elif (c, u) == (0, 1):
                    spread(n_, 2)
            for g, (name, _) in enumerate(MIX_GROUPS):
                for u in range(4 if g else 0):
                    U = U_MIX + 4 * g + u
                    s = ring(U) % SLOTS
                    pe.wait_ge(lo_done, U + 1 + LO_BIAS)
                    for kk in range(2):
                        k = 2 * u + kk
                        n_out = NCC if name in ("kc", "vc") else 8
                        if g == 1 and k == 0:
                            pe.wait_ge(NORM["m"].lo, KT * 3)
                        for n in range(n_out):
                            if k == 0:
                                banks_free(name, n)
                            w0 = kk * HALF
                            tok = slice(n * P, (n + 1) * P) if n_out == 8 else slice(SEQ + n * P, SEQ + (n + 1) * P)
                            w = slice(w0 + H * DK, w0 + HALF) if name == "kc" else slice(w0, w0 + HALF)
                            bank = n + (NCC if name == "vc" else 0)
                            mm = mm3(pe, ps[:, bank, 0:w.stop - w.start], x_hi[:, k, tok], x_lo[:, k, tok],
                                     w_hi[:, s, w], w_lo[:, s, w], k == 0, k == KT - 1)
                            if k == KT - 1:
                                mm.then_inc(mix_mm, 1)
                    if u < 3:
                        mm.then_inc(mix_unit, 1)
                if name == "vc":
                    for kind_i in range(8):
                        _, who, count, _ = order["fu", kind_i]
                        wait_copied(pe, who, count)
                    for n in range(NCH):
                        banks_free("ab", n)
                        for fg in range(FG):
                            mm = pe.matmul(ps[:, 4 + 2 * (n % 2) + fg // 2, (fg % 2) * 2 * FC:(fg % 2 + 1) * 2 * FC],
                                           ut[:, fg, n * P:(n + 1) * P], chan[:, :], start=True, stop=True)
                        mm.then_inc(mix_mm, 1)

            pe.wait_ge(mix_act, order["gb", 1][2])
            pe.wait_ge(mix_dve, MIX_D)
            for n, st in enumerate(STATES):
                pe.wait_ge(kz_done, n + 1)
                if n >= 2:
                    pe.wait_ge(u_ev, n - 1)
                for hd in range(H):
                    mm = pe.matmul(ps[:, n % 2, hd * DV:(hd + 1) * DV], kz[:, n % 2, hd, :],
                                   v[:, (NCH + st) if st < NCC else st - NCC, hd * DV:(hd + 1) * DV], start=True, stop=True)
                mm.then_inc(u_mm, 1)

            def turn(i):
                pe.wait_ge(qq_done, i + 1)
                if i:
                    pe.wait_ge(t_act, i)
                for hd in range(H):
                    pe.transpose(ps[:, 0, hd * CH:(hd + 1) * CH], qq[:, hd, :, :].rearrange("p s c -> p (s c)"), ident[:, :])
                for hd in range(H):
                    mm = pe.transpose(ps[0:DK, 1, hd * CH:(hd + 1) * CH], qk[:, i, (H + hd) * DK:(H + hd + 1) * DK], ident[:, :])
                mm.then_inc(t_mm, 1)

            def turn_y(i):
                pe.wait_ge(y_done, i + 1)
                if i:
                    pe.wait_ge(ylo_done, i)
                for hd in range(H):
                    mm = pe.transpose(ps[:, 3, hd * DV:(hd + 1) * DV], y[:, i % 2, hd, :], ident[:, :])
                mm.then_inc(y_mm, 1)

            pe.wait_ge(rope_done, NCH)
            pe.wait_ge(u_ev, NCC + NCH)
            pe.wait_ge(mix_act, MIX_A)
            turn(0)
            for i in range(NCH):
                pe.wait_ge(t_act, i + 1)
                if i:
                    pe.wait_ge(p_done, i)
                for hd in range(H):
                    mm = pe.matmul(ps[:, 2, hd * CH:(hd + 1) * CH], kT[0:DK, hd, :], qT[0:DK, hd, :], start=True, stop=True)
                mm.then_inc(s_mm, 1)
                if i < NCH - 1:
                    turn(i + 1)
                pe.wait_ge(p_done, i + 1)
                pe.wait_ge(t_dve, i + 1)
                if i >= 2:
                    pe.wait_ge(on_done, i - 1)
                elif i == 0:
                    pe.wait_ge(rec_done, NCH)
                for d in range(2):
                    rows = slice(d * DK, (d + 1) * DK)
                    prev = 1 + (i if d == 0 else NCH - 1 - i)
                    for hd in range(H):
                        o_ = ps[:, 4 + 2 * (i % 2) + d, hd * DV:(hd + 1) * DV]
                        pe.matmul(o_, pr[:, d, hd, :], v[:, i, hd * DV:(hd + 1) * DV], start=True, stop=False)
                        mm = pe.matmul(o_, qxT[rows, i % 2, hd, :], ust[rows, prev, hd * DV:(hd + 1) * DV], start=False, stop=True)
                mm.then_inc(o_mm, 1)
                if i >= 2:
                    turn_y(i - 2)

            pe.wait_ge(lo_done, U_DFT + 4 + LO_BIAS)
            pe.wait_ge(on_done, NCH - 1)
            for n in range(4 * FG):
                s = BRANCHES[n % 4]
                pe.wait_ge(zlo_done, n + 1)
                if n >= 4:
                    pe.wait_ge(flo_done, n - 3)
                for ta in range(4):
                    w = z_hi[:, n % 4, ta // 2, ta % 2, :], z_lo[:, n % 4, ta // 2, ta % 2, :]
                    cols = slice(s * NQ, (s + 1) * NQ)
                    mm = mm3(pe, ps[:, FOUR_BANKS[n % 4], 0:NQ], *w, df_hi[:, ta, cols], df_lo[ta][:, cols], ta == 0, ta == 3)
                mm.then_inc(f_mm, 1)
                if n in (1, 5):
                    turn_y(NCH - 2 + n // 4)

            pe.wait_ge(flo_done, 4 * FG)
            pe.wait_ge(ylo_done, NCH)
            for n, (m, c) in enumerate(OUT_ORDER):
                U = U_OUT + m
                s = ring(U) % SLOTS
                pe.wait_ge(lo_done, U + 1 + LO_BIAS)
                if n >= 4:
                    pe.wait_ge(out_acc, n - 3)
                cols = slice(c * HALF, (c + 1) * HALF)
                for k in range(KT):
                    xh, xl = (ret_hi[:, k, cols], ret_lo[:, k, cols]) if k < H else (four_hi[:, k - H, cols], four_lo[k - H][:, cols])
                    w = slice(k * P, (k + 1) * P)
                    mm = mm3(pe, ps[:, n % 4, :], out_hi[:, s, w], out_lo[:, s, w], xh, xl, k == 0, k == KT - 1)
                mm.then_inc(out_mm, 1)
                if n == len(OUT_ORDER) - SLOTS:
                    sum_partitions(NORM["b"], 0)
                elif n == len(OUT_ORDER) - 2:
                    spread(NORM["b"], 0)
            ffn(FFN[1], NORM["b"], NORM["f"])
            sum_partitions(NORM["f"], 1)
            spread(NORM["f"], 1)

        @block.scalar
        def _(act):
            def hi(u, i=None):
                s = u % SLOTS
                landed = 16 * (u // SLOTS + 1)
                act.wait_ge(stage_in[s], landed if i is None else i * (16 * UP_UNITS // SLOTS) + landed)
                act.activation(halves(u)[0], stage[:, s, :], ACT.Copy).then_inc(hi_done, 1)

            def square(n, c, m):
                if m == 0:
                    dst = n.total[c][:, :]
                else:
                    r = n.add_at[c, m]
                    if r >= 2:
                        act.wait_ge(n.add[n.adder[c]], r - 1)
                    dst = n.square[n.adder[c]][r % 2][:, 0:n.chunks[c][1]]
                act.activation(dst, h_of(m, n.chunks[c]), ACT.Square).then_inc(n.sq, 1)

            def root(n, c):
                act.wait_ge(n.var, c + 1)
                r = rt[:, c, 0:n.chunks[c][1] // P]
                act.activation(r, r, ACT.Sqrt).then_inc(n.root, 1)

            def normed_hi(n, c, m):
                if n.shift is None:
                    return
                q = n.tile_at[c, m]
                start, size, which = n.chunks[c]
                act.wait_ge(n.t, q + 1)
                act.activation(x_hi[:, m, start:start + size], n.scaled[q % 3][:, 0:size], ACT.Identity,
                               bias=mods[:, n.shift, m, which:which + 1]).then_inc(n.hi, 1)

            def ffn(f, behind):
                C = f.C
                end = f.u0 + UP_UNITS * GROUPS == U_END

                def body(i, last):
                    for u in range(4):
                        for c, (start, size, _) in enumerate(f.chunks):
                            if u % 2 == 0:
                                act.wait_ge(f.up_done, 4 * C * i + (u * C + c + 1))
                                if u == 2:
                                    act.wait_ge(f.mult_done, 2 * C * i + (c + 1))
                                act.activation(silu_a[c][:, :], ps[:, c, 0:size], ACT.Silu).then_inc(f.silu_done, 1)
                            else:
                                act.wait_ge(f.mult_done, 2 * C * i + ((u // 2) * C + c + 1))
                                act.activation(g_hi[:, u // 2, start:start + size], prod[c][:, :], ACT.Copy)\
                                    .then_inc(f.ghi_done, 1)
                        if last and end and u + SLOTS >= UP_UNITS:
                            continue
                        act.wait_ge(f.up_done, 4 * C * i + (u + 1) * C)
                        hi(f.u0 + u + SLOTS, i)
                    if last:
                        for what, c, m in last_pass(C) + behind_pass(C):
                            if what == "d":
                                act.wait_ge(f.acc_done, KT * C * i + (2 * C + c * KT + m + 1))
                                square(behind, c, m)
                            elif what == "s":
                                root(behind, c)
                            elif what == "n":
                                normed_hi(behind, c, m)
                            if (what, c, m) == ("n", 0, 4) and not end:
                                act.wait_ge(f.down_done, KT * C * i + KT * C)
                                hi(f.u0 + 4 + SLOTS, i)
                                hi(f.u0 + 5 + SLOTS, i)
                        return
                    act.wait_ge(f.down_done, KT * C * i + KT * C)
                    hi(f.u0 + 4 + SLOTS, i)
                    hi(f.u0 + 5 + SLOTS, i)

                with act.Fori(0, GROUPS - 1) as i:
                    body(i, False)
                body(GROUPS - 1, True)

            act.wait_ge(small_in, 16 * 7)
            act.activation(cond[:, :, :], cond[:, :, :], ACT.Silu).then_inc(cond_ready, 1)
            act.wait_ge(dve_step, 1)
            act.activation(zeta[:, :, :], zeta[:, :, :], ACT.Exp).then_inc(act_prep, 1)
            for d in range(2):
                rows = slice(d * DK, (d + 1) * DK)
                act.activation(dcs[rows, :], lg[rows, d, :], ACT.Exp, scale=float(CH)).then_inc(act_prep, 1)

            n = NORM["a"]
            for c, m in n.squares:
                if c == 2:
                    continue
                if c == 0 and m % 2 == 0:
                    act.wait_ge(x_in[m // 2], 16)
                square(n, c, m)
            root(n, 0)
            root(n, 1)
            for g, group in enumerate(n.groups):
                if g == 1:
                    act.wait_ge(ctx_in, 16)
                    for m in range(KT):
                        square(n, 2, m)
                if g == PRE - 1:
                    act.wait_ge(mod_row_mm, 3)
                    hi(0)
                    root(n, 2)
                for c, m in group:
                    normed_hi(n, c, m)
            act.wait_ge(mod_row_mm, 4)
            hi(1)
            hi(2)
            ffn(FFN[0], NORM["m"])

            def copy_out(kind, i):
                mm, who, _, _ = order[kind, i]
                if who != "a":
                    return
                act.wait_ge(mix_mm, mm)
                if kind == "fu":
                    act.activation(ut[:, i % FG, (i // FG) * HALF:(i // FG + 1) * HALF], ps[:, i, :], ACT.Copy).then_inc(mix_act, 1)
                elif kind == "kc":
                    act.activation(kc[:, i, :], ps[:, i, 0:H * DK], ACT.Copy, scale=DK ** -0.5).then_inc(mix_act, 1)
                elif kind == "vc":
                    act.activation(v[:, NCH + i, :], ps[:, 2 + i, :], ACT.Copy).then_inc(mix_act, 1)
                elif kind == "ab":
                    if i >= 4:
                        act.wait_ge(ab_spill[i % 4], 16 * (i // 4))
                    b = 4 + 2 * (i % 2)
                    act.activation(ab_out[:, i % 4, :].rearrange("p (b c) -> p b c", b=2), ps[:, b:b + 2, :], ACT.Copy).then_inc(mix_act, 1)
                    act.wait_ge(mix_act, order[kind, i][2])
                    act.dma_start(ab_dram[i], ab_out[:, i % 4, :]).then_inc(ab_spill[i % 4], 16)
                elif kind == "qk":
                    if i == 1:
                        for n in range(4):
                            act.wait_ge(ab_spill[n], 32)
                    act.activation(qk[:, i, 0:H * DK], ps[:, i, 0:H * DK], ACT.Copy)
                    act.activation(qk[:, i, H * DK:HALF], ps[:, i, H * DK:HALF], ACT.Copy, scale=DK ** -0.5).then_inc(mix_act, 1)
                elif kind == "v":
                    act.activation(v[:, i, :], ps[:, i, :], ACT.Copy).then_inc(mix_act, 1)
                else:
                    n = i + (NCH if kind == "gb" else 0)
                    if n >= 6:
                        act.wait_ge(gate_spill[n % 6], 16 * (n // 6))
                    gb = gbuf_a[:, n % 6, :] if n % 6 < 2 else gbuf_b[:, n % 6 - 2, :]
                    act.activation(gb, ps[:, i, :], ACT.Silu).then_inc(mix_act, 1)
                    act.wait_ge(mix_act, order[kind, i][2])
                    act.dma_start(gate_dram[i, :, n // NCH, :], gb).then_inc(gate_spill[n % 6], 16)

            for g, (name, _) in enumerate(MIX_GROUPS):
                n_out = NCC if name in ("kc", "vc") else 8
                U = U_MIX + 4 * g + SLOTS
                for u in range(3):
                    if U + u < U_DFT:
                        act.wait_ge(mix_unit, 3 * g + u + 1)
                        hi(U + u)
                if name == "gb":
                    act.wait_ge(mask_in, 16)
                    for d in range(2):
                        rows = slice(d * DK, (d + 1) * DK)
                        for hd in range(H):
                            act.activation(xiT[rows, hd, :], masks[rows, 4, :], ACT.Exp, scale=lg[rows, d, hd:hd + 1]).then_inc(xi_done, 1)
                for i in range(n_out):
                    copy_out(name, i)
                if U + 3 < U_DFT:
                    act.wait_ge(mix_mm, order[name, n_out - 1][0])
                    hi(U + 3)
                if name == "vc":
                    for i in range(NCH):
                        copy_out("ab", i)

            for n, st in enumerate(STATES):
                fw = st
                bw = NCC - 1 - st if st < NCC else NCC + NCH - 1 - (st - NCC)
                act.wait_ge(u_mm, n + 1)
                act.activation(ust[0:DK, fw, :], ps[0:DK, n % 2, :], ACT.Copy)
                act.activation(ust[DK:P, bw, :], ps[DK:P, n % 2, :], ACT.Copy).then_inc(u_ev, 1)
                if n == 1:
                    for n_ in range(6):
                        act.wait_ge(gate_spill[n_], 16 * len(range(n_, 2 * NCH, 6)))
                if n >= 2:
                    d, hd = divmod(n - 2, H)
                    act.activation(dm[:, d, hd, :], masks[:, d, :], ACT.Exp, scale=lg[:, d, hd:hd + 1]).then_inc(dm_exp, 1)

            def turned(i):
                act.wait_ge(t_mm, i + 1)
                if i:
                    act.wait_ge(t_dve, i)
                act.activation(qT[:, :, :], ps[:, 0, :].rearrange("p (h c) -> p h c", h=H), ACT.Copy).then_inc(q_turned, 1)
                act.activation(kT[0:DK, :, :], ps[0:DK, 1, :].rearrange("p (h c) -> p h c", h=H), ACT.Copy).then_inc(t_act, 1)

            def normalise(i):
                act.wait_ge(var_done, i + 1)
                act.activation(rs[:, :], rs[:, :], ACT.Sqrt).then_inc(root_done, 1)
                act.wait_ge(rs_done, i + 1)
                if i >= 2:
                    act.wait_ge(y_done, i - 1)
                for d in range(2):
                    for hd in range(H):
                        n = d * H + hd
                        a = act.activation(on[:, i % 2, d, hd, :], ps[:, 4 + 2 * (i % 2) + d, hd * DV:(hd + 1) * DV], ACT.Identity,
                                           scale=rs[:, n:n + 1], bias=nmr[:, n:n + 1])
                a.then_inc(on_done, 1)

            def y_hi(i):
                act.wait_ge(y_mm, i + 1)
                act.activation(ret_hi[:, :, i * CH:(i + 1) * CH], ps[:, 3, :].rearrange("p (h c) -> p h c", h=H), ACT.Copy)\
                    .then_inc(yhi_done, 1)

            turned(0)
            for i in range(NCH):
                if i < NCH - 1:
                    turned(i + 1)
                if i >= 1:
                    normalise(i - 1)
                if i >= 2:
                    y_hi(i - 2)
                if i < 4:
                    hi(U_DFT + i)

            def z_hi_of(n):
                act.wait_ge(z_done, n + 1)
                if n >= 4:
                    act.wait_ge(f_mm, n - 3)
                else:
                    act.wait_ge(o_mm, NCH)
                act.activation(z_hi[:, n % 4, :, :, :], z_of(n), ACT.Copy).then_inc(zhi_done, 1)

            for n in range(4):
                z_hi_of(n)
            normalise(NCH - 1)
            for n in range(4 * FG):
                act.wait_ge(f_mm, n + 1)
                act.activation(four_hi[:, n // 4, BRANCHES[n % 4]:SEQ:4], ps[:, FOUR_BANKS[n % 4], 0:NQ], ACT.Copy).then_inc(fhi_done, 1)
                if n < 4 * (FG - 1):
                    z_hi_of(n + 4)
                if n in (1, 5):
                    y_hi(NCH - 2 + n // 4)
                if n in (6, 8, 10):
                    hi(U_OUT + (n - 6) // 2)
            n = NORM["b"]
            for at, (m, c) in enumerate(OUT_ORDER):
                if at in UNIT_AT:
                    if at < 2 * (KT - SLOTS):
                        act.wait_ge(out_mm, at + 1)
                    hi(UNIT_AT[at])
                act.wait_ge(out_acc, at + 1)
                square(n, c, m)
                if at == len(OUT_ORDER) - SLOTS:
                    root(n, 0)
            for c in range(2):
                for m in range(KT):
                    if (c, m) == (0, 4):
                        root(n, 1)
                    normed_hi(n, c, m)
            ffn(FFN[1], NORM["f"])

        @block.gpsimd
        def _(pool):
            pool.memset(ones[:, :], 1.0).then_inc(ones_set, 1)

            def lo(u, i=None):
                s = u % SLOTS
                pool.wait_ge(hi_done, u + 1 if i is None else UP_UNITS * i + (u + 1))
                a, b = halves(u)
                pool.tensor_tensor(b, stage[:, s, :], a.bitcast(F32), ALU.subtract).then_inc(lo_done, 1)

            def add_square(n, c, m):
                if m == 0 or n.adder[c]:
                    return
                r = n.add_at[c, m]
                pool.wait_ge(n.sq, n.at[c, m] + 1)
                if r:
                    pool.wait_ge(n.add[0], r)
                pool.tensor_tensor(n.total[c][:, :], n.total[c][:, :], n.square[0][r % 2][:, 0:n.chunks[c][1]], ALU.add).then_inc(n.add[0], 1)

            def ffn(f, behind):
                end = f.u0 + UP_UNITS * GROUPS == U_END
                with pool.Fori(0, GROUPS - 1) as i:
                    for u in range(UP_UNITS):
                        lo(f.u0 + u + SLOTS, i)
                for u in range(SLOTS if end else 4):
                    lo(f.u0 + u + SLOTS, GROUPS - 1)
                for c in range(f.C):
                    for m in range(KT):
                        add_square(behind, c, m)
                if not end:
                    for u in (4, 5):
                        lo(f.u0 + u + SLOTS, GROUPS - 1)

            for c, m in NORM["a"].squares:
                add_square(NORM["a"], c, m)
            for u in range(SLOTS):
                lo(u)
            ffn(FFN[0], NORM["m"])
            for u in range(U_MIX + SLOTS, U_DFT):
                lo(u)
            def gate(i):
                pool.wait_ge(on_done, i + 1)
                pool.wait_ge(gate_in[i % 2], 16 * (i // 2 + 1))
                o2 = on[:, i % 2, :, :, :].rearrange("p d h c -> p d (h c)")
                pool.tensor_tensor(o2, o2, gin[:, i % 2, :, :], ALU.mult).then_inc(gated, 1)
                pool.wait_ge(gated, i + 1)
                if i >= 2:
                    pool.wait_ge(y_mm, i - 1)
                pool.tensor_tensor(y[:, i % 2, :, :], on[:, i % 2, 0, :, :], on[:, i % 2, 1, :, :], ALU.add).then_inc(y_done, 1)

            for i in range(NCH - 1):
                gate(i)
                if i < 2:
                    lo(U_DFT + i)
                elif i == 5:
                    pool.wait_ge(t_mm, NCH)
                    lo(U_DFT + 2)
                    lo(U_DFT + 3)
            for n in range(4 * FG):
                pool.wait_ge(zhi_done, n + 1)
                pool.tensor_tensor(z_lo[:, n % 4, :, :, :], z_of(n), z_hi[:, n % 4, :, :, :].bitcast(F32), ALU.subtract)\
                    .then_inc(zlo_done, 1)
                if n == 3:
                    gate(NCH - 1)
                if n in (11, 13, 15):
                    lo(U_OUT + (n - 11) // 2)
            for at, (m, c) in enumerate(OUT_ORDER):
                if at in UNIT_AT:
                    lo(UNIT_AT[at])
                add_square(NORM["b"], c, m)
            ffn(FFN[1], NORM["f"])

        @block.vector
        def _(dve):
            steps = [0]

            def step(ins):
                steps[0] += 1
                ins.then_inc(dve_step, 1)
                dve.wait_ge(dve_step, steps[0])

            def mods_add_bias(i, bank, conds=2):
                return dve.tensor_tensor(mods[:, bass.ds(i, 1), :, 0:conds].rearrange("p o k w -> p (o k) w"),
                                         ps[:, bank, 0:2 * KT].rearrange("p (k w) -> p k w", w=2)[:, :, 0:conds],
                                         b_mod[:, bass.ds(i * KT, KT)].unsqueeze(2).to_broadcast([P, KT, conds]), ALU.add)

            def columns_of(n):
                j = "amb".index(n.tag)
                conds = 1 + n.chunks[-1][2]
                step(dve.scalar_tensor_tensor(acol[:, j, :, 0:conds], mods[:, n.scale, :, 0:conds], 1.0,
                                              gains[:, n.gain, :].unsqueeze(2).to_broadcast([P, KT, conds]), ALU.add, ALU.mult))

            def rsqrt(n, c):
                T = n.chunks[c][1] // P
                r = rt[:, c, 0:T]
                dve.wait_ge(n.stat, c + 1)
                dve.tensor_scalar(r, ps[:, n.bank[c], 0:T], 1.0 / D, EPS, ALU.mult, ALU.add).then_inc(n.var, 1)
                dve.wait_ge(n.root, c + 1)
                dve.reciprocal(r, r).then_inc(n.rec, 1)
                dve.wait_ge(n.rec, c + 1)
                dve.tensor_tensor(n.total[c][:, :].rearrange("p (q t) -> p q t", q=T), ident[:, :].unsqueeze(1).to_broadcast([P, T, P]),
                                  r.unsqueeze(2).to_broadcast([P, T, P]), ALU.mult).then_inc(n.diag, 1)

            def normed_lo(n, q):
                c, m = n.tiles[q]
                start, size, which = n.chunks[c]
                dve.wait_ge(n.hi, q + 1)
                x = slice(start, start + size)
                dve.scalar_tensor_tensor(x_lo[:, m, x], n.scaled[q % 3][:, 0:size], mods[:, n.shift, m, which:which + 1],
                                         x_hi[:, m, x].bitcast(F32), ALU.add, ALU.subtract).then_inc(n.lo, 1)

            def keep(n, c):
                dve.wait_ge(n.spread, c + 1)
                dve.tensor_copy(n.total[c][:, :], ps[:, n.bank[c], 0:n.chunks[c][1]]).then_inc(n.keep, 1)

            def normed(n, c, m):
                chunk = n.chunks[c]
                if m == 0 and c not in n.kept:
                    dve.wait_ge(n.spread, c + 1)
                elif m == 0:
                    dve.wait_ge(n.keep, n.kept.index(c) + 1)
                factors = n.total[c][:, :] if c in n.kept else ps[:, n.bank[c], 0:chunk[1]]
                if n.shift is None:
                    dve.scalar_tensor_tensor(h_of(m, chunk), h_of(m, chunk), gains[:, n.gain, m:m + 1], factors, ALU.mult, ALU.mult)\
                        .then_inc(fin_done, 1)
                    return
                q = n.tile_at[c, m]
                if q >= 3:
                    dve.wait_ge(n.lo, q - 2)
                j = "amb".index(n.tag)
                dve.scalar_tensor_tensor(n.scaled[q % 3][:, 0:chunk[1]], h_of(m, chunk), acol[:, j, m, chunk[2]:chunk[2] + 1],
                                         factors, ALU.mult, ALU.mult).then_inc(n.t, 1)
                caught = {x + d for x in n.catch_up for d in (1, 2)}
                if q >= 2 and q not in caught:
                    normed_lo(n, q - 2)
                if q in n.catch_up:
                    normed_lo(n, q - 1)
                    normed_lo(n, q)

            def ffn(f, behind):
                C = f.C

                def mod_rows(i, k, mod):
                    dve.wait_ge(mod_in[k % 2], 16 * 4 * i + 16 * (k // 2 + 1))
                    if k:
                        dve.wait_ge(mod_chain, KT * i + (k + 2))
                    for which in range(mod):
                        acc = mod_acc_ctx if which else mod_acc_lat
                        w = mod_stage[:, k % 2, :]
                        s_ = cond[:, k, which:which + 1]
                        if k == 0:
                            a = dve.tensor_scalar(acc[:, :], w, s_, None, ALU.mult)
                        else:
                            a = dve.scalar_tensor_tensor(acc[:, :], w, s_, acc[:, :], ALU.mult, ALU.add)
                    a.then_inc(mod_chain, 1)

                def acc_step(i, c, m):
                    s = c * KT + m
                    chunk = f.chunks[c]
                    dve.wait_ge(f.down_done, KT * C * i + (s + 1))
                    hh = h_of(m, chunk)
                    dve.scalar_tensor_tensor(hh, ps[:, s % (2 * C), 0:chunk[1]], ghalf[:, f.gate, m, chunk[2]:chunk[2] + 1], hh,
                                             ALU.mult, ALU.add).then_inc(f.acc_done, 1)

                def body(i, mod, last=False):
                    for j in range(2):
                        def product(c):
                            start, size, _ = f.chunks[c]
                            dve.wait_ge(f.up_done, 4 * C * i + ((2 * j + 1) * C + c + 1))
                            dve.wait_ge(f.silu_done, 2 * C * i + (j * C + c + 1))
                            dve.wait_ge(f.glo_done, 2 * C * i + (j * C + c + 1))
                            dve.tensor_tensor(prod[c][:, :], silu_a[c][:, :], ps[:, C + c, 0:size], ALU.mult)\
                                .then_inc(f.mult_done, 1)

                        def rest(c):
                            start, size, _ = f.chunks[c]
                            dve.wait_ge(f.ghi_done, 2 * C * i + (j * C + c + 1))
                            g = slice(start, start + size)
                            dve.tensor_tensor(g_lo[:, j, g], prod[c][:, :], g_hi[:, j, g].bitcast(F32), ALU.subtract)\
                                .then_inc(f.glo_done, 1)

                        for c in range(C):
                            product(c)
                            rest(c)
                        if mod and j == 0:
                            for k in range(KT):
                                mod_rows(i, k, mod)
                    if mod:
                        dve.wait_ge(mod_mm, i + (PRE + 1))
                        mods_add_bias(i + 2, 6, mod).then_inc(mod_ready, 1)
                        dve.wait_ge(mod_ready, i + (PRE + 1))
                        dve.tensor_scalar(ghalf[:, 0, :, :], mods[:, 2, :, :], 0.5, None, ALU.mult).then_inc(gate_ready, 1)
                        dve.wait_ge(gate_ready, i + 1)
                    if not last:
                        for c in range(C):
                            for m in range(KT):
                                acc_step(i, c, m)
                        return
                    if behind.shift is not None:
                        columns_of(behind)
                    for what, c, m in last_pass(C) + behind_pass(C):
                        if what == "d":
                            acc_step(i, c, m)
                        elif what == "s":
                            rsqrt(behind, c)
                        elif what == "k":
                            keep(behind, c)
                        elif what == "n":
                            normed(behind, c, m)

                for first, end, mod in f.spans:
                    with dve.Fori(first, end) as i:
                        body(i, mod)
                body(GROUPS - 1, 0, last=True)

            dve.memset(mv[:, 0, 0:1], 0.0).then_inc(lo_done, LO_BIAS)
            dve.memset(mv[:, 1, 0:1], 0.0).then_inc(mod_chain, 2)
            dve.memset(mv[:, 2, 0:1], 0.0).then_inc(FFN[0].acc_done, 2 * 3)
            dve.memset(mv[:, 3, 0:1], 0.0).then_inc(FFN[1].acc_done, 2 * 2)
            dve.memset(mv[:, 4, 0:1], 0.0).then_inc(FFN[0].glo_done, 3)
            dve.memset(mv[:, 5, 0:1], 0.0).then_inc(FFN[1].glo_done, 2)

            dve.wait_ge(small_in, 16 * 7)
            for d in range(2):
                zz = dve.tensor_scalar(zeta[:, d, :], lg[:, d, :], pvec[:, d:d + 1], None, ALU.mult)
            step(zz)
            n = NORM["a"]
            def flatten(g):
                dve.wait_ge(mod_row_mm, g + 1)
                dve.tensor_copy(mod_flat[g % 2][0:2, :], ps[0:2, g % 2, :]).then_inc(mod_flat_done, 1)

            def mod_columns(g):
                two = slice(2 * g, 2 * g + 2)
                dve.wait_ge(mod_mm, g + 1)
                dve.tensor_tensor(mods[:, 0:2, two, :], ps[:, 2 + g % 2, 0:8].rearrange("p (m i w) -> p i m w", m=2, i=2),
                                  b_mod[:, 0:2 * KT].rearrange("p (i m) -> p i m", i=2)[:, :, two].unsqueeze(3).to_broadcast([P, 2, 2, 2]),
                                  ALU.add).then_inc(mod_ready, 1)
                dve.wait_ge(mod_ready, g + 1)
                step(dve.scalar_tensor_tensor(acol[:, 0, two, :], mods[:, 1, two, :], 1.0,
                                              gains[:, 0, two].unsqueeze(2).to_broadcast([P, 2, 2]), ALU.add, ALU.mult))

            for m in range(1, KT):
                if m == 4:
                    flatten(0)
                dve.wait_ge(n.sq, n.at[1, m] + 1)
                if m > 1:
                    dve.wait_ge(n.add[1], m - 1)
                dve.tensor_tensor(n.total[1][:, :], n.total[1][:, :], n.square[1][(m - 1) % 2][:, :], ALU.add).then_inc(n.add[1], 1)
            rsqrt(n, 0)
            rsqrt(n, 1)
            for g, group in enumerate(n.groups):
                if g == PRE - 1:
                    rsqrt(n, 2)
                if g < PRE:
                    if g:
                        flatten(g)
                    mod_columns(g)
                for c, m in group:
                    normed(n, c, m)
            ffn(FFN[0], NORM["m"])

            def copy_out(kind, i):
                mm, who, _, _ = order[kind, i]
                if who != "d":
                    return
                dve.wait_ge(mix_mm, mm)
                if kind == "fu":
                    dve.tensor_copy(ut[:, i % FG, (i // FG) * HALF:(i // FG + 1) * HALF], ps[:, i, :]).then_inc(mix_dve, 1)
                elif kind == "vc":
                    dve.tensor_copy(v[:, NCH + i, :], ps[:, 2 + i, :]).then_inc(mix_dve, 1)
                elif kind == "qk":
                    if i == 0:
                        for n in range(4):
                            dve.wait_ge(ab_spill[n], 32)
                    dve.tensor_copy(qk[:, i, 0:H * DK], ps[:, i, 0:H * DK])
                    dve.tensor_scalar(qk[:, i, H * DK:HALF], ps[:, i, H * DK:HALF], DK ** -0.5, None, ALU.mult).then_inc(mix_dve, 1)
                elif kind == "v":
                    dve.tensor_copy(v[:, i, :], ps[:, i, :]).then_inc(mix_dve, 1)

            def rotate(i):
                _, who, count, _ = order["qk", i]
                wait_copied(dve, who, count)
                heads = qk[:, i, :].rearrange("p (n s c) -> p n s c", n=2 * H, s=2)
                cos = rope[:, i, 0, :].unsqueeze(1).to_broadcast([P, 2 * H, DK // 2])
                sin = rope[:, i, 1, :].unsqueeze(1).to_broadcast([P, 2 * H, DK // 2])
                dve.tensor_tensor(rtmp[:, 0, :, :], heads[:, :, 1, :], sin, ALU.mult)
                step(dve.tensor_tensor(rtmp[:, 1, :, :], heads[:, :, 0, :], sin, ALU.mult))
                dve.tensor_tensor(heads[:, :, 0, :], heads[:, :, 0, :], cos, ALU.mult)
                step(dve.tensor_tensor(heads[:, :, 1, :], heads[:, :, 1, :], cos, ALU.mult))
                dve.tensor_tensor(heads[:, :, 0, :], heads[:, :, 0, :], rtmp[:, 0, :, :], ALU.subtract)
                dve.tensor_tensor(heads[:, :, 1, :], heads[:, :, 1, :], rtmp[:, 1, :, :], ALU.add).then_inc(rope_done, 1)
                dve.wait_ge(rope_done, i + 1)

            for g, (name, _) in enumerate(MIX_GROUPS):
                if name in ("gf", "gb"):
                    continue
                for i in range(NCC if name in ("kc", "vc") else 8):
                    copy_out(name, i)
                if name == "qk":
                    dve.wait_ge(rope_in, 16)
                    for i in range(NCH):
                        rotate(i)

            dve.wait_ge(act_prep, 3)
            dve.wait_ge(mix_act, order["kc", NCC - 1][2])
            dve.wait_ge(mix_mm, len(outs))

            def state(j):
                if j:
                    dve.wait_ge(rec_done, j)
                for hd in range(H):
                    e = slice(hd * DV, (hd + 1) * DV)
                    a = dve.scalar_tensor_tensor(ust[:, j + 1, e], ust[:, j, e], dcs[:, hd:hd + 1], ust[:, j + 1, e], ALU.mult, ALU.add)
                a.then_inc(rec_done, 1)

            def twice(i):
                if i:
                    dve.wait_ge(t_mm, i)
                q_ = qk[:, i, 0:H * DK].rearrange("p (h c) -> p h c", h=H)
                dve.tensor_copy(qq[:, :, 0, :], q_)
                dve.tensor_copy(qq[:, :, 1, :], q_).then_inc(qq_done, 1)

            for n, st in enumerate(STATES):
                k = (kc[:, st, :] if st < NCC else qk[:, st - NCC, H * DK:HALF]).rearrange("p (h c) -> p h c", h=H)
                if n >= 2:
                    dve.wait_ge(u_mm, n - 1)
                for d in range(2):
                    kk = dve.tensor_tensor(kz[:, n % 2, :, d * DK:(d + 1) * DK], k,
                                           zeta[:, d, :].unsqueeze(2).to_broadcast([P, H, DK]), ALU.mult)
                kk.then_inc(kz_done, 1)
                if n % 2 and n > 1:
                    dve.wait_ge(u_ev, n - 1)
                    state((n - 3) // 2)
            twice(0)
            for d in range(2):
                dve.wait_ge(dm_exp, H * (d + 1))
                dve.tensor_tensor(dm[:, d, :, :], dm[:, d, :, :], masks[:, 2 + d, :].unsqueeze(1).to_broadcast([P, H, CH]), ALU.mult)\
                    .then_inc(dm_done, 1)
            dve.wait_ge(u_ev, NCC + NCH)
            for j in range(NCH // 2, NCH):
                state(j)

            def turned(i):
                dve.wait_ge(q_turned, i + 1)
                if i >= 2:
                    dve.wait_ge(o_mm, i - 1)
                dve.tensor_tensor(qxT[:, i % 2, :, :], qT[:, :, :], xiT[:, :, :], ALU.mult)\
                    .then_inc(t_dve, 1)

            def decayed(i):
                dve.wait_ge(s_mm, i + 1)
                if i:
                    dve.wait_ge(o_mm, i)
                for d in range(2):
                    a = dve.tensor_tensor(pr[:, d, :, :], ps[:, 2, :].rearrange("p (h c) -> p h c", h=H), dm[:, d, :, :], ALU.mult)
                a.then_inc(p_done, 1)

            def moments(i):
                dve.wait_ge(o_mm, i + 1)
                if i:
                    dve.wait_ge(on_done, i)
                for n in range(2 * H):
                    a = dve.bn_stats(stats[:, n, :], ps[:, 4 + 2 * (i % 2) + n // H, (n % H) * DV:(n % H + 1) * DV])
                step(a)
                for n in range(2 * H):
                    a = dve.bn_aggr(mv[:, n, :], stats[:, n, :])
                step(a)
                dve.tensor_scalar(rs[:, :], mv[:, :, 1], EPS, None, ALU.add).then_inc(var_done, 1)
                dve.wait_ge(root_done, i + 1)
                step(dve.reciprocal(rs[:, :], rs[:, :]))
                dve.scalar_tensor_tensor(nmr[:, :], mv[:, :, 0], -1.0, rs[:, :], ALU.mult, ALU.mult).then_inc(rs_done, 1)

            def y_lo(i):
                dve.wait_ge(yhi_done, i + 1)
                cc = slice(i * CH, (i + 1) * CH)
                dve.tensor_tensor(ret_lo[:, :, cc], ps[:, 3, :].rearrange("p (h c) -> p h c", h=H), ret_hi[:, :, cc].bitcast(F32), ALU.subtract)\
                    .then_inc(ylo_done, 1)

            dve.wait_ge(dm_done, 2)
            dve.wait_ge(xi_done, 2 * H)
            turned(0)
            twice(1)
            for i in range(NCH):
                decayed(i)
                if i >= 1:
                    moments(i - 1)
                if i < NCH - 1:
                    turned(i + 1)
                if i < NCH - 2:
                    twice(i + 2)
                if i >= 3:
                    y_lo(i - 3)
            y_lo(NCH - 3)

            def butterflies(fg):
                x, e = [abuf[fg % 2][:, j, :, :, :] for j in range(4)], [eb[:, :, :, :] for eb in ebuf[fg % 2]]
                dve.wait_ge(ab_in[fg % 2], 16 * (fg // 2 + 1))
                if fg >= 2:
                    dve.wait_ge(zlo_done, 4 * (fg - 1))
                for j in range(2):
                    dve.tensor_tensor(e[j], x[j], x[2 + j], ALU.add)
                for j in range(2):
                    a = dve.tensor_tensor(x[2 + j], x[j], x[2 + j], ALU.subtract)
                step(a)
                dve.tensor_tensor(x[0], e[0], e[1], ALU.add).then_inc(z_done, 1)
                dve.tensor_tensor(x[1], e[0], e[1], ALU.subtract).then_inc(z_done, 1)
                dve.wait_ge(z_done, 4 * fg + 2)
                d0, d1 = x[2], x[3]
                dve.tensor_tensor(e[0][:, :, 0, :], d0[:, :, 0, :], d1[:, :, 1, :], ALU.subtract)
                dve.tensor_tensor(e[0][:, :, 1, :], d0[:, :, 1, :], d1[:, :, 0, :], ALU.add).then_inc(z_done, 1)
                dve.tensor_tensor(e[1][:, :, 0, :], d0[:, :, 0, :], d1[:, :, 1, :], ALU.add)
                dve.tensor_tensor(e[1][:, :, 1, :], d0[:, :, 1, :], d1[:, :, 0, :], ALU.subtract).then_inc(z_done, 1)

            butterflies(0)
            moments(NCH - 1)
            for n in range(4 * FG):
                fg, s = n // 4, BRANCHES[n % 4]
                if n % 4 == 0 and fg < FG - 1:
                    butterflies(fg + 1)
                dve.wait_ge(fhi_done, n + 1)
                dve.tensor_tensor(four_lo[fg][:, s:SEQ:4], ps[:, FOUR_BANKS[n % 4], 0:NQ], four_hi[:, fg, s:SEQ:4].bitcast(F32), ALU.subtract)\
                    .then_inc(flo_done, 1)
                if n in (1, 5):
                    y_lo(NCH - 2 + n // 4)

            step(dve.tensor_scalar(ghalf[:, 1, :, 0:1], mods[:, 8, :, 0:1], 0.5, None, ALU.mult))
            nb = NORM["b"]
            columns_of(nb)
            for n, (m, c) in enumerate(OUT_ORDER):
                dve.wait_ge(out_mm, n + 1)
                hh = h_lat[:, m, c * HALF:(c + 1) * HALF]
                dve.scalar_tensor_tensor(hh, ps[:, n % 4, :], mods[:, 5, m, 0:1], hh, ALU.mult, ALU.add).then_inc(out_acc, 1)
                if n == len(OUT_ORDER) - SLOTS:
                    rsqrt(nb, 0)
            for c in range(2):
                for m in range(KT):
                    if (c, m) == (0, 4):
                        rsqrt(nb, 1)
                    normed(nb, c, m)
            ffn(FFN[1], NORM["f"])


def constants():
    f = np.float32
    pos = np.arange(CH, dtype=np.float64)
    n_freq = DK // 4
    inv = (f(10000.0) ** (-np.arange(n_freq, dtype=f) / f(n_freq))).astype(f)
    tok = np.arange(SEQ)
    ang = np.concatenate([(tok // 64).astype(f)[:, None] * inv, (tok % 64).astype(f)[:, None] * inv], axis=-1).astype(np.float64)
    rope = np.stack([np.cos(ang), np.sin(ang)], 1).astype(f)
    diff = pos[None, :] - pos[:, None]
    xi = np.concatenate([np.tile(pos + 1, (DK, 1)), np.tile(CH - pos, (DK, 1))])
    masks = np.stack([np.maximum(diff, 0), np.maximum(-diff, 0), diff >= 0, diff <= 0, xi], 1).astype(f)
    pvec = np.stack([CH - 1 - pos, pos], 1).astype(f)
    a = 2 * np.pi * np.outer(np.arange(FC), np.arange(FC)) / FC
    chan = np.concatenate([np.cos(a), np.sin(a)], 1) / np.sqrt(SEQ * FC)
    n = np.arange(NQ)[:, None, None]
    k = 4 * np.arange(NQ)[None, None, :] + np.arange(4)[None, :, None]
    a = 2 * np.pi * (n * k % SEQ) / SEQ
    dft = np.stack([np.cos(a), -np.sin(a)], 0).reshape(2, 2, P, 4 * NQ).transpose(1, 0, 2, 3).reshape(4, P, 4 * NQ)
    return {
        "ident": np.eye(P, dtype=f),
        "chan": chan.astype(f),
        "pvec": pvec,
        "rope": np.ascontiguousarray(rope.reshape(NCH, P, 2, DK // 2).transpose(1, 0, 2, 3)),
        "masks": masks,
        "dft": np.ascontiguousarray(dft.astype(f)),
    }


def kernel(x, c, ctx, c_ctx, w_mod, b_mod, norm_ffn1, w13_ffn1, w2_ffn1, norm_mix, w_in, ret_log_decay, w_out,
           norm_ffn2, w13_ffn2, w2_ffn2, norm_final):
    import concourse.bacc as bacc
    from concourse.bass_utils import run_bass_kernel_spmd

    A = lambda a: np.asarray(a)
    tiles = lambda a: A(a).reshape(KT, P, -1)
    columns = lambda a: A(a).reshape(-1, P).T

    def w13(a):
        return A(a)[0].reshape(KT, P, 2, FT, P).transpose(3, 2, 1, 0, 4).reshape(2 * FT, P, UNIT)

    arrays = {
        "x": tiles(A(x)[0].T), "ctx": tiles(A(ctx)[0].T),
        "cond": np.stack([columns(A(c)[0]), columns(c_ctx)], 2),
        "w_mod01": A(w_mod)[0][:, :2 * D].reshape(4, 2, P, 2, PRE, 2, P).transpose(4, 0, 2, 1, 5, 3, 6)\
        .reshape(2 * KT, P, UNIT),
        "w_mod": A(w_mod)[0][:, 2 * D:].reshape(KT, P, NMOD - 2, D).transpose(2, 0, 1, 3).reshape((NMOD - 2) * KT, P, D),
        "b_mod": columns(A(b_mod)[0]),
        "gains": np.stack([columns(A(g).reshape(-1)) for g in (norm_ffn1, norm_mix, norm_ffn2, norm_final)], 1),
        "w13_1": w13(w13_ffn1), "w2_1": A(w2_ffn1)[0].reshape(FT, P, D),
        "w13_2": w13(w13_ffn2), "w2_2": A(w2_ffn2)[0].reshape(FT, P, D),
        "w_in": A(w_in)[0].reshape(4, 2, P, 5, HALF).transpose(3, 0, 2, 1, 4).reshape(5, 4, P, UNIT),
        "lg": A(ret_log_decay)[0],
        "w_out": A(w_out)[0].reshape(KT, P, KT, P).transpose(2, 1, 0, 3).reshape(KT, P, UNIT),
        **constants(),
    }
    arrays = {"in_" + k: np.ascontiguousarray(a) for k, a in arrays.items()}
    nc = bacc.Bacc("TRN2", target_bir_lowering=False, num_devices=1)
    t = {k[3:]: nc.dram_tensor(k, a.shape, F32, kind="ExternalInput").ap() for k, a in arrays.items()}
    t["lg"] = t["lg"].partition_broadcast(P)
    t["out"] = nc.dram_tensor("out", (KT, P, SEQ), F32, kind="ExternalOutput").ap()
    build(nc, t)
    got = run_bass_kernel_spmd(nc, [arrays], core_ids=[0]).results[0]["out"]
    return np.ascontiguousarray(got.reshape(D, SEQ).T)[None]
```
